# Optimizing a Trainium2 kernel written in Bass

```python
import functools
import jax, jax.numpy as jnp
from jax import lax
import numpy as np

D_MODEL = 2048
BATCH = 1
SEQ = 256
DEPTH = 2

HEAD_DIM = 128
N_HEADS = D_MODEL // HEAD_DIM
MIX_WIDTH = N_HEADS * HEAD_DIM
N_SB_HEADS = N_HEADS // 2
N_FOX_HEADS = N_HEADS - N_SB_HEADS
SB_WIDTH = N_SB_HEADS * HEAD_DIM
FOX_WIDTH = N_FOX_HEADS * HEAD_DIM
P_IN = 3 * SB_WIDTH + 4 * FOX_WIDTH + N_FOX_HEADS
D_FF = (11 * D_MODEL) // 4
N_EXPERTS = 8
TOP_K = 2
D_FF_EXPERT = D_MODEL // 2
BLOCK_Q = 128
N_QUERY_CHUNKS = 8
NORM_EPS = 1e-6

kernel_name = "hybrid_stickbreak_fox_moe_trunk"

def rmsnorm(x, g):
    xf = x.astype(jnp.float32)
    y = xf * lax.rsqrt(jnp.mean(xf * xf, axis=-1, keepdims=True) + NORM_EPS)
    return (y * g.astype(jnp.float32)).astype(x.dtype)

def head_rmsnorm(o, g):
    b, s, w = o.shape
    h = w // HEAD_DIM
    return rmsnorm(o.reshape(b, s, h, HEAD_DIM), g.reshape(h, HEAD_DIM)).reshape(b, s, w)

def split_heads(t):
    b, s, w = t.shape
    return t.reshape(b, s, w // HEAD_DIM, HEAD_DIM)

def to_query_blocks(t):
    b, s, h, d = t.shape
    return t.reshape(b, s // BLOCK_Q, BLOCK_Q, h, d).transpose(1, 0, 3, 2, 4)

def from_query_blocks(o):
    nb, b, h, q, d = o.shape
    return o.transpose(1, 0, 3, 2, 4).reshape(b, nb * q, h * d)

def causal_sweep(block_fn, per_block, s_len):
    nb = s_len // BLOCK_Q
    starts = jnp.arange(nb, dtype=jnp.int32) * BLOCK_Q
    n_chunks = min(N_QUERY_CHUNKS, nb)
    outs = []
    for c in range(n_chunks):
        b0 = (c * nb) // n_chunks
        b1 = ((c + 1) * nb) // n_chunks
        xs = tuple(a[b0:b1] for a in per_block) + (starts[b0:b1],)
        outs.append(lax.map(functools.partial(block_fn, key_len=b1 * BLOCK_Q), xs))
    return jnp.concatenate(outs, axis=0)

def stick_breaking_attention(q, k, v):
    s_len = q.shape[1]
    kh = k.transpose(0, 2, 1, 3)
    vh = v.transpose(0, 2, 1, 3)
    scale = HEAD_DIM ** -0.5
    r = jnp.arange(BLOCK_Q)
    tri_incl = (r[:, None] >= r[None, :]).astype(jnp.float32)

    def block(args, key_len):
        q_blk, t0 = args
        nk = key_len // BLOCK_Q
        kk = kh[:, :, :key_len]
        vv = vh[:, :, :key_len]
        z = jnp.einsum('bhqd,bhkd->bhqk', q_blk, kk,
                       preferred_element_type=jnp.float32) * scale
        q_pos = t0 + jnp.arange(BLOCK_Q)
        mask = jnp.arange(key_len)[None, :] < q_pos[:, None]
        sp = jnp.where(mask, jax.nn.softplus(z), 0.0)
        b, h, nq, _ = sp.shape
        sp_b = sp.reshape(b, h, nq, nk, BLOCK_Q)
        within = jnp.einsum('bhqnj,js->bhqns', sp_b, tri_incl)
        nb_idx = jnp.arange(nk)
        strict = (nb_idx[:, None] > nb_idx[None, :]).astype(jnp.float32)
        after = jnp.einsum('bhqn,nm->bhqm', jnp.sum(sp_b, axis=-1), strict)
        rev = (within + after[..., None]).reshape(b, h, nq, key_len)
        w = jnp.exp(jnp.where(mask, z - rev, -jnp.inf))
        return jnp.einsum('bhqk,bhkd->bhqd', w.astype(vv.dtype), vv)

    out = causal_sweep(block, (to_query_blocks(q),), s_len)
    return from_query_blocks(out)

def forgetting_attention(q, k, v, log_f):
    b, s_len, h, _ = q.shape
    nb = s_len // BLOCK_Q
    kh = k.transpose(0, 2, 1, 3)
    vh = v.transpose(0, 2, 1, 3)
    c = lax.cumsum(log_f, axis=1).transpose(0, 2, 1)
    c_blocks = c.reshape(b, h, nb, BLOCK_Q).transpose(2, 0, 1, 3)
    scale = HEAD_DIM ** -0.5

    def block(args, key_len):
        q_blk, c_q, t0 = args
        kk = kh[:, :, :key_len]
        vv = vh[:, :, :key_len]
        logits = jnp.einsum('bhqd,bhkd->bhqk', q_blk, kk,
                            preferred_element_type=jnp.float32) * scale
        logits = logits + c_q[..., :, None] - c[:, :, None, :key_len]
        q_pos = t0 + jnp.arange(BLOCK_Q)
        mask = jnp.arange(key_len)[None, :] <= q_pos[:, None]
        p = jax.nn.softmax(jnp.where(mask, logits, -jnp.inf), axis=-1)
        return jnp.einsum('bhqk,bhkd->bhqd', p.astype(vv.dtype), vv)

    out = causal_sweep(block, (to_query_blocks(q), c_blocks), s_len)
    return from_query_blocks(out)

def hybrid_mixer(a, w_in, b_forget, q_norm, k_norm, sb_out_norm, fox_out_norm, w_out):
    proj = a @ w_in
    offs = [SB_WIDTH, 2 * SB_WIDTH, 3 * SB_WIDTH,
            3 * SB_WIDTH + FOX_WIDTH, 3 * SB_WIDTH + 2 * FOX_WIDTH,
            3 * SB_WIDTH + 3 * FOX_WIDTH, 3 * SB_WIDTH + 4 * FOX_WIDTH]
    sb_q, sb_k, sb_v, fx_q, fx_k, fx_v, fx_g, fx_f = jnp.split(proj, offs, axis=-1)
    sb_o = stick_breaking_attention(split_heads(sb_q), split_heads(sb_k), split_heads(sb_v))
    sb_o = head_rmsnorm(sb_o, sb_out_norm)
    fq = rmsnorm(split_heads(fx_q), q_norm)
    fk = rmsnorm(split_heads(fx_k), k_norm)
    log_f = jax.nn.log_sigmoid((fx_f + b_forget).astype(jnp.float32))
    fox_o = forgetting_attention(fq, fk, split_heads(fx_v), log_f)
    fox_o = head_rmsnorm(fox_o, fox_out_norm) * jax.nn.sigmoid(fx_g)
    return jnp.concatenate([sb_o, fox_o], axis=-1) @ w_out

def swiglu(h, wg, wu, wd):
    return (jax.nn.silu(h @ wg) * (h @ wu)) @ wd

def moe_swiglu(h, router_w, wg, wu, wd):
    b, s, d = h.shape
    tokens = h.reshape(b * s, d)
    probs = jax.nn.softmax((tokens @ router_w).astype(jnp.float32), axis=-1)
    top_p, top_i = lax.top_k(probs, TOP_K)
    top_p = top_p / jnp.sum(top_p, axis=-1, keepdims=True)
    gates = jnp.sum(jax.nn.one_hot(top_i, N_EXPERTS, dtype=jnp.float32) * top_p[..., None],
                    axis=1).astype(tokens.dtype)
    y = jnp.zeros_like(tokens)
    for e in range(N_EXPERTS):
        y = y + gates[:, e:e + 1] * swiglu(tokens, wg[e], wu[e], wd[e])
    return y.reshape(b, s, d)

def setup_inputs(seed: int = 0) -> dict:
    key = jax.random.key(seed)
    ks = jax.random.split(key, 20)
    n_dense = (DEPTH + 1) // 2
    n_moe = DEPTH // 2
    nrm = jax.random.normal
    f32 = jnp.float32

    def gain(k, shape):
        return 1.0 + 0.02 * nrm(k, shape, f32)

    return {
        "x": nrm(ks[0], (BATCH, SEQ, D_MODEL), f32),
        "attn_norm": gain(ks[1], (DEPTH, D_MODEL)),
        "w_in": nrm(ks[2], (DEPTH, D_MODEL, P_IN), f32) * D_MODEL ** -0.5,
        "b_forget": 0.1 * nrm(ks[3], (DEPTH, N_FOX_HEADS), f32),
        "fox_q_norm": gain(ks[4], (DEPTH, HEAD_DIM)),
        "fox_k_norm": gain(ks[5], (DEPTH, HEAD_DIM)),
        "sb_out_norm": gain(ks[6], (DEPTH, SB_WIDTH)),
        "fox_out_norm": gain(ks[7], (DEPTH, FOX_WIDTH)),
        "w_out": nrm(ks[8], (DEPTH, MIX_WIDTH, D_MODEL), f32) * MIX_WIDTH ** -0.5,
        "ffn_norm": gain(ks[9], (DEPTH, D_MODEL)),
        "dense_w_gate": nrm(ks[10], (n_dense, D_MODEL, D_FF), f32) * D_MODEL ** -0.5,
        "dense_w_up": nrm(ks[11], (n_dense, D_MODEL, D_FF), f32) * D_MODEL ** -0.5,
        "dense_w_down": nrm(ks[12], (n_dense, D_FF, D_MODEL), f32) * D_FF ** -0.5,
        "router_w": nrm(ks[13], (n_moe, D_MODEL, N_EXPERTS), f32) * D_MODEL ** -0.5,
        "moe_w_gate": nrm(ks[14], (n_moe, N_EXPERTS, D_MODEL, D_FF_EXPERT), f32) * D_MODEL ** -0.5,
        "moe_w_up": nrm(ks[15], (n_moe, N_EXPERTS, D_MODEL, D_FF_EXPERT), f32) * D_MODEL ** -0.5,
        "moe_w_down": nrm(ks[16], (n_moe, N_EXPERTS, D_FF_EXPERT, D_MODEL), f32) * D_FF_EXPERT ** -0.5,
        "final_norm": gain(ks[17], (D_MODEL,)),
    }

def reference(x, attn_norm, w_in, b_forget, fox_q_norm, fox_k_norm, sb_out_norm,
              fox_out_norm, w_out, ffn_norm, dense_w_gate, dense_w_up, dense_w_down,
              router_w, moe_w_gate, moe_w_up, moe_w_down, final_norm):
    h = x
    for layer in range(DEPTH):
        a = rmsnorm(h, attn_norm[layer])
        h = h + hybrid_mixer(a, w_in[layer], b_forget[layer], fox_q_norm[layer],
                             fox_k_norm[layer], sb_out_norm[layer], fox_out_norm[layer],
                             w_out[layer])
        m = rmsnorm(h, ffn_norm[layer])
        i = layer // 2
        if layer % 2 == 0:
            h = h + swiglu(m, dense_w_gate[i], dense_w_up[i], dense_w_down[i])
        else:
            h = h + moe_swiglu(m, router_w[i], moe_w_gate[i], moe_w_up[i], moe_w_down[i])
    return rmsnorm(h, final_norm)


_drawn_inputs = setup_inputs


def setup_inputs(seed=0):
    import zlib

    import numpy as np

    out = dict(_drawn_inputs(seed))
    spreads = {}
    factors = {'fox_q_norm': 7.249, 'fox_k_norm': 4.584, 'fox_out_norm': 2.913, 'final_norm': 2.826}
    for name, (base, spread) in spreads.items():
        noise = np.random.default_rng([zlib.crc32(name.encode()), seed]).standard_normal(out[name].shape)
        drawn = base * np.exp(spread * noise) if base else spread * noise
        out[name] = __import__('jax').numpy.asarray(drawn.astype(out[name].dtype))
    for name, factor in factors.items():
        out[name] = (out[name] * factor).astype(out[name].dtype)
    return out
```

```python
from contextlib import ExitStack

import concourse.bass as bass
from concourse import mybir

F32 = mybir.dt.float32
F32R = mybir.dt.float32r
U32 = mybir.dt.uint32
ALU = mybir.AluOpType
ACT = mybir.ActivationFunctionType
AX = mybir.AxisListType

P = 128
COLS = 512
BLOCKS = 2
UNIT_CHUNKS = 2
TILE_UNITS = 2
RAW_SLOTS = 4
SPLIT_SLOTS = 4
LEAD = 3
QUAD = 4
QUAD_PAIRS = 2
NEG = -1e30
EPS = 1e-6


class Own:

    def __init__(self):
        self.n, self.i, self.per = 0, None, 0

    def up(self):
        self.n += 1
        return self.n if self.i is None else self.i * self.per + self.n

    def enter(self, i, per):
        self.i, self.per, self.start = i, per, self.n

    def leave(self, trips):
        assert self.n - self.start == self.per, (self.n, self.start, self.per)
        self.n, self.i = self.start + self.per * trips, None


def lin(const, per=0, i=None):
    return const if i is None else i * per + const


def trunk(nc, x, attn_norm, w_in, b_forget, fox_q_norm, fox_k_norm, sb_out_norm, fox_out_norm, w_out,
          ffn_norm, dense_w_gate, dense_w_up, dense_w_down, router_w, moe_w_gate, moe_w_up, moe_w_down,
          final_norm, out):
    D = x.shape[2]
    DEPTH = w_in.shape[0]
    CH = D // P
    HEADS = sb_out_norm.shape[1] // P
    W = sb_out_norm.shape[1]
    EXPERTS = router_w.shape[2]
    F_EXP = moe_w_gate.shape[3]
    SCALE = float(P) ** -0.5
    assert x.shape[1] == BLOCKS * P and DEPTH == 2 and CH == 16 and HEADS == 8 and EXPERTS == 8
    NCOL = D // COLS
    GC = COLS // P

    JOB_UNITS = CH // UNIT_CHUNKS
    jobs = []
    for quad in range(4):
        base = (quad % 2) * COLS + (0 if quad < 2 else 3 * W)
        for n, what in enumerate("qkv" if quad < 2 else "qkvg"):
            jobs.append((quad, what, base + n * W))
    NJ = len(jobs)
    PROJ_UNITS = NJ * JOB_UNITS
    out_units = []
    for c in (0, 2):
        for cc, us in ((c, range(6)), (c + 1, range(6)), (c, (6, 7)), (c + 1, (6, 7))):
            out_units += [(cc, u) for u in us]
    ATT_UNITS = PROJ_UNITS + len(out_units)
    quad_start = [(1 + max(j for j in range(NJ) if jobs[j][0] == q)) * JOB_UNITS for q in range(4)]
    PAIR_STEPS = (("scores", 0, 0), ("second", 3, 2), ("values", 5, 3), ("turn", 8, 5))
    steps = {}
    for q in range(4):
        steps.setdefault(quad_start[q], []).append(("qk", q, 0))
        for p in range(QUAD_PAIRS):
            for name, at, late in PAIR_STEPS:
                u = quad_start[q] + (1 + 5 * p + late if q == 3 else 2 + 10 * p + at)
                steps.setdefault(u, []).append((name, q, p))

    GROUPS = [dense_w_gate.shape[2] // COLS, EXPERTS * F_EXP // COLS]
    UP_UNITS, DOWN_UNITS = JOB_UNITS, GC // UNIT_CHUNKS
    GROUP_UNITS = 2 * UP_UNITS + NCOL * DOWN_UNITS
    TURN_AT = UP_UNITS + 1
    ffn_start = [ATT_UNITS, 2 * ATT_UNITS + GROUPS[0] * GROUP_UNITS]
    layer_start = [0, ATT_UNITS + GROUPS[0] * GROUP_UNITS]
    UNITS = ffn_start[1] + GROUPS[1] * GROUP_UNITS
    TILES = UNITS // TILE_UNITS
    groups_before = [0, GROUPS[0]]
    ATT_USES = (NJ + NCOL) // 2
    att_uses = [0, ATT_USES + 3 * GROUPS[0]]
    ffn_uses = [u + ATT_USES for u in att_uses]
    LATE_QUARTERS = {1: 2, 3: 3}
    OWN_DVE_GROUP = 2
    gexp = [0, 2 + GROUPS[0]]

    with ExitStack() as ctx:
        def sb(name, shape, dt=F32):
            return ctx.enter_context(nc.sbuf_tensor(name, shape, dt))

        def sem(name):
            return ctx.enter_context(nc.semaphore(name))

        raw = sb("raw", [P, RAW_SLOTS, TILE_UNITS, UNIT_CHUNKS, COLS])
        w_hi = sb("w_hi", [P, SPLIT_SLOTS, UNIT_CHUNKS, COLS], F32R)
        w_lo = sb("w_lo", [P, SPLIT_SLOTS, UNIT_CHUNKS, COLS], F32R)
        h = sb("h", [P, BLOCKS, D])
        a_hi = sb("a_hi", [P, CH, BLOCKS * P], F32R)
        a_lo = sb("a_lo", [P, CH, BLOCKS * P], F32R)
        o_hi = sb("o_hi", [P, CH, BLOCKS * P], F32R)
        o_lo = sb("o_lo", [P, CH, BLOCKS * P], F32R)
        scr = sb("scr", [P, 4 * COLS])
        xn = scr[:].rearrange("p (s b n) -> p s b n", s=2, b=BLOCKS)
        PW = 3 * P
        zs = scr[:, 0:2 * PW].rearrange("p (a n) -> p a n", a=2)
        t1 = scr[:, 2 * PW:4 * PW].rearrange("p (a n) -> p a n", a=2)
        sp = sb("sp", [P, 2, PW])
        wT = sb("wT", [P, 2, PW])
        nat = sb("nat", [P, 4, BLOCKS, COLS])
        q_nat, k_nat, v_nat, g_nat = (nat[:, n] for n in range(4))
        silu, hid = nat[:, 1], nat[:, 2]
        eg = sb("eg", [P, BLOCKS, COLS])
        qT = sb("qT", [P, QUAD, BLOCKS * P])
        kT = sb("kT", [P, QUAD, BLOCKS * P])
        ob = sb("ob", [P, 4, P])
        ident = sb("ident", [P, P])
        ones = sb("ones", [P, P])
        tri_ge = sb("tri_ge", [P, P])
        tri_le = sb("tri_le", [P, P])
        sb_keep = sb("sb_keep", [P, PW])
        sb_neg = sb("sb_neg", [P, PW])
        fx_neg = sb("fx_neg", [P, PW])
        onehot = sb("onehot", [HEADS, HEADS, P])
        thin_hi = sb("thin_hi", [P, 3, CH, HEADS], F32R)
        thin_lo = sb("thin_lo", [P, 3, CH, HEADS], F32R)
        thin = eg[:, 0, 0:3 * P].rearrange("p (t c n) -> p t c n", t=3, c=CH)
        rows = eg[:, 1, 0:P]
        NG_ATT, NG_FFN, NG_HEAD, NG_QK = 0, 2 * CH, 4 * CH, 4 * CH + 4 * HEADS
        NROWS = NG_QK + 4
        gain = sb("gain", [P, P])
        gq = sb("gq", [P, 2])
        bf = sb("bf", [P, 2, HEADS])
        epsc = sb("epsc", [P, 1])
        sm = sb("sm", [P, 192])
        ss, rr, xx, tt = (sm[:, 2 * n:2 * n + 2] for n in range(4))
        hss, hr, hx, ht = (sm[:, 8 + 8 * n:16 + 8 * n] for n in range(4))
        kss, kr = (sm[:, 40 + 8 * n:48 + 8 * n] for n in range(2))
        fz, fl, logf = (sm[:, 56 + 16 * n:72 + 16 * n].rearrange("p (b n) -> p b n", b=2) for n in range(3))
        cum = sm[:, 104:120].rearrange("p (b n) -> p b n", b=2)
        nm = sm[:, 120:124]
        lsum = sm[:, 124:128]
        rl = sm[:, 128:132]
        lg, gts, eq = (sm[:, 136 + 16 * n:152 + 16 * n].rearrange("p (b n) -> p b n", b=2) for n in range(3))
        top, gt1 = (sb(f"top{n}", [P, 2, 8]) for n in range(2))
        topi = sb("topi", [P, 2, 8], U32)
        topf = sb("topf", [P, 2, 8])
        iota8 = sb("iota8", [P, 8])
        gates = sb("gates", [P, BLOCKS, 2 * EXPERTS])
        ncT = sb("ncT", [HEADS, BLOCKS * P])
        acc = ctx.enter_context(nc.psum_tensor("acc", [P, 2, BLOCKS, COLS], F32))
        X = ctx.enter_context(nc.psum_tensor("X", [P, 4, COLS], F32))

        loaded = [sem(f"loaded{s}") for s in range(RAW_SLOTS)]
        hi_ready = sem("hi_ready")
        lo_ready = sem("lo_ready")
        used = sem("used")
        free = [sem(f"free{s}") for s in range(2)]
        x_in = sem("x_in")
        small_in = sem("small_in")
        fin_in = sem("fin_in")
        stored = sem("stored")
        consts = sem("consts")
        gain_ps = sem("gain_ps")
        gain_ready = sem("gain_ready")
        thin_h = sem("thin_h")
        thin_ready = sem("thin_ready")
        ss_ready = sem("ss_ready")
        r_ready = sem("r_ready")
        xn_ready = sem("xn_ready")
        xnT_ps = sem("xnT_ps")
        a_hi_ready = sem("a_hi_ready")
        a_ready = sem("a_ready")
        f_ps = sem("f_ps")
        f_x = sem("f_x")
        f_ln = sem("f_ln")
        f_log = sem("f_log")
        c_ps = sem("c_ps")
        c_ready = sem("c_ready")
        g_exp = sem("g_exp")
        sq_ready = sem("sq_ready")
        sq_sum = sem("sq_sum")
        sq_r = sem("sq_r")
        q_done = sem("q_done")
        k_done = sem("k_done")
        v_done = sem("v_done")
        qkT_ps = sem("qkT_ps")
        qT_ready = sem("qT_ready")
        kT_ready = sem("kT_ready")
        z_ps = sem("z_ps")
        z_scaled = sem("z_scaled")
        z_ln = sem("z_ln")
        sp_ready = sem("sp_ready")
        rev_ps = sem("rev_ps")
        arg_ready = sem("arg_ready")
        m_ready = sem("m_ready")
        p_ready = sem("p_ready")
        pT_ps = sem("pT_ps")
        w_ready = sem("w_ready")
        o_ps = sem("o_ps")
        o_sum = sem("o_sum")
        o_r = sem("o_r")
        o_normed = sem("o_normed")
        oT_ps = sem("oT_ps")
        oT_hi = sem("oT_hi")
        oT_ready = sem("oT_ready")
        rt_ps = sem("rt_ps")
        rt_max = sem("rt_max")
        rt_exp = sem("rt_exp")
        gates_ready = sem("gates_ready")
        hT_ps = sem("hT_ps")
        hT_hi = sem("hT_hi")
        hT_ready = sem("hT_ready")
        act_own = sem("act_own")
        dve_own = sem("dve_own")
        pool_own = sem("pool_own")

        block = ctx.enter_context(nc.Block())
        N_SMALL = 13

        @block.sync
        def _(sp_):
            def load(tile, src, per=0, i=None):
                slot = tile % RAW_SLOTS
                if i is not None or tile >= RAW_SLOTS:
                    sp_.wait_ge(lo_ready, lin(TILE_UNITS * (tile - RAW_SLOTS + 1), TILE_UNITS * per, i))
                sp_.dma_start(raw[:, slot].rearrange("p u c n -> p (u c) n"),
                              src.rearrange("(c p) n -> p c n", p=P)).then_inc(loaded[slot], 16)

            def load_wide(tile, w, col, per=0, i=None):
                for t in range(CH // GC):
                    load(tile + t, w[t * COLS:(t + 1) * COLS, col], per, i)

            for b in range(BLOCKS):
                sp_.dma_start(h[:, b, :], x[0, b * P:(b + 1) * P, :]).then_inc(x_in, 16)
            for layer in range(DEPTH):
                tile = layer_start[layer] // TILE_UNITS
                for j, (_, _, col) in enumerate(jobs):
                    load_wide(tile + j * CH // GC, w_in[layer], slice(col, col + COLS))
                for n, (c, u) in enumerate(out_units):
                    if n % TILE_UNITS == 0:
                        r = u * UNIT_CHUNKS * P
                        load(tile + (PROJ_UNITS + n) // TILE_UNITS,
                             w_out[layer, r:r + COLS, c * COLS:(c + 1) * COLS])
                tile = ffn_start[layer] // TILE_UNITS
                per_group = GROUP_UNITS // TILE_UNITS
                if layer == 0:
                    wg, wu, wd = dense_w_gate[0], dense_w_up[0], dense_w_down[0]
                    load_wide(tile, wg, slice(0, COLS))
                    tile += CH // GC
                    with sp_.Fori(0, GROUPS[0] - 1) as i:
                        load_wide(tile, wu, bass.ts(i, COLS), per_group, i)
                        load_wide(tile + CH // GC, wg, bass.ds(i * COLS + COLS, COLS), per_group, i)
                        for c in range(NCOL):
                            load(tile + 2 * CH // GC + c, wd[bass.ts(i, COLS), c * COLS:(c + 1) * COLS],
                                 per_group, i)
                    tile += per_group * (GROUPS[0] - 1)
                    last = GROUPS[0] - 1
                    load_wide(tile, wu, slice(last * COLS, (last + 1) * COLS))
                    for c in range(NCOL):
                        load(tile + CH // GC + c, wd[last * COLS:(last + 1) * COLS, c * COLS:(c + 1) * COLS])
                else:
                    wg, wu, wd = moe_w_gate[0], moe_w_up[0], moe_w_down[0]
                    load_wide(tile, wg[0], slice(0, COLS))
                    tile += CH // GC
                    halves = F_EXP // COLS
                    per_expert = halves * per_group

                    def load_group(t0, e, half, e_next, half_next, per=0, i=None):
                        load_wide(t0, wu[e], slice(half * COLS, (half + 1) * COLS), per, i)
                        t0 += CH // GC
                        if e_next is not None:
                            load_wide(t0, wg[e_next], slice(half_next * COLS, (half_next + 1) * COLS), per, i)
                            t0 += CH // GC
                        for c in range(NCOL):
                            load(t0 + c, wd[e][half * COLS:(half + 1) * COLS, c * COLS:(c + 1) * COLS], per, i)

                    with sp_.Fori(0, EXPERTS - 1) as e:
                        for half in range(halves):
                            nxt = (e, half + 1) if half + 1 < halves else (e + 1, 0)
                            load_group(tile + half * per_group, e, half, *nxt, per_expert, e)
                    tile += per_expert * (EXPERTS - 1)
                    for half in range(halves):
                        nxt = (EXPERTS - 1, half + 1) if half + 1 < halves else (None, None)
                        load_group(tile + half * per_group, EXPERTS - 1, half, *nxt)
            sp_.wait_ge(xnT_ps, 4 * 4)
            sp_.dma_start(scr[:, 0:D], final_norm.rearrange("(a n) -> a n", a=1).broadcast_to([P, D]))\
               .then_inc(fin_in, 16)
            for b in range(BLOCKS):
                sp_.wait_ge(r_ready, 1 + b)
                sp_.dma_start(out[0, b * P:(b + 1) * P, :], h[:, b, :]).then_inc(stored, 16)
            sp_.wait_ge(stored, 16 * BLOCKS)

        @block.gpsimd
        def _(pool):
            pool.memset(onehot[:], 0.0).then_inc(pool_own, 1)
            pool.memset(ident[:], 0.0).then_inc(pool_own, 1)
            pool.memset(ones[:], 1.0).then_inc(pool_own, 1)
            pool.memset(sb_keep[:], 1.0).then_inc(pool_own, 1)
            pool.memset(sb_neg[:], 0.0).then_inc(pool_own, 1)
            pool.memset(fx_neg[:], 0.0).then_inc(pool_own, 1)
            pool.memset(epsc[:], EPS).then_inc(pool_own, 1)
            pool.wait_ge(pool_own, 7)
            pool.affine_select(out=ident[:], in_=ident[:], compare_op=ALU.not_equal, fill=1.0, base=0,
                               pattern=[[-1, P]], channel_multiplier=1).then_inc(consts, 1)
            pool.affine_select(out=tri_ge[:], in_=ones[:], compare_op=ALU.is_ge, fill=0.0, base=0,
                               pattern=[[-1, P]], channel_multiplier=1).then_inc(consts, 1)
            pool.affine_select(out=tri_le[:], in_=ones[:], compare_op=ALU.is_ge, fill=0.0, base=0,
                               pattern=[[1, P]], channel_multiplier=-1).then_inc(consts, 1)
            for at in (0, 2 * P):
                pool.affine_select(out=sb_keep[:, at:at + P], in_=sb_keep[:, at:at + P], compare_op=ALU.is_gt,
                                   fill=0.0, base=0, pattern=[[1, P]], channel_multiplier=-1).then_inc(consts, 1)
                pool.affine_select(out=sb_neg[:, at:at + P], in_=sb_neg[:, at:at + P], compare_op=ALU.is_gt,
                                   fill=NEG, base=0, pattern=[[1, P]], channel_multiplier=-1).then_inc(consts, 1)
                pool.affine_select(out=fx_neg[:, at:at + P], in_=fx_neg[:, at:at + P], compare_op=ALU.is_ge,
                                   fill=NEG, base=0, pattern=[[-1, P]], channel_multiplier=1).then_inc(consts, 1)
            pool.affine_select(out=onehot[:], in_=onehot[:], compare_op=ALU.not_equal, fill=1.0, base=0,
                               pattern=[[-1, HEADS], [0, P]], channel_multiplier=1).then_inc(consts, 1)
            pool.iota(iota8[:], pattern=[[1, 8]], base=0, channel_multiplier=0,
                      allow_small_or_imprecise_dtypes=True).then_inc(consts, 1)
        N_CONSTS = 11

        @block.scalar
        def _(act):
            own = Own()

            def split_hi(u, per=0, i=None):
                if i is None and u >= UNITS:
                    return
                slot = u % SPLIT_SLOTS
                tile = u // TILE_UNITS
                if u % TILE_UNITS == 0:
                    act.wait_ge(loaded[tile % RAW_SLOTS],
                                lin(16 * (tile // RAW_SLOTS + 1), 16 * per // (TILE_UNITS * RAW_SLOTS), i))
                if i is not None or u >= SPLIT_SLOTS:
                    act.wait_ge(used, lin(u - SPLIT_SLOTS + 1, per, i))
                nc.scalar.activation(w_hi[:, slot], raw[:, tile % RAW_SLOTS, u % TILE_UNITS], ACT.Copy)\
                  .then_inc(hi_ready, 1)

            def rsqrt_guess(y, s, n, scale, signal):
                nc.scalar.activation(y, s, ACT.Ln, bias=epsc[:, 0:1], scale=scale).then_inc(act_own, 1)
                act.wait_ge(act_own, own.up())
                nc.scalar.activation(y, y, ACT.Exp, scale=-0.5).then_inc(signal, 1)

            def norm_guess(n):
                for b in range(BLOCKS):
                    nc.scalar.activation(scr[:, 0:D], h[:, b, :], ACT.Square, accum_out=ss[:, b:b + 1])\
                      .then_inc(act_own, 1)
                    act.wait_ge(act_own, own.up())
                rsqrt_guess(rr, ss, 2, 1.0 / D, ss_ready)

            def input_hi(n, quarter):
                act.wait_ge(xnT_ps, 4 * n + quarter + 1)
                for k in range(4 * quarter, 4 * quarter + 4):
                    g = (NG_ATT if n % 2 == 0 else NG_FFN) + (n // 2) * CH + k
                    bank = 2 * (quarter % 2) + (k % 4) // 2
                    nc.scalar.activation(a_hi[:, k, :], X[:, bank, (k % 2) * 256:(k % 2) * 256 + 256], ACT.Copy,
                                         scale=gain[:, g:g + 1]).then_inc(a_hi_ready, 1)

            nc.scalar.preload_act_table_set("natural_log_exp_and_others")
            for l in range(DEPTH):
                for src, at, n in ((attn_norm, NG_ATT + l * CH, CH), (ffn_norm, NG_FFN + l * CH, CH),
                                   (sb_out_norm, NG_HEAD + 2 * l * HEADS, HEADS),
                                   (fox_out_norm, NG_HEAD + (2 * l + 1) * HEADS, HEADS)):
                    act.dma_start(rows[at:at + n, :], src[l].rearrange("(c p) -> c p", p=P)).then_inc(small_in, 16)
            act.dma_start(rows[NG_QK:NG_QK + 2, :], fox_q_norm[:, :]).then_inc(small_in, 16)
            act.dma_start(rows[NG_QK + 2:NG_QK + 4, :], fox_k_norm[:, :]).then_inc(small_in, 16)
            for l in range(DEPTH):
                act.dma_start(thin[:, l], w_in[l].rearrange("(c p) n -> p c n", p=P)[:, :, 3 * W + 4 * W:])\
                   .then_inc(small_in, 16)
            act.dma_start(thin[:, 2], router_w[0].rearrange("(c p) n -> p c n", p=P)).then_inc(small_in, 16)
            act.dma_start(bf[:], b_forget.rearrange("(a l) n -> a l n", a=1).broadcast_to([P, DEPTH, HEADS]))\
               .then_inc(small_in, 16)
            act.wait_ge(consts, 1)
            act.wait_ge(small_in, 16 * (4 * DEPTH + 6))
            nc.scalar.activation(thin_hi[:], thin, ACT.Copy).then_inc(thin_h, 1)
            for u in range(LEAD):
                split_hi(u)
            act.wait_ge(x_in, 16 * BLOCKS)

            for layer in range(DEPTH):
                L = layer
                U0 = layer_start[layer]
                if layer:
                    act.wait_ge(free[0], att_uses[layer])
                    act.wait_ge(free[1], att_uses[layer])
                norm_guess(2 * L)
                if layer == 0:
                    act.wait_ge(gain_ready, 1)
                for quarter in range(2):
                    input_hi(2 * L, quarter)
                for u in range(ATT_UNITS):
                    split_hi(U0 + u + LEAD)
                    if u in LATE_QUARTERS:
                        input_hi(2 * L, LATE_QUARTERS[u])
                    j, last = u // JOB_UNITS, u % JOB_UNITS == JOB_UNITS - 1
                    if u == JOB_UNITS:
                        act.wait_ge(f_x, L + 1)
                        nc.scalar.activation(fl, fz, ACT.Abs).then_inc(act_own, 1)
                        act.wait_ge(act_own, own.up())
                        nc.scalar.activation(fl, fl, ACT.Exp, scale=-1.0).then_inc(act_own, 1)
                        act.wait_ge(act_own, own.up())
                        nc.scalar.activation(fl, fl, ACT.Ln, bias=1.0).then_inc(f_ln, 1)
                    if j < NJ and last:
                        quad, what, _ = jobs[j]
                        pair = acc[:, j % 2]
                        use = att_uses[layer] + j // 2 + 1
                        if what == "q":
                            act.wait_ge(used, U0 + u + 1)
                            if quad == 3:
                                act.wait_ge(free[(j - 1) % 2], att_uses[layer] + (j - 1) // 2 + 1)
                            if quad < 2:
                                nc.scalar.activation(q_nat, pair, ACT.Copy).then_inc(free[j % 2], 1)
                            else:
                                nc.scalar.activation(q_nat, pair, ACT.Copy).then_inc(q_done, 1)
                        if quad >= 2 and what in "qk":
                            act.wait_ge(used, U0 + u + 1)
                            if what == "k":
                                act.wait_ge(k_done, 4 * L + (quad - 2) * 2 + 1)
                            nc.scalar.activation(eg[:], pair, ACT.Square).then_inc(free[j % 2], 1)
                        if what == "v":
                            act.wait_ge(used, U0 + u + 1)
                            nc.scalar.activation(v_nat, pair, ACT.Copy).then_inc(free[j % 2], 1)
                        if what == "g":
                            act.wait_ge(used, U0 + u + 1)
                            nc.scalar.activation(eg[:], pair, ACT.Exp, scale=-1.0).then_inc(g_exp, 1)
                    if 0 < j <= NJ and u % JOB_UNITS == 0 and jobs[j - 1][0] >= 2 and jobs[j - 1][1] in "qk":
                        n = 4 * L + (jobs[j - 1][0] - 2) * 2 + "qk".index(jobs[j - 1][1])
                        act.wait_ge(sq_sum, n + 1)
                        rsqrt_guess(kr, kss, 8, 1.0 / P, sq_r)
                    for name, q, p in steps.get(u, ()):
                        nq, np_ = 4 * L + q, 8 * L + 2 * q + p
                        fx = q >= 2
                        if name == "qk":
                            act.wait_ge(qkT_ps, nq + 1)
                            nc.scalar.activation(qT[:], X[:, 0:2].rearrange("p a (h n) -> p (a h) n", h=2), ACT.Copy,
                                                 scale=gq[:, L:L + 1] if fx else 1.0).then_inc(qT_ready, 1)
                        elif name == "scores" and not fx:
                            zp = X[:, 0:2, 0:PW]
                            act.wait_ge(z_ps, np_ + 1)
                            nc.scalar.activation(zs, zp, ACT.Copy, scale=SCALE).then_inc(z_scaled, 1)
                            nc.scalar.activation(t1, zp, ACT.Abs, scale=SCALE).then_inc(act_own, 1)
                            act.wait_ge(act_own, own.up())
                            nc.scalar.activation(t1, t1, ACT.Exp, scale=-1.0).then_inc(act_own, 1)
                            act.wait_ge(act_own, own.up())
                            nc.scalar.activation(t1, t1, ACT.Ln, bias=1.0).then_inc(z_ln, 1)
                        elif name == "scores":
                            act.wait_ge(m_ready, 4 * L + 2 * (q - 2) + p + 1)
                            for a in range(2):
                                for s, e, n in ((0, P, 0), (P, PW, 1)):
                                    ins = nc.scalar.activation(sp[:, a, s:e], zs[:, a, s:e], ACT.Exp,
                                                               bias=nm[:, 2 * a + n:2 * a + n + 1],
                                                               accum_out=lsum[:, 2 * n + a:2 * n + a + 1])
                            ins.then_inc(p_ready, 1)
                        elif name == "second" and not fx:
                            act.wait_ge(arg_ready, 4 * L + 2 * q + p + 1)
                            nc.scalar.activation(wT[:], zs, ACT.Exp).then_inc(w_ready, 1)
                        elif name == "second":
                            act.wait_ge(pT_ps, 4 * L + 2 * (q - 2) + p + 1)
                            nc.scalar.activation(wT[:], X[:, 2:4, 0:PW], ACT.Copy).then_inc(w_ready, 1)
                        elif name == "values":
                            act.wait_ge(o_sum, np_ + 1)
                            rsqrt_guess(hr[:, 0:4], hss[:, 0:4], 4, 1.0 / P, o_r)
                        elif name == "turn":
                            act.wait_ge(oT_ps, np_ + 1)
                            for a in range(2):
                                hd = 4 * q + 2 * p + a
                                g = NG_HEAD + 2 * L * HEADS + hd
                                nc.scalar.activation(
                                    o_hi[:, hd, :].rearrange("p (b n) -> p b n", b=2),
                                    X[:, 1].rearrange("p (b a n) -> p a b n", b=2, a=2)[:, a], ACT.Copy,
                                    scale=gain[:, g:g + 1]).then_inc(oT_hi, 1)
                act.wait_ge(free[0], ffn_uses[layer])
                act.wait_ge(free[1], ffn_uses[layer])
                norm_guess(2 * L + 1)
                for quarter in range(2):
                    input_hi(2 * L + 1, quarter)

                F0, G0, A0, NG = ffn_start[layer], groups_before[layer], ffn_uses[layer], GROUPS[layer]

                def gate_exp(end, i=None):
                    act.wait_ge(used, lin(end, GROUP_UNITS, i))
                    nc.scalar.activation(eg[:], acc[:, 0], ACT.Exp, scale=-1.0).then_inc(g_exp, 1)

                def hidden_hi(n, per=0, i=None):
                    act.wait_ge(hT_ps, lin(G0 + n + 1, per, i))
                    nc.scalar.activation(o_hi[:, 0:GC].rearrange("p c n -> p (c n)"),
                                         X[:, 0:2].rearrange("p a n -> p (a n)"), ACT.Copy).then_inc(hT_hi, 1)

                for u in range(UP_UNITS):
                    split_hi(F0 + u + LEAD)
                    if u in LATE_QUARTERS:
                        input_hi(2 * L + 1, LATE_QUARTERS[u])
                gate_exp(F0 + UP_UNITS)
                if layer == 1:
                    act.wait_ge(rt_max, 1)
                    nc.scalar.activation(eq, lg, ACT.Exp).then_inc(rt_exp, 1)
                F1 = F0 + UP_UNITS
                with act.Fori(0, NG - 1) as i:
                    for u in range(GROUP_UNITS):
                        split_hi(F1 + u + LEAD, GROUP_UNITS, i)
                        if u == TURN_AT:
                            hidden_hi(0, 1, i)
                        if u == 2 * UP_UNITS - 1:
                            gate_exp(F1 + u + 1, i)
                F2 = F1 + GROUP_UNITS * (NG - 1)
                for u in range(GROUP_UNITS - UP_UNITS):
                    split_hi(F2 + u + LEAD)
                    if u == UP_UNITS - 1:
                        hidden_hi(NG - 1)
            act.wait_ge(free[0], ffn_uses[1] + 3 * GROUPS[1])
            act.wait_ge(free[1], ffn_uses[1] + 3 * GROUPS[1])
            for b in range(BLOCKS):
                nc.scalar.activation(nat[:, 0:2].rearrange("p a b n -> p (a b n)"), h[:, b, :], ACT.Square,
                                     accum_out=ss[:, b:b + 1]).then_inc(act_own, 1)
                act.wait_ge(act_own, own.up())
            rsqrt_guess(rr, ss, 2, 1.0 / D, ss_ready)

        @block.vector
        def _(dve):
            own = Own()

            def split_lo(u, per=0, i=None):
                if i is None and u >= UNITS:
                    return
                slot = u % SPLIT_SLOTS
                dve.wait_ge(hi_ready, lin(u + 1, per, i))
                nc.vector.tensor_tensor(w_lo[:, slot], raw[:, (u // TILE_UNITS) % RAW_SLOTS, u % TILE_UNITS],
                                        w_hi[:, slot].bitcast(F32), ALU.subtract).then_inc(lo_ready, 1)

            def refine(y, s, x_, t_, scale, guessed, value):
                nc.vector.tensor_scalar(x_, s, scale, EPS, ALU.mult, ALU.add).then_inc(dve_own, 1)
                own.up()
                dve.wait_ge(guessed, value)
                nc.vector.tensor_tensor(t_, y, y, ALU.mult).then_inc(dve_own, 1)
                dve.wait_ge(dve_own, own.up())
                nc.vector.tensor_tensor(t_, t_, x_, ALU.mult).then_inc(dve_own, 1)
                dve.wait_ge(dve_own, own.up())
                nc.vector.tensor_scalar(t_, t_, -0.5, 1.5, ALU.mult, ALU.add).then_inc(dve_own, 1)
                dve.wait_ge(dve_own, own.up())
                nc.vector.tensor_tensor(y, y, t_, ALU.mult).then_inc(dve_own, 1)
                dve.wait_ge(dve_own, own.up())

            def input_lo(n, quarter):
                for k in range(4 * quarter, 4 * quarter + 4):
                    g = (NG_ATT if n % 2 == 0 else NG_FFN) + (n // 2) * CH + k
                    bank = 2 * (quarter % 2) + (k % 4) // 2
                    dve.wait_ge(a_hi_ready, CH * n + k // 2 * 2 + 2)
                    nc.vector.scalar_tensor_tensor(
                        out=a_lo[:, k, :], in0=X[:, bank, (k % 2) * 256:(k % 2) * 256 + 256],
                        scalar=gain[:, g:g + 1], in1=a_hi[:, k, :].bitcast(F32), op0=ALU.mult,
                        op1=ALU.subtract).then_inc(a_ready, 1)

            def norm(n):
                dve.wait_ge(ss_ready, n + 1)
                refine(rr, ss, xx, tt, 1.0 / D, ss_ready, n + 1)

                def rows_quarter(quarter):
                    if quarter >= 2:
                        dve.wait_ge(xnT_ps, 4 * n + quarter - 1)
                    for b in range(BLOCKS):
                        ins = nc.vector.tensor_scalar(xn[:, quarter % 2, b], h[:, b, quarter * COLS:(quarter + 1) * COLS],
                                                      rr[:, b:b + 1], None, ALU.mult)
                    ins.then_inc(xn_ready, 1)

                rows_quarter(0)
                rows_quarter(1)
                if n == 0:
                    dve.wait_ge(gain_ps, 1)
                    nc.vector.tensor_copy(gain[:, 0:NROWS], X[:, 3, 0:NROWS]).then_inc(gain_ready, 1)
                    dve.wait_ge(gain_ready, 1)
                    nc.vector.tensor_scalar(gq[:], gain[:, NG_QK:NG_QK + 2], SCALE, None, ALU.mult)
                for quarter in range(2):
                    input_lo(n, quarter)
                    rows_quarter(quarter + 2)

            def wide(ap, n):
                return ap.rearrange("p (n o) -> p n o", o=1).broadcast_to([P, n, P])

            def both(mask):
                return mask[:].rearrange("p (o n) -> p o n", o=1).broadcast_to([P, 2, PW])

            def add_to_h(c, s, end):
                dve.wait_ge(used, end)
                nc.vector.tensor_tensor(h[:, :, c * COLS:(c + 1) * COLS], h[:, :, c * COLS:(c + 1) * COLS],
                                        acc[:, s], ALU.add).then_inc(free[s], 1)

            dve.wait_ge(thin_h, 1)
            nc.vector.tensor_tensor(thin_lo[:], thin, thin_hi[:].bitcast(F32), ALU.subtract).then_inc(thin_ready, 1)
            for u in range(LEAD):
                split_lo(u)
            dve.wait_ge(consts, N_CONSTS)

            for layer in range(DEPTH):
                L = layer
                U0 = layer_start[layer]
                norm(2 * L)
                for u in range(ATT_UNITS):
                    split_lo(U0 + u + LEAD)
                    if u in LATE_QUARTERS:
                        input_lo(2 * L, LATE_QUARTERS[u])
                    j, last = u // JOB_UNITS, u % JOB_UNITS == JOB_UNITS - 1
                    if u == JOB_UNITS:
                        dve.wait_ge(f_ps, L + 1)
                        for b in range(BLOCKS):
                            ins = nc.vector.tensor_tensor(fz[:, b], X[:, 0, b * HEADS:(b + 1) * HEADS], bf[:, L], ALU.add)
                        ins.then_inc(f_x, 1)
                        dve.wait_ge(f_ln, L + 1)
                        nc.vector.scalar_tensor_tensor(out=logf, in0=fz, scalar=0.0, in1=fl, op0=ALU.min,
                                                       op1=ALU.subtract).then_inc(f_log, 1)
                    if u == JOB_UNITS + 2:
                        dve.wait_ge(c_ps, L + 1)
                        nc.vector.tensor_copy(cum, X[:, 1, 0:2 * HEADS].rearrange("p (b n) -> p b n", b=2))
                        nc.vector.tensor_scalar(ncT[:], X[0:HEADS, 2, 0:BLOCKS * P], -1.0, None, ALU.mult)\
                          .then_inc(c_ready, 1)
                    if j < NJ and last:
                        quad, what, _ = jobs[j]
                        pair = acc[:, j % 2]
                        use = att_uses[layer] + j // 2 + 1
                        if what == "k":
                            dve.wait_ge(used, U0 + u + 1)
                            if quad < 2:
                                nc.vector.tensor_copy(k_nat, pair).then_inc(free[j % 2], 1)
                            else:
                                nc.vector.tensor_copy(k_nat, pair).then_inc(k_done, 1)
                        if quad >= 2 and what in "qk":
                            dve.wait_ge(free[j % 2], use)
                            nc.vector.reduce_sum(kss, eg[:].rearrange("p b (h n) -> p (b h) n", n=P), AX.X)\
                              .then_inc(sq_sum, 1)
                        if what == "g":
                            dve.wait_ge(g_exp, gexp[L] + quad - 1)
                            nc.vector.tensor_scalar(g_nat, eg[:], 1.0, None, ALU.add).then_inc(dve_own, 1)
                            dve.wait_ge(dve_own, own.up())
                            nc.vector.reciprocal(g_nat, g_nat).then_inc(free[j % 2], 1)
                    if 0 < j <= NJ and u % JOB_UNITS == 0 and jobs[j - 1][0] >= 2 and jobs[j - 1][1] in "qk":
                        what = jobs[j - 1][1]
                        n = 4 * L + (jobs[j - 1][0] - 2) * 2 + "qk".index(what)
                        dve.wait_ge(sq_sum, n + 1)
                        refine(kr, kss, hx, ht, 1.0 / P, sq_r, n + 1)
                        v = (q_nat if what == "q" else k_nat).rearrange("p b (h n) -> p (b h) n", n=P)
                        nc.vector.tensor_tensor(v, v, wide(kr, 8), ALU.mult).then_inc(q_done if what == "q" else k_done, 1)
                    for name, q, p in steps.get(u, ()):
                        nq, np_ = 4 * L + q, 8 * L + 2 * q + p
                        fx = q >= 2
                        if name == "qk":
                            kp = X[:, 2:4].rearrange("p a n -> p (a n)")
                            kv = kT[:].rearrange("p h n -> p (h n)")
                            dve.wait_ge(qkT_ps, nq + 1)
                            if fx:
                                nc.vector.tensor_scalar(kv, kp, gain[:, NG_QK + 2 + L:NG_QK + 3 + L], None, ALU.mult)\
                                  .then_inc(kT_ready, 1)
                            else:
                                nc.vector.tensor_copy(kv, kp).then_inc(kT_ready, 1)
                        elif name == "scores" and not fx:
                            dve.wait_ge(z_scaled, 4 * L + 2 * q + p + 1)
                            dve.wait_ge(z_ln, 4 * L + 2 * q + p + 1)
                            nc.vector.scalar_tensor_tensor(out=sp[:], in0=zs, scalar=0.0, in1=t1, op0=ALU.max,
                                                           op1=ALU.add).then_inc(dve_own, 1)
                            dve.wait_ge(dve_own, own.up())
                            nc.vector.tensor_tensor(sp[:], sp[:], both(sb_keep), ALU.mult).then_inc(sp_ready, 1)
                            nc.vector.tensor_tensor(zs, zs, both(sb_neg), ALU.add).then_inc(dve_own, 1)
                            own.up()
                        elif name == "scores":
                            dve.wait_ge(z_ps, np_ + 1)
                            for a in range(2):
                                hd = 4 * (q - 2) + 2 * p + a
                                for s, e, n in ((0, P, 0), (P, PW, 1)):
                                    ins = nc.vector.scalar_tensor_tensor(
                                        out=zs[:, a, s:e], in0=X[:, a, s:e], scalar=cum[:, n, hd:hd + 1],
                                        in1=fx_neg[:, s:e], op0=ALU.add, op1=ALU.add)
                            ins.then_inc(dve_own, 1)
                            dve.wait_ge(dve_own, own.up())
                            for a in range(2):
                                for s, e, n in ((0, P, 0), (P, PW, 1)):
                                    ins = nc.vector.tensor_reduce(nm[:, 2 * a + n:2 * a + n + 1], zs[:, a, s:e],
                                                                  AX.X, ALU.max, negate=True)
                            ins.then_inc(m_ready, 1)
                        elif name == "second" and not fx:
                            dve.wait_ge(rev_ps, 4 * L + 2 * q + p + 1)
                            dve.wait_ge(dve_own, own.n)
                            nc.vector.tensor_tensor(zs, zs, X[:, 2:4, 0:PW], ALU.subtract).then_inc(arg_ready, 1)
                        elif name == "values":
                            po = X[:, 0].rearrange("p (g n) -> p g n", n=P)
                            dve.wait_ge(o_ps, np_ + 1)
                            if fx:
                                dve.wait_ge(p_ready, 4 * L + 2 * (q - 2) + p + 1)
                                nc.vector.reciprocal(rl, lsum).then_inc(dve_own, 1)
                                dve.wait_ge(dve_own, own.up())
                                nc.vector.tensor_tensor(ob[:], po, wide(rl, 4), ALU.mult).then_inc(dve_own, 1)
                            else:
                                nc.vector.tensor_copy(ob[:], po).then_inc(dve_own, 1)
                            dve.wait_ge(dve_own, own.up())
                            sq = scr[:, 2 * PW:2 * PW + 4 * P].rearrange("p (g n) -> p g n", n=P)
                            nc.vector.tensor_tensor(sq, ob[:], ob[:], ALU.mult).then_inc(dve_own, 1)
                            dve.wait_ge(dve_own, own.up())
                            nc.vector.reduce_sum(hss[:, 0:4], sq, AX.X).then_inc(o_sum, 1)
                            dve.wait_ge(o_sum, np_ + 1)
                            refine(hr[:, 0:4], hss[:, 0:4], hx[:, 0:4], ht[:, 0:4], 1.0 / P, o_r, np_ + 1)
                            if fx:
                                nc.vector.tensor_tensor(ob[:], ob[:], wide(hr[:, 0:4], 4), ALU.mult).then_inc(dve_own, 1)
                                dve.wait_ge(dve_own, own.up())
                                gg = g_nat[:, :, 2 * p * P:(2 * p + 2) * P]
                                o2 = ob[:].rearrange("p (b a) n -> p b (a n)", b=2)
                                nc.vector.tensor_tensor(o2, o2, gg, ALU.mult).then_inc(o_normed, 1)
                            else:
                                nc.vector.tensor_tensor(ob[:], ob[:], wide(hr[:, 0:4], 4), ALU.mult).then_inc(o_normed, 1)
                        elif name == "turn":
                            for a in range(2):
                                hd = 4 * q + 2 * p + a
                                g = NG_HEAD + 2 * L * HEADS + hd
                                dve.wait_ge(oT_hi, 2 * np_ + 2)
                                ins = nc.vector.scalar_tensor_tensor(
                                    out=o_lo[:, hd, :].rearrange("p (b n) -> p b n", b=2),
                                    in0=X[:, 1].rearrange("p (b a n) -> p a b n", b=2, a=2)[:, a],
                                    scalar=gain[:, g:g + 1],
                                    in1=o_hi[:, hd, :].rearrange("p (b n) -> p b n", b=2).bitcast(F32),
                                    op0=ALU.mult, op1=ALU.subtract)
                            ins.then_inc(oT_ready, 1)
                    if u >= PROJ_UNITS and out_units[u - PROJ_UNITS][1] == JOB_UNITS - 1:
                        c = out_units[u - PROJ_UNITS][0]
                        add_to_h(c, c % 2, U0 + u + 1)
                norm(2 * L + 1)

                F0, G0, A0, NG = ffn_start[layer], groups_before[layer], ffn_uses[layer], GROUPS[layer]

                F1 = F0 + UP_UNITS

                def gate_silu(n, per=0, i=None):
                    dve.wait_ge(g_exp, lin(gexp[L] + 2 + n + 1, per, i))
                    nc.vector.tensor_scalar(eg[:], eg[:], 1.0, None, ALU.add).then_inc(dve_own, 1)
                    dve.wait_ge(dve_own, own.up())
                    nc.vector.reciprocal(eg[:], eg[:]).then_inc(dve_own, 1)
                    dve.wait_ge(dve_own, own.up())
                    nc.vector.tensor_tensor(silu, acc[:, 0], eg[:], ALU.mult).then_inc(free[0], 1)

                def hidden(n, per=0, i=None):
                    dve.wait_ge(used, lin(F1 + GROUP_UNITS * n + UP_UNITS, GROUP_UNITS * per, i))
                    dve.wait_ge(free[0], lin(A0 + 3 * n + 1, 3 * per, i))
                    if L == 0:
                        nc.vector.tensor_tensor(hid, acc[:, 1], silu, ALU.mult).then_inc(free[1], 1)
                    else:
                        for b in range(BLOCKS):
                            at = slice(n, n + 1) if i is None else bass.ds(i + n, 1)
                            ins = nc.vector.scalar_tensor_tensor(out=hid[:, b], in0=acc[:, 1, b],
                                                                 scalar=gates[:, b, at], in1=silu[:, b],
                                                                 op0=ALU.mult, op1=ALU.mult)
                        ins.then_inc(free[1], 1)

                def hidden_lo(n, per=0, i=None):
                    dve.wait_ge(hT_hi, lin(G0 + n + 1, per, i))
                    nc.vector.tensor_tensor(o_lo[:, 0:GC].rearrange("p c n -> p (c n)"),
                                            X[:, 0:2].rearrange("p a n -> p (a n)"),
                                            o_hi[:, 0:GC].rearrange("p c n -> p (c n)").bitcast(F32),
                                            ALU.subtract).then_inc(hT_ready, 1)

                for u in range(UP_UNITS):
                    split_lo(F0 + u + LEAD)
                    if u in LATE_QUARTERS:
                        input_lo(2 * L + 1, LATE_QUARTERS[u])
                gate_silu(0)
                if L == 1:
                    dve.wait_ge(rt_ps, 1)
                    nc.vector.tensor_copy(gts, X[:, 2, 0:16].rearrange("p (b n) -> p b n", b=2)).then_inc(dve_own, 1)
                    dve.wait_ge(dve_own, own.up())
                    for b in range(BLOCKS):
                        nc.vector.max(top[:, b], gts[:, b]).then_inc(dve_own, 1)
                        own.up()
                    dve.wait_ge(dve_own, own.n)
                    for b in range(BLOCKS):
                        nc.vector.max_index(topi[:, b], top[:, b], gts[:, b])
                        ins = nc.vector.tensor_scalar(lg[:, b], top[:, b], top[:, b, 0:1], None, ALU.subtract)
                    ins.then_inc(rt_max, 1)
                    dve.wait_ge(rt_max, 1)
                    nc.vector.tensor_copy(topf[:], topi[:]).then_inc(dve_own, 1)
                    dve.wait_ge(dve_own, own.up())
                    dve.wait_ge(rt_exp, 1)
                    for b in range(BLOCKS):
                        nc.vector.tensor_tensor(gt1[:, b, 0:1], eq[:, b, 0:1], eq[:, b, 1:2], ALU.add).then_inc(dve_own, 1)
                        own.up()
                    dve.wait_ge(dve_own, own.n)
                    nc.vector.reciprocal(gt1[:, :, 1:2], gt1[:, :, 0:1]).then_inc(dve_own, 1)
                    dve.wait_ge(dve_own, own.up())
                    for b in range(BLOCKS):
                        nc.vector.tensor_scalar(gt1[:, b, 2:4], eq[:, b, 0:2], gt1[:, b, 1:2], None, ALU.mult)\
                          .then_inc(dve_own, 1)
                        own.up()
                    dve.wait_ge(dve_own, own.n)
                    for b in range(BLOCKS):
                        nc.vector.tensor_scalar(gts[:, b], iota8[:], topf[:, b, 0:1], gt1[:, b, 2:3], ALU.is_equal,
                                                ALU.mult)
                        nc.vector.tensor_scalar(lg[:, b], iota8[:], topf[:, b, 1:2], gt1[:, b, 3:4], ALU.is_equal,
                                                ALU.mult).then_inc(dve_own, 1)
                        own.up()
                    dve.wait_ge(dve_own, own.n)
                    for b in range(BLOCKS):
                        for s in range(2):
                            ins = nc.vector.tensor_tensor(gates[:, b].rearrange("p (e s) -> p e s", s=2)[:, :, s],
                                                          gts[:, b], lg[:, b], ALU.add)
                    ins.then_inc(gates_ready, 1)
                    dve.wait_ge(gates_ready, 1)
                F1 = F0 + UP_UNITS
                with dve.Fori(0, NG - 1) as i:
                    own.enter(i, OWN_DVE_GROUP)
                    for u in range(GROUP_UNITS):
                        split_lo(F1 + u + LEAD, GROUP_UNITS, i)
                        if u == UP_UNITS - 1:
                            hidden(0, 1, i)
                        if u == TURN_AT:
                            hidden_lo(0, 1, i)
                        if u == 2 * UP_UNITS - 1:
                            gate_silu(1, 1, i)
                        if u >= 2 * UP_UNITS and u % DOWN_UNITS == DOWN_UNITS - 1:
                            c = (u - 2 * UP_UNITS) // DOWN_UNITS
                            add_to_h(c, 1 - c % 2, lin(F1 + u + 1, GROUP_UNITS, i))
                    own.leave(NG - 1)
                F2 = F1 + GROUP_UNITS * (NG - 1)
                for u in range(GROUP_UNITS - UP_UNITS):
                    split_lo(F2 + u + LEAD)
                    if u == UP_UNITS - 1:
                        hidden(NG - 1)
                        hidden_lo(NG - 1)
                    if u >= UP_UNITS and u % DOWN_UNITS == DOWN_UNITS - 1:
                        c = (u - UP_UNITS) // DOWN_UNITS
                        add_to_h(c, 1 - c % 2, F2 + u + 1)
            dve.wait_ge(ss_ready, 5)
            refine(rr, ss, xx, tt, 1.0 / D, ss_ready, 5)
            dve.wait_ge(fin_in, 16)
            for b in range(BLOCKS):
                nc.vector.scalar_tensor_tensor(out=h[:, b, :], in0=h[:, b, :], scalar=rr[:, b:b + 1], in1=scr[:, 0:D],
                                               op0=ALU.mult, op1=ALU.mult).then_inc(r_ready, 1)

        @block.tensor
        def _(pe):
            def products(lhs_hi, lhs_lo, k0, s, first, last, u, per=0, i=None):
                slot = u % SPLIT_SLOTS
                pe.wait_ge(lo_ready, lin(u + 1, per, i))
                for c in range(UNIT_CHUNKS):
                    for b in range(BLOCKS):
                        hi = lhs_hi[:, k0 + c, b * P:(b + 1) * P]
                        lo = lhs_lo[:, k0 + c, b * P:(b + 1) * P]
                        dst = acc[:, s, b]
                        nc.tensor.matmul(dst, hi, w_hi[:, slot, c], start=first and c == 0, stop=False)
                        nc.tensor.matmul(dst, hi, w_lo[:, slot, c], start=False, stop=False)
                        ins = nc.tensor.matmul(dst, lo, w_hi[:, slot, c], start=False,
                                               stop=last and c == UNIT_CHUNKS - 1)
                return ins

            def turn_input(n, quarter):
                pe.wait_ge(xn_ready, 4 * n + quarter + 1)
                if quarter >= 2:
                    pe.wait_ge(a_ready, CH * n + 4 * (quarter - 1))
                for k in range(4):
                    for b in range(BLOCKS):
                        bank = 2 * (quarter % 2) + k // 2
                        at = (k % 2) * 256 + b * P
                        ins = nc.tensor.transpose(X[:, bank, at:at + P], xn[:, quarter % 2, b, k * P:(k + 1) * P], ident[:])
                ins.then_inc(xnT_ps, 1)

            def thin_products(n, dst, signal):
                for b in range(BLOCKS):
                    for k in range(CH):
                        hi, lo = a_hi[:, k, b * P:(b + 1) * P], a_lo[:, k, b * P:(b + 1) * P]
                        d = dst[:, b * HEADS:(b + 1) * HEADS]
                        nc.tensor.matmul(d, hi, thin_hi[:, n, k], start=k == 0, stop=False)
                        nc.tensor.matmul(d, hi, thin_lo[:, n, k], start=False, stop=False)
                        ins = nc.tensor.matmul(d, lo, thin_hi[:, n, k], start=False, stop=k == CH - 1)
                ins.then_inc(signal, 1)

            pe.wait_ge(consts, N_CONSTS)
            pe.wait_ge(thin_ready, 1)
            nc.tensor.transpose(X[:, 3, 0:NROWS], rows[0:NROWS, :], ident[0:NROWS, 0:NROWS]).then_inc(gain_ps, 1)

            for layer in range(DEPTH):
                L = layer
                U0 = layer_start[layer]
                turn_input(2 * L, 0)
                if layer == 0:
                    pe.wait_ge(gain_ready, 1)
                turn_input(2 * L, 1)
                for u in range(ATT_UNITS):
                    if u < PROJ_UNITS:
                        j, ju = u // JOB_UNITS, u % JOB_UNITS
                        s, use = j % 2, att_uses[layer] + j // 2
                        if ju == 0 and use > 0:
                            pe.wait_ge(free[s], use)
                        if j == 0:
                            if ju in (2, 4):
                                turn_input(2 * L, ju // 2 + 1)
                            pe.wait_ge(a_ready, CH * 2 * L + UNIT_CHUNKS * (ju + 1))
                        first, last, lhs, k0 = ju == 0, ju == JOB_UNITS - 1, (a_hi, a_lo), UNIT_CHUNKS * ju
                    else:
                        c, ju = out_units[u - PROJ_UNITS]
                        s, use = c % 2, att_uses[layer] + NJ // 2 + c // 2
                        if ju == 0:
                            pe.wait_ge(free[s], use)
                        if c == 0:
                            pe.wait_ge(oT_ready, 8 * L + ju + 1)
                        first, last, lhs, k0 = ju == 0, ju == JOB_UNITS - 1, (o_hi, o_lo), UNIT_CHUNKS * ju
                    ins = products(*lhs, k0, s, first, last, U0 + u)
                    ins.then_inc(used, 1)
                    if u == JOB_UNITS - 1:
                        thin_products(L, X[:, 0], f_ps)
                    if u == JOB_UNITS + 1:
                        pe.wait_ge(f_log, L + 1)
                        nc.tensor.matmul(X[:, 1, 0:HEADS], tri_le[:], logf[:, 0], start=True, stop=True)
                        nc.tensor.matmul(X[:, 1, HEADS:2 * HEADS], ones[:], logf[:, 0], start=True, stop=False)
                        nc.tensor.matmul(X[:, 1, HEADS:2 * HEADS], tri_le[:], logf[:, 1], start=False, stop=True)
                        nc.tensor.matmul(X[0:HEADS, 2, 0:P], logf[:, 0], tri_le[:], start=True, stop=True)
                        nc.tensor.matmul(X[0:HEADS, 2, P:2 * P], logf[:, 0], ones[:], start=True, stop=False)
                        nc.tensor.matmul(X[0:HEADS, 2, P:2 * P], logf[:, 1], tri_le[:], start=False, stop=True)\
                          .then_inc(c_ps, 1)
                    for name, q, p in steps.get(u, ()):
                        nq, np_ = 4 * L + q, 8 * L + 2 * q + p
                        fx = q >= 2
                        if name == "qk":
                            if fx:
                                pe.wait_ge(q_done, 4 * L + 2 * (q - 2) + 2)
                                pe.wait_ge(k_done, 4 * L + 2 * (q - 2) + 2)
                            else:
                                jq = 3 * q
                                pe.wait_ge(free[jq % 2], att_uses[layer] + jq // 2 + 1)
                                pe.wait_ge(free[(jq + 1) % 2], att_uses[layer] + (jq + 1) // 2 + 1)
                            if q == 0:
                                pe.wait_ge(c_ready, L + 1)
                            else:
                                pe.wait_ge(oT_ready, np_)
                            for n, v in enumerate((q_nat, k_nat)):
                                for hd in range(QUAD):
                                    for b in range(BLOCKS):
                                        at = (hd % 2) * 256 + b * P
                                        ins = nc.tensor.transpose(X[:, 2 * n + hd // 2, at:at + P],
                                                                  v[:, b, hd * P:(hd + 1) * P], ident[:])
                            ins.then_inc(qkT_ps, 1)
                        elif name == "scores":
                            pe.wait_ge(qT_ready, nq + 1)
                            pe.wait_ge(kT_ready, nq + 1)
                            if p:
                                pe.wait_ge(oT_ready, np_)
                            if fx:
                                pe.wait_ge(c_ready, L + 1)
                            for a in range(2):
                                hd = 2 * p + a
                                qh, kh = qT[:, hd], kT[:, hd]
                                if fx:
                                    hot = onehot[:, 4 * (q - 2) + hd, :]
                                    nc.tensor.matmul(X[:, a, 0:P], qh[:, 0:P], kh[:, 0:P], start=True, stop=False)
                                    nc.tensor.matmul(X[:, a, 0:P], hot, ncT[:, 0:P], start=False, stop=True)
                                    nc.tensor.matmul(X[:, a, P:PW], qh[:, P:2 * P], kh, start=True, stop=False)
                                    ins = nc.tensor.matmul(X[:, a, P:PW], hot, ncT[:], start=False, stop=True)
                                else:
                                    nc.tensor.matmul(X[:, a, 0:2 * P], kh[:, 0:P], qh, start=True, stop=True)
                                    ins = nc.tensor.matmul(X[:, a, 2 * P:PW], kh[:, P:2 * P], qh[:, P:2 * P],
                                                           start=True, stop=True)
                            ins.then_inc(z_ps, 1)
                        elif name == "second" and not fx:
                            pe.wait_ge(sp_ready, 4 * L + 2 * q + p + 1)
                            for a in range(2):
                                nc.tensor.matmul(X[:, 2 + a, 0:PW], tri_ge[:], sp[:, a], start=True, stop=False)
                                ins = nc.tensor.matmul(X[:, 2 + a, P:2 * P], ones[:], sp[:, a, 2 * P:PW],
                                                       start=False, stop=True)
                            ins.then_inc(rev_ps, 1)
                        elif name == "second":
                            pe.wait_ge(p_ready, 4 * L + 2 * (q - 2) + p + 1)
                            for a in range(2):
                                for n in range(3):
                                    ins = nc.tensor.transpose(X[:, 2 + a, n * P:(n + 1) * P],
                                                              sp[:, a, n * P:(n + 1) * P], ident[:])
                            ins.then_inc(pT_ps, 1)
                        elif name == "values":
                            pe.wait_ge(w_ready, np_ + 1)
                            jv = max(j for j in range(NJ) if jobs[j][0] == q and jobs[j][1] == "v")
                            pe.wait_ge(free[jv % 2], att_uses[layer] + jv // 2 + 1)
                            for a in range(2):
                                v = v_nat[:, :, (2 * p + a) * P:(2 * p + a + 1) * P]
                                lo, hi_ = a * P, (2 + a) * P
                                nc.tensor.matmul(X[:, 0, lo:lo + P], wT[:, a, 0:P], v[:, 0], start=True, stop=True)
                                nc.tensor.matmul(X[:, 0, hi_:hi_ + P], wT[:, a, P:2 * P], v[:, 0], start=True, stop=False)
                                ins = nc.tensor.matmul(X[:, 0, hi_:hi_ + P], wT[:, a, 2 * P:PW], v[:, 1], start=False,
                                                       stop=True)
                            ins.then_inc(o_ps, 1)
                        elif name == "turn":
                            pe.wait_ge(o_normed, np_ + 1)
                            for n in range(4):
                                ins = nc.tensor.transpose(X[:, 1, n * P:(n + 1) * P], ob[:, n], ident[:])
                            ins.then_inc(oT_ps, 1)

                F0, G0, A0, NG = ffn_start[layer], groups_before[layer], ffn_uses[layer], GROUPS[layer]
                turn_input(2 * L + 1, 0)
                turn_input(2 * L + 1, 1)

                def input_job(s, use, u0, uses_per=0, per=0, i=None, after=None, fresh=None):
                    pe.wait_ge(free[s], lin(use, uses_per, i))
                    for u in range(JOB_UNITS):
                        if fresh is not None:
                            if u in (2, 4):
                                turn_input(fresh, u // 2 + 1)
                            pe.wait_ge(a_ready, CH * fresh + UNIT_CHUNKS * (u + 1))
                        ins = products(a_hi, a_lo, UNIT_CHUNKS * u, s, u == 0, u == JOB_UNITS - 1, u0 + u, per, i)
                        ins.then_inc(used, 1)
                        if after is not None:
                            after(u)

                def turn_hidden(n, per=0, i=None):
                    pe.wait_ge(free[1], lin(A0 + 3 * n + 1, 3 * per, i))
                    if i is None or per:
                        pe.wait_ge(hT_ready, lin(G0 + n, per, i)) if G0 + n > 0 else None
                    for c in range(GC):
                        for b in range(BLOCKS):
                            at = (c % 2) * 256 + b * P
                            ins = nc.tensor.transpose(X[:, c // 2, at:at + P], hid[:, b, c * P:(c + 1) * P], ident[:])
                    ins.then_inc(hT_ps, 1)

                def down_jobs(n, gate_between, u0, per=0, i=None):
                    pe.wait_ge(hT_ready, lin(G0 + n + 1, per, i))
                    for c in range(NCOL):
                        s = 1 - c % 2
                        use = A0 + 3 * n + c // 2 + 1 + (1 if s == 0 and gate_between else 0)
                        pe.wait_ge(free[s], lin(use, 3 * per, i))
                        for u in range(DOWN_UNITS):
                            ins = products(o_hi, o_lo, UNIT_CHUNKS * u, s, u == 0, u == DOWN_UNITS - 1,
                                           u0 + DOWN_UNITS * c + u, GROUP_UNITS * per, i)
                            ins.then_inc(used, 1)

                input_job(0, A0, F0, fresh=2 * L + 1)
                if layer == 1:
                    thin_products(2, X[:, 2], rt_ps)
                F1 = F0 + UP_UNITS
                with pe.Fori(0, NG - 1) as i:
                    input_job(1, A0, F1, 3, GROUP_UNITS, i)

                    def then(u):
                        if u == TURN_AT - UP_UNITS:
                            turn_hidden(0, 1, i)
                    input_job(0, A0 + 1, F1 + UP_UNITS, 3, GROUP_UNITS, i, after=then)
                    down_jobs(0, True, F1 + 2 * UP_UNITS, 1, i)
                F2 = F1 + GROUP_UNITS * (NG - 1)
                input_job(1, A0 + 3 * (NG - 1), F2)
                turn_hidden(NG - 1)
                down_jobs(NG - 1, False, F2 + UP_UNITS)


_INS = ["x", "attn_norm", "w_in", "b_forget", "fox_q_norm", "fox_k_norm", "sb_out_norm", "fox_out_norm", "w_out",
        "ffn_norm", "dense_w_gate", "dense_w_up", "dense_w_down", "router_w", "moe_w_gate", "moe_w_up",
        "moe_w_down", "final_norm"]


def kernel(**inputs):
    import numpy as _np
    import concourse.bacc as _bacc
    from concourse import mybir as _mybir
    from concourse.bass_utils import run_bass_kernel_spmd as _run

    nc = _bacc.Bacc("TRN2", target_bir_lowering=False, num_devices=1)
    arrays, args = {}, []
    for name in _INS:
        a = _np.ascontiguousarray(inputs[name])
        arrays[f"in_{name}"] = a
        args.append(nc.dram_tensor(f"in_{name}", a.shape, _mybir.dt.from_np(a.dtype), kind="ExternalInput").ap())
    shape = arrays["in_x"].shape
    args.append(nc.dram_tensor("out_0", shape, _mybir.dt.float32, kind="ExternalOutput").ap())
    trunk(nc, *args)
    r = _run(nc, [arrays], core_ids=[0])
    return r.results[0]["out_0"]
```

```python
from contextlib import ExitStack

import concourse.bass as bass
from concourse import mybir

F32 = mybir.dt.float32
F32R = mybir.dt.float32r
U32 = mybir.dt.uint32
ALU = mybir.AluOpType
ACT = mybir.ActivationFunctionType
AX = mybir.AxisListType

P = 128
COLS = 512
BLOCKS = 2
UNIT_CHUNKS = 2
TILE_UNITS = 2
RAW_SLOTS = 4
SPLIT_SLOTS = 4
POOL_UNIT = 3
LEAD = 3
QUAD = 4
QUAD_PAIRS = 2
NEG = -1e30
EPS = 1e-6


class Own:

    def __init__(self):
        self.n, self.i, self.per = 0, None, 0

    def up(self):
        self.n += 1
        return self.n if self.i is None else self.i * self.per + self.n

    def now(self):
        return self.n if self.i is None else self.i * self.per + self.n

    def enter(self, i, per):
        self.i, self.per, self.start = i, per, self.n

    def leave(self, trips):
        assert self.n - self.start == self.per, (self.n, self.start, self.per)
        self.n, self.i = self.start + self.per * trips, None


def lin(const, per=0, i=None):
    return const if i is None else i * per + const


def trunk(nc, x, attn_norm, w_in, b_forget, fox_q_norm, fox_k_norm, sb_out_norm, fox_out_norm, w_out,
          ffn_norm, dense_w_gate, dense_w_up, dense_w_down, router_w, moe_w_gate, moe_w_up, moe_w_down,
          final_norm, out):
    D = x.shape[2]
    DEPTH = w_in.shape[0]
    CH = D // P
    HEADS = sb_out_norm.shape[1] // P
    W = sb_out_norm.shape[1]
    EXPERTS = router_w.shape[2]
    F_EXP = moe_w_gate.shape[3]
    SCALE = float(P) ** -0.5
    assert x.shape[1] == BLOCKS * P and DEPTH == 2 and CH == 16 and HEADS == 8 and EXPERTS == 8
    NCOL = D // COLS
    GC = COLS // P

    JOB_UNITS = CH // UNIT_CHUNKS
    jobs = []
    for quad in range(4):
        base = (quad % 2) * COLS + (0 if quad < 2 else 3 * W)
        for n, what in enumerate("qkv" if quad < 2 else "qkvg"):
            jobs.append((quad, what, base + n * W))
    NJ = len(jobs)
    PROJ_UNITS = NJ * JOB_UNITS
    out_units = []
    for c in (0, 2):
        for cc, us in ((c, range(6)), (c + 1, range(6)), (c, (6, 7)), (c + 1, (6, 7))):
            out_units += [(cc, u) for u in us]
    ATT_UNITS = PROJ_UNITS + len(out_units)
    F_AT = 2 * JOB_UNITS
    quad_start = [(1 + max(j for j in range(NJ) if jobs[j][0] == q)) * JOB_UNITS for q in range(4)]
    PAIR_STEPS = (("scores", 0, 0), ("second", 3, 2), ("values", 5, 3), ("turn", 8, 5))
    steps = {}
    for q in range(4):
        steps.setdefault(quad_start[q], []).append(("qk", q, 0))
        for p in range(QUAD_PAIRS):
            for name, at, late in PAIR_STEPS:
                u = quad_start[q] + (1 + 5 * p + late if q == 3 else 2 + 10 * p + at)
                steps.setdefault(u, []).append((name, q, p))

    GROUPS = [dense_w_gate.shape[2] // COLS, EXPERTS * F_EXP // COLS]
    UP_UNITS, DOWN_UNITS = JOB_UNITS, GC // UNIT_CHUNKS
    GROUP_UNITS = 2 * UP_UNITS + NCOL * DOWN_UNITS
    TURN_AT = UP_UNITS + 1
    ffn_start = [ATT_UNITS, 2 * ATT_UNITS + GROUPS[0] * GROUP_UNITS]
    layer_start = [0, ATT_UNITS + GROUPS[0] * GROUP_UNITS]
    HALVES = F_EXP // COLS
    M0 = ffn_start[1]
    DOWN0 = 2 * HALVES * UP_UNITS
    down_units = [(c, k) for cs in ((0, 1),) for k0 in (0, 2) for c in cs for k in (k0, k0 + 1)]
    down_units += [(c, k) for c in range(2, NCOL) for k in range(HALVES * DOWN_UNITS)]
    PASS_UNITS = DOWN0 + len(down_units)
    PASS_TILES = PASS_UNITS // TILE_UNITS
    down_end = {DOWN0 + n: c for n, (c, k) in enumerate(down_units) if k == HALVES * DOWN_UNITS - 1}
    put_at = {u + 2 if c < NCOL - 1 else u: c for u, c in down_end.items()}
    pick_at = {DOWN0 + 3: 0, DOWN0 + 6: 1, DOWN0 + 9: 2, PASS_UNITS - 1: 3}
    turn_at = {2 * UP_UNITS + 1: 0, DOWN0 + 1: 1}
    MAX_PASSES = EXPERTS + (2 * BLOCKS * P - EXPERTS) // P
    TABLE = 16
    OWN_DVE_PASS = 9
    assert MAX_PASSES < TABLE and M0 % 8 == 0 and PASS_UNITS % 8 == 0
    groups_before = [0, GROUPS[0]]
    ATT_USES = (NJ + NCOL) // 2
    att_uses = [0, ATT_USES + 3 * GROUPS[0]]
    ffn_uses = [u + ATT_USES for u in att_uses]
    LATE_QUARTERS = {1: 2, 3: 3}
    SILU_STEPS = 2 + BLOCKS
    OWN_DVE_GROUP = SILU_STEPS
    silu_at = {2 * UP_UNITS - 1: 0, 2 * UP_UNITS: 1, 2 * UP_UNITS + 2: 2, 2 * UP_UNITS + 4: 3}
    gexp = [0, 2 + GROUPS[0]]

    with ExitStack() as ctx:
        def sb(name, shape, dt=F32):
            return ctx.enter_context(nc.sbuf_tensor(name, shape, dt))

        def sem(name):
            return ctx.enter_context(nc.semaphore(name))

        raw = sb("raw", [P, RAW_SLOTS, TILE_UNITS, UNIT_CHUNKS, COLS])
        w_hi = sb("w_hi", [P, SPLIT_SLOTS, UNIT_CHUNKS, COLS], F32R)
        w_lo = sb("w_lo", [P, SPLIT_SLOTS, UNIT_CHUNKS, COLS], F32R)
        h = sb("h", [P, BLOCKS, D])
        a_hi = sb("a_hi", [P, CH, BLOCKS * P], F32R)
        a_lo = sb("a_lo", [P, CH, BLOCKS * P], F32R)
        o_hi = sb("o_hi", [P, CH, BLOCKS * P], F32R)
        o_lo = sb("o_lo", [P, CH, BLOCKS * P], F32R)
        scr = sb("scr", [P, 4 * COLS])
        xn = scr[:].rearrange("p (s b n) -> p s b n", s=2, b=BLOCKS)
        PW = 3 * P
        zs = scr[:, 0:2 * PW].rearrange("p (a n) -> p a n", a=2)
        t1 = scr[:, 2 * PW:4 * PW].rearrange("p (a n) -> p a n", a=2)
        sp = sb("sp", [P, 2, PW])
        wT = sb("wT", [P, 2, PW])
        nat = sb("nat", [P, 4, BLOCKS, COLS])
        q_nat, k_nat, v_nat, g_nat = (nat[:, n] for n in range(4))
        silu, hid = nat[:, 1], nat[:, 2]
        silu1, hid1 = nat[:, 2, 0], nat[:, 3, 0]
        eg = sb("eg", [P, BLOCKS, COLS])
        qT = sb("qT", [P, QUAD, BLOCKS * P])
        kT = sb("kT", [P, QUAD, BLOCKS * P])
        ob = sb("ob", [P, 4, P])
        ident = sb("ident", [P, P])
        ones = sb("ones", [P, P])
        tri_ge = sb("tri_ge", [P, P])
        tri_le = sb("tri_le", [P, P])
        sb_off = sb("sb_off", [P, PW])
        fx_neg = sb("fx_neg", [P, PW])
        onehot = sb("onehot", [HEADS, HEADS, P])
        thin_hi = sb("thin_hi", [P, 3, CH, HEADS], F32R)
        thin_lo = sb("thin_lo", [P, 3, CH, HEADS], F32R)
        thin = eg[:, 0, 0:3 * P].rearrange("p (t c n) -> p t c n", t=3, c=CH)
        rows = eg[:, 1, 0:P]
        NG_ATT, NG_FFN, NG_HEAD, NG_QK = 0, 2 * CH, 4 * CH, 4 * CH + 4 * HEADS
        NROWS = NG_QK + 4
        gain = sb("gain", [P, P])
        gq = sb("gq", [P, 2])
        bf = sb("bf", [HEADS, DEPTH])
        epsc = sb("epsc", [P, 1])
        sm = sb("sm", [P, 192])
        ss, rr, xx, tt = (sm[:, 2 * n:2 * n + 2] for n in range(4))
        hss, hr, hx, ht = (sm[:, 8 + 8 * n:16 + 8 * n] for n in range(4))
        kss, kr = (sm[:, 40 + 8 * n:48 + 8 * n] for n in range(2))
        fz, fl, fm, fc = (eg[0:HEADS, n // 2, n % 2 * BLOCKS * P:(n % 2 + 1) * BLOCKS * P] for n in range(4))
        rt_logits = eg[0:EXPERTS, 0, 0:BLOCKS * P]
        cum = sm[:, 104:120].rearrange("p (b n) -> p b n", b=2)
        nm = sm[:, 120:124]
        lsum = sm[:, 124:128]
        rl = sm[:, 128:132]
        lg, gts, eq = (sm[:, 136 + 16 * n:152 + 16 * n].rearrange("p (b n) -> p b n", b=2) for n in range(3))
        top, gt1 = (sb(f"top{n}", [P, 2, 8]) for n in range(2))
        topi = sb("topi", [P, 2, 8], U32)
        topf = sb("topf", [P, 2, 8])
        count = sp[:].rearrange("p a n -> p (a n)")[:, 0:P]
        pick_a = wT[:].rearrange("p a n -> p (a n)")[:, 0:2 * P].rearrange("p (b n) -> p b n", b=2)
        pick_b = wT[:].rearrange("p a n -> p (a n)")[:, 2 * P:4 * P].rearrange("p (b n) -> p b n", b=2)
        pick_g = wT[:].rearrange("p a n -> p (a n)")[:, 4 * P:6 * P].rearrange("p (b n) -> p b n", b=2)
        pick = sb("pick", [P, BLOCKS, P], F32R)
        put = sb("put", [P, BLOCKS * P], F32R)
        ident_r = sb("ident_r", [P, P], F32R)
        rt = sb("rt", [P, 96])
        first, second, both_e, where = (rt[:, 16 * n:16 * n + 16].rearrange("p (b e) -> p b e", b=2) for n in range(4))
        n_pass, last_pass, off_e = (rt[:, 64 + 8 * n:72 + 8 * n] for n in range(3))
        pos = rt[:, 88:92]
        slot_gate = rt[:, 92:93]
        hits = ob[:].rearrange("p a n -> p (a n)")[:, 0:TABLE * EXPERTS].rearrange("p (t e) -> p t e", t=TABLE)
        table_f = sb("table_f", [P, TABLE])
        table = sb("table", [P, TABLE + 1], mybir.dt.int32)
        flat = lambda t: t[:].rearrange("p c n -> p (c n)")
        n_hi, n_lo = (flat(t).rearrange("p (b n) -> p b n", b=BLOCKS) for t in (o_hi, o_lo))
        x_hi, x_lo = (flat(t)[:, 0:D].rearrange("p (c n) -> p c n", c=CH) for t in (a_hi, a_lo))
        hT_h, hT_l = (flat(t)[:, D:D + F_EXP].rearrange("p (c n) -> p c n", n=P) for t in (a_hi, a_lo))
        y_h, y_l = (flat(t)[:, D + F_EXP:D + F_EXP + 2 * COLS].rearrange("p (s n) -> p s n", s=2)
                    for t in (a_hi, a_lo))
        gain_row = nat[:, 0:2].rearrange("p a b n -> p (a b n)")
        ncT = sb("ncT", [HEADS, BLOCKS * P])
        acc = ctx.enter_context(nc.psum_tensor("acc", [P, 2, BLOCKS, COLS], F32))
        X = ctx.enter_context(nc.psum_tensor("X", [P, 4, COLS], F32))

        loaded = [sem(f"loaded{s}") for s in range(RAW_SLOTS)]
        hi_ready = sem("hi_ready")
        lo_ready = sem("lo_ready")
        pool_ready = sem("pool_ready")
        used = sem("used")
        free = [sem(f"free{s}") for s in range(2)]
        x_in = [sem(f"x_in{b}") for b in range(BLOCKS)]
        small_in = sem("small_in")
        fin_in = sem("fin_in")
        stored = sem("stored")
        consts = sem("consts")
        gain_ps = sem("gain_ps")
        gain_ready = sem("gain_ready")
        thin_in = sem("thin_in")
        thin_h = sem("thin_h")
        thin_ready = sem("thin_ready")
        ss_ready = sem("ss_ready")
        r_ready = sem("r_ready")
        xn_ready = sem("xn_ready")
        xnT_ps = sem("xnT_ps")
        a_hi_ready = sem("a_hi_ready")
        a_ready = sem("a_ready")
        f_ps = sem("f_ps")
        f_x = sem("f_x")
        f_ln = sem("f_ln")
        f_log = sem("f_log")
        c_ps = sem("c_ps")
        c_ready = sem("c_ready")
        g_exp = sem("g_exp")
        sq_ready = sem("sq_ready")
        sq_sum = sem("sq_sum")
        sq_r = sem("sq_r")
        q_done = sem("q_done")
        k_done = sem("k_done")
        v_done = sem("v_done")
        qkT_ps = sem("qkT_ps")
        qT_ready = sem("qT_ready")
        kT_ready = sem("kT_ready")
        z_ps = sem("z_ps")
        z_scaled = sem("z_scaled")
        z_ln = sem("z_ln")
        sp_ready = sem("sp_ready")
        rev_ps = sem("rev_ps")
        arg_ready = sem("arg_ready")
        m_ready = sem("m_ready")
        p_ready = sem("p_ready")
        pT_ps = sem("pT_ps")
        w_ready = sem("w_ready")
        o_ps = sem("o_ps")
        o_sum = sem("o_sum")
        o_r = sem("o_r")
        o_normed = sem("o_normed")
        oT_ps = sem("oT_ps")
        oT_hi = sem("oT_hi")
        oT_ready = sem("oT_ready")
        rt_ps = sem("rt_ps")
        rt_copied = sem("rt_copied")
        rtT_ps = sem("rtT_ps")
        rt_max = sem("rt_max")
        rt_exp = sem("rt_exp")
        chosen = sem("chosen")
        ranks_ps = sem("ranks_ps")
        table_ready = sem("table_ready")
        row_in = sem("row_in")
        n_ready = sem("n_ready")
        n_hi_ready = sem("n_hi_ready")
        n_lo_ready = sem("n_lo_ready")
        pick_ready = sem("pick_ready")
        picked_ps = sem("picked_ps")
        picked_hi = sem("picked_hi")
        picked_lo = sem("picked_lo")
        put_ps = sem("put_ps")
        put_ready = sem("put_ready")
        slot_ready = sem("slot_ready")
        y_hi_ready = sem("y_hi_ready")
        y_lo_ready = sem("y_lo_ready")
        y_ps = sem("y_ps")
        y_added = sem("y_added")
        hT_ps = sem("hT_ps")
        hT_hi = sem("hT_hi")
        hT_ready = sem("hT_ready")
        act_own = sem("act_own")
        dve_own = sem("dve_own")
        pool_own = sem("pool_own")

        def pools(u):
            return u % 2 == 1 if u >= M0 else u % 4 == POOL_UNIT

        def low_ready(eng, u, per=0, i=None):
            if u >= M0:
                if pools(u):
                    eng.wait_ge(pool_ready, lin(M0 // 4 + (u - M0) // 2 + 1, per // 2, i))
                else:
                    eng.wait_ge(lo_ready, lin(3 * M0 // 4 + (u - M0) // 2 + 1, per // 2, i))
            elif pools(u):
                eng.wait_ge(pool_ready, lin(u // 4 + 1, per // 4, i))
            else:
                eng.wait_ge(lo_ready, lin(3 * (u // 4) + u % 4 + 1, 3 * per // 4, i))

        block = ctx.enter_context(nc.Block())
        N_SMALL = 5 * DEPTH + 2

        @block.sync
        def _(sp_):
            def load(tile, src, per=0, i=None):
                slot = tile % RAW_SLOTS
                if i is not None or tile >= RAW_SLOTS:
                    u = TILE_UNITS * (tile - RAW_SLOTS) + TILE_UNITS - 1
                    low_ready(sp_, u, TILE_UNITS * per, i)
                sp_.dma_start(raw[:, slot].rearrange("p u c n -> p (u c) n"),
                              src.rearrange("(c p) n -> p c n", p=P)).then_inc(loaded[slot], 16)

            def load_wide(tile, w, col, per=0, i=None):
                for t in range(CH // GC):
                    load(tile + t, w[t * COLS:(t + 1) * COLS, col], per, i)

            for b in range(BLOCKS):
                sp_.dma_start(h[:, b, :], x[0, b * P:(b + 1) * P, :]).then_inc(x_in[b], 16)
            for layer in range(DEPTH):
                tile = layer_start[layer] // TILE_UNITS
                for j, (_, _, col) in enumerate(jobs):
                    load_wide(tile + j * CH // GC, w_in[layer], slice(col, col + COLS))
                for n, (c, u) in enumerate(out_units):
                    if n % TILE_UNITS == 0:
                        r = u * UNIT_CHUNKS * P
                        load(tile + (PROJ_UNITS + n) // TILE_UNITS,
                             w_out[layer, r:r + COLS, c * COLS:(c + 1) * COLS])
                tile = ffn_start[layer] // TILE_UNITS
                per_group = GROUP_UNITS // TILE_UNITS
                if layer == 0:
                    wg, wu, wd = dense_w_gate[0], dense_w_up[0], dense_w_down[0]
                    load_wide(tile, wg, slice(0, COLS))
                    tile += CH // GC
                    with sp_.Fori(0, GROUPS[0] - 1) as i:
                        load_wide(tile, wu, bass.ts(i, COLS), per_group, i)
                        load_wide(tile + CH // GC, wg, bass.ds(i * COLS + COLS, COLS), per_group, i)
                        for c in range(NCOL):
                            load(tile + 2 * CH // GC + c, wd[bass.ts(i, COLS), c * COLS:(c + 1) * COLS],
                                 per_group, i)
                    tile += per_group * (GROUPS[0] - 1)
                    last = GROUPS[0] - 1
                    load_wide(tile, wu, slice(last * COLS, (last + 1) * COLS))
                    for c in range(NCOL):
                        load(tile + CH // GC + c, wd[last * COLS:(last + 1) * COLS, c * COLS:(c + 1) * COLS])
                else:
                    wg, wu, wd = moe_w_gate[0], moe_w_up[0], moe_w_down[0]
                    sp_.wait_ge(qkT_ps, 4 * DEPTH)
                    sp_.dma_start(gain_row, ffn_norm[1:2, :].broadcast_to([P, D])).then_inc(row_in, 16)
                    load_wide(tile, wg[0], slice(0, COLS))
                    tile += CH // GC
                    sp_.wait_ge(table_ready, 1)
                    passes = sp_.value_load(table[0:1, TABLE:TABLE + 1], min_val=EXPERTS, max_val=MAX_PASSES)
                    with sp_.Fori(0, passes) as i:
                        e = sp_.value_load(table[0:1, bass.ds(i, 1)], min_val=0, max_val=EXPERTS - 1)
                        t = tile
                        for half in range(HALVES):
                            col = slice(half * COLS, (half + 1) * COLS)
                            if half:
                                load_wide(t, wg[e], col, PASS_TILES, i)
                                t += CH // GC
                            load_wide(t, wu[e], col, PASS_TILES, i)
                            t += CH // GC
                        for n, (c, k) in enumerate(down_units):
                            if n % TILE_UNITS == 0:
                                r = k * UNIT_CHUNKS * P
                                load(t, wd[e][r:r + COLS, c * COLS:(c + 1) * COLS], PASS_TILES, i)
                                t += 1
                        e = sp_.value_load(table[0:1, bass.ds(i + 1, 1)], min_val=0, max_val=EXPERTS - 1)
                        load_wide(t, wg[e], slice(0, COLS), PASS_TILES, i)
                    for slot in range(RAW_SLOTS):
                        sp_.wait_ge(loaded[slot], passes * (16 * PASS_TILES // RAW_SLOTS) + 16 * (tile // RAW_SLOTS))
            sp_.wait_ge(xnT_ps, 4 * 4)
            sp_.dma_start(scr[:, 0:D], final_norm.rearrange("(a n) -> a n", a=1).broadcast_to([P, D]))\
               .then_inc(fin_in, 16)
            for b in range(BLOCKS):
                sp_.wait_ge(r_ready, 1 + b)
                sp_.dma_start(out[0, b * P:(b + 1) * P, :], h[:, b, :]).then_inc(stored, 16)
            sp_.wait_ge(stored, 16 * BLOCKS)

        @block.gpsimd
        def _(pool):
            pool.memset(onehot[:], 0.0).then_inc(pool_own, 1)
            pool.memset(ident[:], 0.0).then_inc(pool_own, 1)
            pool.memset(ones[:], 1.0).then_inc(pool_own, 1)
            pool.memset(sb_off[:], 0.0).then_inc(pool_own, 1)
            pool.memset(fx_neg[:], 0.0).then_inc(pool_own, 1)
            pool.memset(epsc[:], EPS).then_inc(pool_own, 1)
            pool.wait_ge(pool_own, 6)
            pool.affine_select(out=ident[:], in_=ident[:], compare_op=ALU.not_equal, fill=1.0, base=0,
                               pattern=[[-1, P]], channel_multiplier=1).then_inc(consts, 1)
            pool.affine_select(out=tri_ge[:], in_=ones[:], compare_op=ALU.is_ge, fill=0.0, base=0,
                               pattern=[[-1, P]], channel_multiplier=1).then_inc(consts, 1)
            pool.affine_select(out=tri_le[:], in_=ones[:], compare_op=ALU.is_ge, fill=0.0, base=0,
                               pattern=[[1, P]], channel_multiplier=-1).then_inc(consts, 1)
            for at in (0, 2 * P):
                pool.affine_select(out=sb_off[:, at:at + P], in_=sb_off[:, at:at + P], compare_op=ALU.is_gt,
                                   fill=-1.0, base=0, pattern=[[1, P]], channel_multiplier=-1).then_inc(consts, 1)
                pool.affine_select(out=fx_neg[:, at:at + P], in_=fx_neg[:, at:at + P], compare_op=ALU.is_ge,
                                   fill=NEG, base=0, pattern=[[-1, P]], channel_multiplier=1).then_inc(consts, 1)
            pool.affine_select(out=onehot[:], in_=onehot[:], compare_op=ALU.not_equal, fill=1.0, base=0,
                               pattern=[[-1, HEADS], [0, P]], channel_multiplier=1).then_inc(consts, 1)

            def low_parts(u, per, i):
                pool.wait_ge(hi_ready, lin(u + 1, per, i))
                low_ready(pool, u - 1, per, i)
                nc.gpsimd.tensor_tensor(w_lo[:, u % SPLIT_SLOTS],
                                        raw[:, (u // TILE_UNITS) % RAW_SLOTS, u % TILE_UNITS],
                                        w_hi[:, u % SPLIT_SLOTS].bitcast(F32), ALU.subtract).then_inc(pool_ready, 1)

            with pool.Fori(0, M0 // 8) as i:
                low_parts(POOL_UNIT, 8, i)
                low_parts(4 + POOL_UNIT, 8, i)
            low_parts(M0 + 1, 0, None)
            pool.wait_ge(w_ready, 8 * DEPTH)
            nc.gpsimd.iota(count, pattern=[[1, P]], base=0, channel_multiplier=0,
                           allow_small_or_imprecise_dtypes=True).then_inc(pool_own, 1)
            for q in range(4):
                pool.wait_ge(n_hi_ready, q + 1)
                nc.gpsimd.tensor_tensor(n_lo[:, :, q * COLS:(q + 1) * COLS], nat[:, 2 + q % 2],
                                        n_hi[:, :, q * COLS:(q + 1) * COLS].bitcast(F32), ALU.subtract)\
                  .then_inc(n_lo_ready, 1)
            pool.wait_ge(table_ready, 1)
            passes = pool.value_load(table[0:1, TABLE:TABLE + 1], min_val=EXPERTS, max_val=MAX_PASSES)
            with pool.Fori(0, passes * (PASS_UNITS // 8)) as i:
                for n in range(3, 11, 2):
                    low_parts(M0 + n, 8, i)
        N_CONSTS = 8

        @block.scalar
        def _(act):
            own = Own()

            def split_hi(u, per=0, i=None):
                slot = u % SPLIT_SLOTS
                tile = u // TILE_UNITS
                if u % TILE_UNITS == 0:
                    act.wait_ge(loaded[tile % RAW_SLOTS],
                                lin(16 * (tile // RAW_SLOTS + 1), 16 * per // (TILE_UNITS * RAW_SLOTS), i))
                if i is not None or u >= SPLIT_SLOTS:
                    act.wait_ge(used, lin(u - SPLIT_SLOTS + 1, per, i))
                nc.scalar.activation(w_hi[:, slot], raw[:, tile % RAW_SLOTS, u % TILE_UNITS], ACT.Copy)\
                  .then_inc(hi_ready, 1)

            def rsqrt_guess(y, s, n, scale, signal):
                nc.scalar.activation(y, s, ACT.Ln, bias=epsc[:, 0:1], scale=scale).then_inc(act_own, 1)
                act.wait_ge(act_own, own.up())
                nc.scalar.activation(y, y, ACT.Exp, scale=-0.5).then_inc(signal, 1)

            def norm_guess(n):
                for b in range(BLOCKS):
                    if n == 0:
                        act.wait_ge(x_in[b], 16)
                    nc.scalar.activation(scr[:, 0:D], h[:, b, :], ACT.Square, accum_out=ss[:, b:b + 1])\
                      .then_inc(act_own, 1)
                    act.wait_ge(act_own, own.up())
                rsqrt_guess(rr, ss, 2, 1.0 / D, ss_ready)

            def input_hi(n, quarter):
                act.wait_ge(xnT_ps, 4 * n + quarter + 1)
                for k in range(4 * quarter, 4 * quarter + 4):
                    g = (NG_ATT if n % 2 == 0 else NG_FFN) + (n // 2) * CH + k
                    bank = 2 * (quarter % 2) + (k % 4) // 2
                    nc.scalar.activation(a_hi[:, k, :], X[:, bank, (k % 2) * 256:(k % 2) * 256 + 256], ACT.Copy,
                                         scale=gain[:, g:g + 1]).then_inc(a_hi_ready, 1)

            nc.scalar.preload_act_table_set("natural_log_exp_and_others")
            for l in range(DEPTH):
                for src, at, n in ((attn_norm, NG_ATT + l * CH, CH), (ffn_norm, NG_FFN + l * CH, CH),
                                   (sb_out_norm, NG_HEAD + 2 * l * HEADS, HEADS),
                                   (fox_out_norm, NG_HEAD + (2 * l + 1) * HEADS, HEADS)):
                    act.dma_start(rows[at:at + n, :], src[l].rearrange("(c p) -> c p", p=P)).then_inc(small_in, 16)
            act.dma_start(rows[NG_QK:NG_QK + 2, :], fox_q_norm[:, :]).then_inc(small_in, 16)
            act.dma_start(rows[NG_QK + 2:NG_QK + 4, :], fox_k_norm[:, :]).then_inc(small_in, 16)
            for l in range(DEPTH):
                act.dma_start(bf[:, l:l + 1], b_forget[l].rearrange("(n o) -> n o", o=1)).then_inc(small_in, 16)
            act.wait_ge(consts, 1)

            for layer in range(DEPTH):
                L = layer
                U0 = layer_start[layer]
                if layer:
                    act.wait_ge(free[0], att_uses[layer])
                    act.wait_ge(free[1], att_uses[layer])
                norm_guess(2 * L)
                if layer == 0:
                    for l in range(DEPTH):
                        act.dma_start(thin[:, l], w_in[l].rearrange("(c p) n -> p c n", p=P)[:, :, 3 * W + 4 * W:])\
                           .then_inc(thin_in, 16)
                    act.dma_start(thin[:, 2], router_w[0].rearrange("(c p) n -> p c n", p=P)).then_inc(thin_in, 16)
                    for u in range(LEAD):
                        split_hi(u)
                    act.wait_ge(gain_ready, 1)
                for quarter in range(2):
                    input_hi(2 * L, quarter)
                for u in range(ATT_UNITS):
                    split_hi(U0 + u + LEAD)
                    if u in LATE_QUARTERS:
                        input_hi(2 * L, LATE_QUARTERS[u])
                    j, last = u // JOB_UNITS, u % JOB_UNITS == JOB_UNITS - 1
                    if layer == 0 and u == JOB_UNITS - 3:
                        act.wait_ge(thin_in, 16 * (DEPTH + 1))
                        nc.scalar.activation(thin_hi[:], thin, ACT.Copy).then_inc(thin_h, 1)
                    if u == F_AT + 1:
                        act.wait_ge(f_x, L + 1)
                        nc.scalar.activation(fl, fz, ACT.Abs).then_inc(act_own, 1)
                        act.wait_ge(act_own, own.up())
                        nc.scalar.activation(fl, fl, ACT.Exp, scale=-1.0).then_inc(act_own, 1)
                        act.wait_ge(act_own, own.up())
                        nc.scalar.activation(fl, fl, ACT.Ln, bias=1.0).then_inc(f_ln, 1)
                    if j < NJ and last:
                        quad, what, _ = jobs[j]
                        pair = acc[:, j % 2]
                        use = att_uses[layer] + j // 2 + 1
                        if what == "q":
                            act.wait_ge(used, U0 + u + 1)
                            if quad == 3:
                                act.wait_ge(free[(j - 1) % 2], att_uses[layer] + (j - 1) // 2 + 1)
                            if quad < 2:
                                nc.scalar.activation(q_nat, pair, ACT.Copy).then_inc(free[j % 2], 1)
                            else:
                                nc.scalar.activation(q_nat, pair, ACT.Copy).then_inc(q_done, 1)
                        if quad >= 2 and what in "qk":
                            act.wait_ge(used, U0 + u + 1)
                            if what == "k":
                                act.wait_ge(k_done, 4 * L + (quad - 2) * 2 + 1)
                            nc.scalar.activation(eg[:], pair, ACT.Square).then_inc(free[j % 2], 1)
                        if what == "v":
                            act.wait_ge(used, U0 + u + 1)
                            nc.scalar.activation(v_nat, pair, ACT.Copy).then_inc(free[j % 2], 1)
                        if what == "g":
                            act.wait_ge(used, U0 + u + 1)
                            nc.scalar.activation(eg[:], pair, ACT.Exp, scale=-1.0).then_inc(g_exp, 1)
                    if 0 < j <= NJ and u % JOB_UNITS == 0 and jobs[j - 1][0] >= 2 and jobs[j - 1][1] in "qk":
                        n = 4 * L + (jobs[j - 1][0] - 2) * 2 + "qk".index(jobs[j - 1][1])
                        act.wait_ge(sq_sum, n + 1)
                        rsqrt_guess(kr, kss, 8, 1.0 / P, sq_r)
                    for name, q, p in steps.get(u, ()):
                        nq, np_ = 4 * L + q, 8 * L + 2 * q + p
                        fx = q >= 2
                        if name == "qk":
                            act.wait_ge(qkT_ps, nq + 1)
                            nc.scalar.activation(qT[:], X[:, 0:2].rearrange("p a (h n) -> p (a h) n", h=2), ACT.Copy,
                                                 scale=gq[:, L:L + 1] if fx else 1.0).then_inc(qT_ready, 1)
                        elif name == "scores" and not fx:
                            zp = X[:, 0:2, 0:PW]
                            act.wait_ge(z_ps, np_ + 1)
                            nc.scalar.activation(zs, zp, ACT.Copy, scale=SCALE).then_inc(z_scaled, 1)
                            nc.scalar.activation(t1, zp, ACT.Abs, scale=SCALE).then_inc(act_own, 1)
                            act.wait_ge(act_own, own.up())
                            nc.scalar.activation(t1, t1, ACT.Exp, scale=-1.0).then_inc(act_own, 1)
                            act.wait_ge(act_own, own.up())
                            nc.scalar.activation(t1, t1, ACT.Ln, bias=1.0).then_inc(z_ln, 1)
                        elif name == "scores":
                            act.wait_ge(m_ready, 4 * L + 2 * (q - 2) + p + 1)
                            for a in range(2):
                                for s, e, n in ((0, P, 0), (P, PW, 1)):
                                    ins = nc.scalar.activation(sp[:, a, s:e], zs[:, a, s:e], ACT.Exp,
                                                               bias=nm[:, 2 * a + n:2 * a + n + 1],
                                                               accum_out=lsum[:, 2 * n + a:2 * n + a + 1])
                            ins.then_inc(p_ready, 1)
                        elif name == "second" and not fx:
                            act.wait_ge(arg_ready, 4 * L + 2 * q + p + 1)
                            nc.scalar.activation(wT[:], zs, ACT.Exp).then_inc(w_ready, 1)
                        elif name == "second":
                            act.wait_ge(pT_ps, 4 * L + 2 * (q - 2) + p + 1)
                            nc.scalar.activation(wT[:], X[:, 2:4, 0:PW], ACT.Copy).then_inc(w_ready, 1)
                        elif name == "values":
                            act.wait_ge(o_sum, np_ + 1)
                            rsqrt_guess(hr[:, 0:4], hss[:, 0:4], 4, 1.0 / P, o_r)
                        elif name == "turn":
                            act.wait_ge(oT_ps, np_ + 1)
                            for a in range(2):
                                hd = 4 * q + 2 * p + a
                                g = NG_HEAD + 2 * L * HEADS + hd
                                nc.scalar.activation(
                                    o_hi[:, hd, :].rearrange("p (b n) -> p b n", b=2),
                                    X[:, 1].rearrange("p (b a n) -> p a b n", b=2, a=2)[:, a], ACT.Copy,
                                    scale=gain[:, g:g + 1]).then_inc(oT_hi, 1)
                act.wait_ge(free[0], ffn_uses[layer])
                act.wait_ge(free[1], ffn_uses[layer])
                norm_guess(2 * L + 1)
                for quarter in range(2 if L == 0 else 4):
                    input_hi(2 * L + 1, quarter)
                if L == 1:
                    break

                F0, G0, A0, NG = ffn_start[layer], groups_before[layer], ffn_uses[layer], GROUPS[layer]

                def gate_exp(end, i=None):
                    if i is not None:
                        act.wait_ge(free[1], lin(A0 + 1, 3, i))
                    act.wait_ge(used, lin(end, GROUP_UNITS, i))
                    nc.scalar.activation(eg[:], acc[:, 0], ACT.Exp, scale=-1.0).then_inc(g_exp, 1)
                    nc.scalar.activation(silu, acc[:, 0], ACT.Copy).then_inc(free[0], 1)

                def hidden_hi(n, per=0, i=None):
                    act.wait_ge(hT_ps, lin(G0 + n + 1, per, i))
                    nc.scalar.activation(o_hi[:, 0:GC].rearrange("p c n -> p (c n)"),
                                         X[:, 0:2].rearrange("p a n -> p (a n)"), ACT.Copy).then_inc(hT_hi, 1)

                for u in range(UP_UNITS):
                    split_hi(F0 + u + LEAD)
                    if u in LATE_QUARTERS:
                        input_hi(2 * L + 1, LATE_QUARTERS[u])
                gate_exp(F0 + UP_UNITS)
                F1 = F0 + UP_UNITS
                with act.Fori(0, NG - 1) as i:
                    for u in range(GROUP_UNITS):
                        split_hi(F1 + u + LEAD, GROUP_UNITS, i)
                        if u == TURN_AT:
                            hidden_hi(0, 1, i)
                        if u == 2 * UP_UNITS - 1:
                            gate_exp(F1 + u + 1, i)
                F2 = F1 + GROUP_UNITS * (NG - 1)
                for u in range(GROUP_UNITS - UP_UNITS):
                    split_hi(F2 + u + LEAD)
                    if u == UP_UNITS - 1:
                        hidden_hi(NG - 1)
            nc.scalar.activation(ident_r[:], ident[:], ACT.Copy).then_inc(act_own, 1)
            own.up()
            for q in range(4):
                act.wait_ge(n_ready, q + 1)
                nc.scalar.activation(n_hi[:, :, q * COLS:(q + 1) * COLS], nat[:, 2 + q % 2], ACT.Copy)\
                  .then_inc(n_hi_ready, 1)
            act.wait_ge(rt_max, 1)
            nc.scalar.activation(eq, lg, ACT.Exp).then_inc(rt_exp, 1)

            def picked_high(n, per=0, i=None):
                act.wait_ge(picked_ps, lin(n + 1, per, i))
                nc.scalar.activation(x_hi[:, n % 4 * 4:n % 4 * 4 + 4].rearrange("p c n -> p (c n)"),
                                     X[:, 2 - 2 * (n % 2)], ACT.Copy).then_inc(picked_hi, 1)

            for n in range(4):
                picked_high(n)
            act.wait_ge(table_ready, 1)
            passes = act.value_load(table[0:1, TABLE:TABLE + 1], min_val=EXPERTS, max_val=MAX_PASSES)
            with act.Fori(0, passes) as i:
                for u in range(PASS_UNITS):
                    split_hi(M0 + u + LEAD, PASS_UNITS, i)
                    if u == 3:
                        act.wait_ge(put_ps, i + 1)
                        nc.scalar.activation(put[:], X[:, 1, 0:BLOCKS * P], ACT.Copy).then_inc(put_ready, 1)
                    if u < DOWN0 and u % (2 * UP_UNITS) == UP_UNITS - 1:
                        act.wait_ge(used, lin(M0 + u + 1, PASS_UNITS, i))
                        nc.scalar.activation(eg[:, 0], acc[:, 0, 0], ACT.Exp, scale=-1.0).then_inc(g_exp, 1)
                    if u in turn_at:
                        act.wait_ge(hT_ps, lin(GROUPS[0] + turn_at[u] + 1, HALVES, i))
                        nc.scalar.activation(hT_h[:, turn_at[u] * GC:turn_at[u] * GC + GC].rearrange("p c n -> p (c n)"),
                                             X[:, 0], ACT.Copy).then_inc(hT_hi, 1)
                    if u in down_end:
                        c = down_end[u]
                        act.wait_ge(used, lin(M0 + u + 1, PASS_UNITS, i))
                        if c >= 2:
                            act.wait_ge(y_ps, lin(c - 1, NCOL, i))
                        nc.scalar.activation(y_h[:, c % 2], acc[:, 0, c % 2], ACT.Copy).then_inc(y_hi_ready, 1)
                    if u in pick_at:
                        picked_high(4 + pick_at[u], 4, i)
            act.wait_ge(y_added, passes * NCOL)
            for b in range(BLOCKS):
                nc.scalar.activation(nat[:, 0:2].rearrange("p a b n -> p (a b n)"), h[:, b, :], ACT.Square,
                                     accum_out=ss[:, b:b + 1]).then_inc(act_own, 1)
                act.wait_ge(act_own, own.up())
            rsqrt_guess(rr, ss, 2, 1.0 / D, ss_ready)

        @block.vector
        def _(dve):
            own = Own()

            def split_lo(u, per=0, i=None):
                if pools(u):
                    return
                slot = u % SPLIT_SLOTS
                dve.wait_ge(hi_ready, lin(u + 1, per, i))
                nc.vector.tensor_tensor(w_lo[:, slot], raw[:, (u // TILE_UNITS) % RAW_SLOTS, u % TILE_UNITS],
                                        w_hi[:, slot].bitcast(F32), ALU.subtract).then_inc(lo_ready, 1)

            def refine(y, s, x_, t_, scale, guessed, value):
                nc.vector.tensor_scalar(x_, s, scale, EPS, ALU.mult, ALU.add).then_inc(dve_own, 1)
                own.up()
                dve.wait_ge(guessed, value)
                nc.vector.tensor_tensor(t_, y, y, ALU.mult).then_inc(dve_own, 1)
                dve.wait_ge(dve_own, own.up())
                nc.vector.tensor_tensor(t_, t_, x_, ALU.mult).then_inc(dve_own, 1)
                dve.wait_ge(dve_own, own.up())
                nc.vector.tensor_scalar(t_, t_, -0.5, 1.5, ALU.mult, ALU.add).then_inc(dve_own, 1)
                dve.wait_ge(dve_own, own.up())
                nc.vector.tensor_tensor(y, y, t_, ALU.mult).then_inc(dve_own, 1)
                dve.wait_ge(dve_own, own.up())

            def input_lo(n, quarter):
                for k in range(4 * quarter, 4 * quarter + 4):
                    g = (NG_ATT if n % 2 == 0 else NG_FFN) + (n // 2) * CH + k
                    bank = 2 * (quarter % 2) + (k % 4) // 2
                    dve.wait_ge(a_hi_ready, CH * n + k // 2 * 2 + 2)
                    nc.vector.scalar_tensor_tensor(
                        out=a_lo[:, k, :], in0=X[:, bank, (k % 2) * 256:(k % 2) * 256 + 256],
                        scalar=gain[:, g:g + 1], in1=a_hi[:, k, :].bitcast(F32), op0=ALU.mult,
                        op1=ALU.subtract).then_inc(a_ready, 1)

            def norm(n):
                dve.wait_ge(ss_ready, n + 1)
                refine(rr, ss, xx, tt, 1.0 / D, ss_ready, n + 1)

                def rows_quarter(quarter):
                    if quarter >= 2:
                        dve.wait_ge(xnT_ps, 4 * n + quarter - 1)
                    for b in range(BLOCKS):
                        ins = nc.vector.tensor_scalar(xn[:, quarter % 2, b], h[:, b, quarter * COLS:(quarter + 1) * COLS],
                                                      rr[:, b:b + 1], None, ALU.mult)
                    ins.then_inc(xn_ready, 1)

                rows_quarter(0)
                rows_quarter(1)
                if n == 0:
                    for u in range(LEAD):
                        split_lo(u)
                    dve.wait_ge(consts, N_CONSTS)
                    dve.wait_ge(gain_ps, 1)
                    nc.vector.tensor_copy(gain[:, 0:NROWS], X[:, 3, 0:NROWS]).then_inc(gain_ready, 1)
                    dve.wait_ge(gain_ready, 1)
                    nc.vector.tensor_scalar(gq[:], gain[:, NG_QK:NG_QK + 2], SCALE, None, ALU.mult)
                for quarter in range(2):
                    input_lo(n, quarter)
                    rows_quarter(quarter + 2)

            def wide(ap, n):
                return ap.rearrange("p (n o) -> p n o", o=1).broadcast_to([P, n, P])

            def add_to_h(c, s, end):
                dve.wait_ge(used, end)
                nc.vector.tensor_tensor(h[:, :, c * COLS:(c + 1) * COLS], h[:, :, c * COLS:(c + 1) * COLS],
                                        acc[:, s], ALU.add).then_inc(free[s], 1)


            for layer in range(DEPTH):
                L = layer
                U0 = layer_start[layer]
                norm(2 * L)
                for u in range(ATT_UNITS):
                    split_lo(U0 + u + LEAD)
                    if u in LATE_QUARTERS:
                        input_lo(2 * L, LATE_QUARTERS[u])
                    j, last = u // JOB_UNITS, u % JOB_UNITS == JOB_UNITS - 1
                    if layer == 0 and u == JOB_UNITS - 2:
                        dve.wait_ge(thin_h, 1)
                        nc.vector.tensor_tensor(thin_lo[:], thin, thin_hi[:].bitcast(F32), ALU.subtract)\
                          .then_inc(thin_ready, 1)
                    if u == F_AT:
                        dve.wait_ge(small_in, 16 * N_SMALL)
                        dve.wait_ge(f_ps, L + 1)
                        nc.vector.tensor_scalar(fz, X[0:HEADS, 0, 0:BLOCKS * P], bf[:, L:L + 1], None, ALU.add)
                        nc.vector.tensor_scalar(fm, X[0:HEADS, 0, 0:BLOCKS * P], bf[:, L:L + 1], 0.0, ALU.add, ALU.min)\
                          .then_inc(f_x, 1)
                    if u == F_AT + 2:
                        dve.wait_ge(f_ln, L + 1)
                        nc.vector.tensor_tensor_scan(fc, fm, fl, 0.0, ALU.add, ALU.subtract).then_inc(f_log, 1)
                        dve.wait_ge(f_log, L + 1)
                        nc.vector.tensor_scalar(ncT[:], fc, -1.0, None, ALU.mult)
                    if u == F_AT + 5:
                        dve.wait_ge(c_ps, L + 1)
                        nc.vector.tensor_copy(cum, X[:, 1, 0:2 * HEADS].rearrange("p (b n) -> p b n", b=2))\
                          .then_inc(c_ready, 1)
                    if j < NJ and last:
                        quad, what, _ = jobs[j]
                        pair = acc[:, j % 2]
                        use = att_uses[layer] + j // 2 + 1
                        if what == "k":
                            dve.wait_ge(used, U0 + u + 1)
                            if quad < 2:
                                nc.vector.tensor_copy(k_nat, pair).then_inc(free[j % 2], 1)
                            else:
                                nc.vector.tensor_copy(k_nat, pair).then_inc(k_done, 1)
                        if quad >= 2 and what in "qk":
                            dve.wait_ge(free[j % 2], use)
                            nc.vector.reduce_sum(kss, eg[:].rearrange("p b (h n) -> p (b h) n", n=P), AX.X)\
                              .then_inc(sq_sum, 1)
                        if what == "g":
                            dve.wait_ge(g_exp, gexp[L] + quad - 1)
                            nc.vector.tensor_scalar(g_nat, eg[:], 1.0, None, ALU.add).then_inc(free[j % 2], 1)
                    if 0 < j <= NJ and u % JOB_UNITS < BLOCKS and jobs[j - 1][1] == "g":
                        dve.wait_ge(free[(j - 1) % 2], att_uses[layer] + (j - 1) // 2 + 1)
                        gb = g_nat[:, u % JOB_UNITS]
                        nc.vector.reciprocal(gb, gb).then_inc(dve_own, 1)
                        own.up()
                    if 0 < j <= NJ and u % JOB_UNITS == 0 and jobs[j - 1][0] >= 2 and jobs[j - 1][1] in "qk":
                        what = jobs[j - 1][1]
                        n = 4 * L + (jobs[j - 1][0] - 2) * 2 + "qk".index(what)
                        dve.wait_ge(sq_sum, n + 1)
                        refine(kr, kss, hx, ht, 1.0 / P, sq_r, n + 1)
                        v = (q_nat if what == "q" else k_nat).rearrange("p b (h n) -> p (b h) n", n=P)
                        nc.vector.tensor_tensor(v, v, wide(kr, 8), ALU.mult).then_inc(q_done if what == "q" else k_done, 1)
                    for name, q, p in steps.get(u, ()):
                        nq, np_ = 4 * L + q, 8 * L + 2 * q + p
                        fx = q >= 2
                        if name == "qk":
                            kp = X[:, 2:4].rearrange("p a n -> p (a n)")
                            kv = kT[:].rearrange("p h n -> p (h n)")
                            dve.wait_ge(qkT_ps, nq + 1)
                            if fx:
                                nc.vector.tensor_scalar(kv, kp, gain[:, NG_QK + 2 + L:NG_QK + 3 + L], None, ALU.mult)\
                                  .then_inc(kT_ready, 1)
                            else:
                                nc.vector.tensor_copy(kv, kp).then_inc(kT_ready, 1)
                        elif name == "scores" and not fx:
                            dve.wait_ge(z_scaled, 4 * L + 2 * q + p + 1)
                            dve.wait_ge(z_ln, 4 * L + 2 * q + p + 1)
                            nc.vector.scalar_tensor_tensor(out=sp[:], in0=zs, scalar=0.0, in1=t1, op0=ALU.max,
                                                           op1=ALU.add).then_inc(dve_own, 1)
                            dve.wait_ge(dve_own, own.up())
                            for a in range(2):
                                ins = nc.vector.scalar_tensor_tensor(out=sp[:, a], in0=sb_off[:], scalar=1.0,
                                                                     in1=sp[:, a], op0=ALU.add, op1=ALU.mult)
                            ins.then_inc(sp_ready, 1)
                            for a in range(2):
                                ins = nc.vector.scalar_tensor_tensor(out=zs[:, a], in0=sb_off[:], scalar=-NEG,
                                                                     in1=zs[:, a], op0=ALU.mult, op1=ALU.add)
                            ins.then_inc(dve_own, 1)
                            own.up()
                        elif name == "scores":
                            dve.wait_ge(z_ps, np_ + 1)
                            for a in range(2):
                                hd = 4 * (q - 2) + 2 * p + a
                                for s, e, n in ((0, P, 0), (P, PW, 1)):
                                    ins = nc.vector.scalar_tensor_tensor(
                                        out=zs[:, a, s:e], in0=X[:, a, s:e], scalar=cum[:, n, hd:hd + 1],
                                        in1=fx_neg[:, s:e], op0=ALU.add, op1=ALU.add)
                            ins.then_inc(dve_own, 1)
                            dve.wait_ge(dve_own, own.up())
                            for a in range(2):
                                for s, e, n in ((0, P, 0), (P, PW, 1)):
                                    ins = nc.vector.tensor_reduce(nm[:, 2 * a + n:2 * a + n + 1], zs[:, a, s:e],
                                                                  AX.X, ALU.max, negate=True)
                            ins.then_inc(m_ready, 1)
                        elif name == "second" and not fx:
                            dve.wait_ge(rev_ps, 4 * L + 2 * q + p + 1)
                            dve.wait_ge(dve_own, own.n)
                            nc.vector.tensor_tensor(zs, zs, X[:, 2:4, 0:PW], ALU.subtract).then_inc(arg_ready, 1)
                        elif name == "values":
                            po = X[:, 0].rearrange("p (g n) -> p g n", n=P)
                            dve.wait_ge(o_ps, np_ + 1)
                            if fx:
                                dve.wait_ge(p_ready, 4 * L + 2 * (q - 2) + p + 1)
                                nc.vector.reciprocal(rl, lsum).then_inc(dve_own, 1)
                                dve.wait_ge(dve_own, own.up())
                                nc.vector.tensor_tensor(ob[:], po, wide(rl, 4), ALU.mult).then_inc(dve_own, 1)
                            else:
                                nc.vector.tensor_copy(ob[:], po).then_inc(dve_own, 1)
                            dve.wait_ge(dve_own, own.up())
                            sq = scr[:, 2 * PW:2 * PW + 4 * P].rearrange("p (g n) -> p g n", n=P)
                            nc.vector.tensor_tensor(sq, ob[:], ob[:], ALU.mult).then_inc(dve_own, 1)
                            dve.wait_ge(dve_own, own.up())
                            nc.vector.reduce_sum(hss[:, 0:4], sq, AX.X).then_inc(o_sum, 1)
                            dve.wait_ge(o_sum, np_ + 1)
                            refine(hr[:, 0:4], hss[:, 0:4], hx[:, 0:4], ht[:, 0:4], 1.0 / P, o_r, np_ + 1)
                            if fx:
                                nc.vector.tensor_tensor(ob[:], ob[:], wide(hr[:, 0:4], 4), ALU.mult).then_inc(dve_own, 1)
                                dve.wait_ge(dve_own, own.up())
                                gg = g_nat[:, :, 2 * p * P:(2 * p + 2) * P]
                                o2 = ob[:].rearrange("p (b a) n -> p b (a n)", b=2)
                                nc.vector.tensor_tensor(o2, o2, gg, ALU.mult).then_inc(o_normed, 1)
                            else:
                                nc.vector.tensor_tensor(ob[:], ob[:], wide(hr[:, 0:4], 4), ALU.mult).then_inc(o_normed, 1)
                        elif name == "turn":
                            for a in range(2):
                                hd = 4 * q + 2 * p + a
                                g = NG_HEAD + 2 * L * HEADS + hd
                                dve.wait_ge(oT_hi, 2 * np_ + 2)
                                ins = nc.vector.scalar_tensor_tensor(
                                    out=o_lo[:, hd, :].rearrange("p (b n) -> p b n", b=2),
                                    in0=X[:, 1].rearrange("p (b a n) -> p a b n", b=2, a=2)[:, a],
                                    scalar=gain[:, g:g + 1],
                                    in1=o_hi[:, hd, :].rearrange("p (b n) -> p b n", b=2).bitcast(F32),
                                    op0=ALU.mult, op1=ALU.subtract)
                            ins.then_inc(oT_ready, 1)
                    if u >= PROJ_UNITS and out_units[u - PROJ_UNITS][1] == JOB_UNITS - 1:
                        c = out_units[u - PROJ_UNITS][0]
                        add_to_h(c, c % 2, U0 + u + 1)
                norm(2 * L + 1)
                if L == 1:
                    input_lo(3, 2)
                    input_lo(3, 3)
                    break

                F0, G0, A0, NG = ffn_start[layer], groups_before[layer], ffn_uses[layer], GROUPS[layer]
                F1 = F0 + UP_UNITS

                def gate_silu(step, n, per=0, i=None):
                    if step == 0:
                        dve.wait_ge(g_exp, lin(gexp[L] + 2 + n + 1, per, i))
                        nc.vector.tensor_scalar(eg[:], eg[:], 1.0, None, ALU.add).then_inc(dve_own, 1)
                    elif step <= BLOCKS:
                        dve.wait_ge(dve_own, own.now())
                        nc.vector.reciprocal(eg[:, step - 1], eg[:, step - 1]).then_inc(dve_own, 1)
                    else:
                        dve.wait_ge(free[0], lin(A0 + max(3 * n - 1, 1), 3 * per, i))
                        dve.wait_ge(dve_own, own.now())
                        nc.vector.tensor_tensor(silu, silu, eg[:], ALU.mult).then_inc(dve_own, 1)
                    own.up()

                def hidden(n, per=0, i=None):
                    dve.wait_ge(used, lin(F1 + GROUP_UNITS * n + UP_UNITS, GROUP_UNITS * per, i))
                    dve.wait_ge(dve_own, own.now())
                    nc.vector.tensor_tensor(hid, acc[:, 1], silu, ALU.mult).then_inc(free[1], 1)

                def hidden_lo(n, per=0, i=None):
                    dve.wait_ge(hT_hi, lin(G0 + n + 1, per, i))
                    nc.vector.tensor_tensor(o_lo[:, 0:GC].rearrange("p c n -> p (c n)"),
                                            X[:, 0:2].rearrange("p a n -> p (a n)"),
                                            o_hi[:, 0:GC].rearrange("p c n -> p (c n)").bitcast(F32),
                                            ALU.subtract).then_inc(hT_ready, 1)

                for u in range(UP_UNITS):
                    split_lo(F0 + u + LEAD)
                    if u in LATE_QUARTERS:
                        input_lo(2 * L + 1, LATE_QUARTERS[u])
                for step in range(SILU_STEPS):
                    gate_silu(step, 0)
                with dve.Fori(0, NG - 1) as i:
                    own.enter(i, OWN_DVE_GROUP)
                    for u in range(GROUP_UNITS):
                        split_lo(F1 + u + LEAD, GROUP_UNITS, i)
                        if u == UP_UNITS - 1:
                            hidden(0, 1, i)
                        if u == TURN_AT:
                            hidden_lo(0, 1, i)
                        if u in silu_at:
                            gate_silu(silu_at[u], 1, 1, i)
                        if u >= 2 * UP_UNITS and u % DOWN_UNITS == DOWN_UNITS - 1:
                            c = (u - 2 * UP_UNITS) // DOWN_UNITS
                            add_to_h(c, 1 - c % 2, lin(F1 + u + 1, GROUP_UNITS, i))
                    own.leave(NG - 1)
                F2 = F1 + GROUP_UNITS * (NG - 1)
                for u in range(GROUP_UNITS - UP_UNITS):
                    split_lo(F2 + u + LEAD)
                    if u == UP_UNITS - 1:
                        hidden(NG - 1)
                        hidden_lo(NG - 1)
                    if u >= UP_UNITS and u % DOWN_UNITS == DOWN_UNITS - 1:
                        c = (u - UP_UNITS) // DOWN_UNITS
                        add_to_h(c, 1 - c % 2, F2 + u + 1)
            dve.wait_ge(row_in, 16)
            for q in range(4):
                if q >= 2:
                    dve.wait_ge(n_lo_ready, q - 1)
                for b in range(BLOCKS):
                    ins = nc.vector.scalar_tensor_tensor(out=nat[:, 2 + q % 2, b],
                                                         in0=h[:, b, q * COLS:(q + 1) * COLS], scalar=rr[:, b:b + 1],
                                                         in1=gain_row[:, q * COLS:(q + 1) * COLS], op0=ALU.mult,
                                                         op1=ALU.mult)
                ins.then_inc(n_ready, 1)
            dve.wait_ge(rt_ps, 1)
            nc.vector.tensor_copy(rt_logits, acc[0:EXPERTS, 0, 0, 0:BLOCKS * P]).then_inc(rt_copied, 1)
            dve.wait_ge(rtT_ps, 1)
            nc.vector.tensor_copy(gts, acc[:, 0, 1, 0:16].rearrange("p (b n) -> p b n", b=2)).then_inc(dve_own, 1)
            dve.wait_ge(dve_own, own.up())
            for b in range(BLOCKS):
                nc.vector.max(top[:, b], gts[:, b]).then_inc(dve_own, 1)
                own.up()
            dve.wait_ge(dve_own, own.n)
            for b in range(BLOCKS):
                nc.vector.max_index(topi[:, b], top[:, b], gts[:, b])
                ins = nc.vector.tensor_scalar(lg[:, b], top[:, b], top[:, b, 0:1], None, ALU.subtract)
            ins.then_inc(rt_max, 1)
            dve.wait_ge(rt_max, 1)
            nc.vector.tensor_copy(topf[:], topi[:]).then_inc(dve_own, 1)
            dve.wait_ge(dve_own, own.up())
            dve.wait_ge(pool_own, 7)
            for b in range(BLOCKS):
                nc.vector.tensor_scalar(first[:, b], count[:, 0:8], topf[:, b, 0:1], None, ALU.is_equal)
                ins = nc.vector.tensor_scalar(second[:, b], count[:, 0:8], topf[:, b, 1:2], None, ALU.is_equal)
            ins.then_inc(dve_own, 1)
            dve.wait_ge(dve_own, own.up())
            nc.vector.tensor_tensor(both_e, first, second, ALU.add).then_inc(chosen, 1)
            dve.wait_ge(rt_exp, 1)
            nc.vector.tensor_tensor(gt1[:, :, 0:1], eq[:, :, 0:1], eq[:, :, 1:2], ALU.add).then_inc(dve_own, 1)
            dve.wait_ge(dve_own, own.up())
            nc.vector.reciprocal(gt1[:, :, 1:2], gt1[:, :, 0:1]).then_inc(dve_own, 1)
            dve.wait_ge(dve_own, own.up())
            for b in range(BLOCKS):
                ins = nc.vector.tensor_scalar(gt1[:, b, 2:4], eq[:, b, 0:2], gt1[:, b, 1:2], None, ALU.mult)
            ins.then_inc(dve_own, 1)
            own.up()
            dve.wait_ge(ranks_ps, 1)
            nc.vector.memset(off_e, 0.0)
            nc.vector.tensor_scalar(n_pass, X[:, 0, 2 * EXPERTS:3 * EXPERTS], float(P), 1.0, ALU.is_gt, ALU.add)\
              .then_inc(dve_own, 1)
            dve.wait_ge(dve_own, own.up())
            nc.vector.tensor_tensor_scan(last_pass, n_pass, off_e, 0.0, ALU.add, ALU.add).then_inc(dve_own, 1)
            dve.wait_ge(dve_own, own.up())
            nc.vector.tensor_tensor(off_e, last_pass, n_pass, ALU.subtract).then_inc(dve_own, 1)
            dve.wait_ge(dve_own, own.up())
            nc.vector.tensor_scalar(off_e, off_e, float(P), -1.0, ALU.mult, ALU.add).then_inc(dve_own, 1)
            dve.wait_ge(dve_own, own.up())
            for b in range(BLOCKS):
                ins = nc.vector.tensor_tensor(where[:, b], X[:, 0, b * EXPERTS:(b + 1) * EXPERTS], off_e, ALU.add)
            ins.then_inc(dve_own, 1)
            dve.wait_ge(dve_own, own.up())
            nc.vector.tensor_tensor(first, first, where, ALU.mult)
            nc.vector.tensor_tensor(second, second, where, ALU.mult).then_inc(dve_own, 1)
            dve.wait_ge(dve_own, own.up())
            nc.vector.reduce_sum(pos[:, 0:2], first, AX.X)
            nc.vector.reduce_sum(pos[:, 2:4], second, AX.X).then_inc(dve_own, 1)
            own.up()
            nc.vector.tensor_tensor(hits, last_pass.rearrange("p (o e) -> p o e", o=1).broadcast_to([P, TABLE, EXPERTS]),
                                    count[:, 0:TABLE].rearrange("p (t o) -> p t o", o=1)
                                    .broadcast_to([P, TABLE, EXPERTS]), ALU.is_le).then_inc(dve_own, 1)
            dve.wait_ge(dve_own, own.up())
            nc.vector.reduce_sum(table_f[:], hits, AX.X).then_inc(dve_own, 1)
            dve.wait_ge(dve_own, own.up())
            nc.vector.tensor_scalar(table[:, 0:TABLE], table_f[:], float(EXPERTS - 1), None, ALU.min)
            nc.vector.tensor_copy(table[:, TABLE:TABLE + 1], last_pass[:, EXPERTS - 1:EXPERTS]).then_inc(table_ready, 1)

            def make_pick():
                for b in range(BLOCKS):
                    ins = nc.vector.tensor_scalar(pick_a[:, b], count, pos[:, b:b + 1], None, ALU.is_equal)
                ins.then_inc(dve_own, 1)
                dve.wait_ge(dve_own, own.up())
                for b in range(BLOCKS):
                    nc.vector.scalar_tensor_tensor(out=pick[:, b], in0=count, scalar=pos[:, 2 + b:3 + b],
                                                   in1=pick_a[:, b], op0=ALU.is_equal, op1=ALU.add)
                    nc.vector.tensor_scalar(pick_b[:, b], count, pos[:, b:b + 1], gt1[:, b, 2:3], ALU.is_equal,
                                            ALU.mult)
                    ins = nc.vector.tensor_scalar(pick_g[:, b], count, pos[:, 2 + b:3 + b], gt1[:, b, 3:4],
                                                  ALU.is_equal, ALU.mult)
                ins.then_inc(dve_own, 1)
                dve.wait_ge(dve_own, own.up())
                nc.vector.tensor_scalar(pos, pos, -float(P), None, ALU.add).then_inc(dve_own, 1)
                dve.wait_ge(dve_own, own.up())
                nc.vector.tensor_tensor(pick_g, pick_g, pick_b, ALU.add).then_inc(pick_ready, 1)

            def picked_low(n, per=0, i=None):
                dve.wait_ge(picked_ps, lin(n + 1, per, i))
                nc.vector.tensor_copy(x_lo[:, n % 4 * 4:n % 4 * 4 + 4].rearrange("p c n -> p (c n)"),
                                      X[:, 3 - 2 * (n % 2)]).then_inc(picked_lo, 1)

            dve.wait_ge(dve_own, own.n)
            make_pick()
            for n in range(4):
                picked_low(n)
            dve.wait_ge(table_ready, 1)
            passes = dve.value_load(table[0:1, TABLE:TABLE + 1], min_val=EXPERTS, max_val=MAX_PASSES)
            with dve.Fori(0, passes) as i:
                own.enter(i, OWN_DVE_PASS)
                for u in range(PASS_UNITS):
                    split_lo(M0 + u + LEAD, PASS_UNITS, i)
                    if u == 3:
                        dve.wait_ge(put_ready, i + 1)
                        nc.vector.tensor_copy(slot_gate, X[:, 1, BLOCKS * P:BLOCKS * P + 1]).then_inc(slot_ready, 1)
                    half, step = u // (2 * UP_UNITS), u % (2 * UP_UNITS) - (UP_UNITS - 1)
                    if u < DOWN0 and step == 0:
                        dve.wait_ge(g_exp, lin(gexp[1] + 2 + half + 1, HALVES, i))
                        nc.vector.tensor_scalar(eg[:, 0], eg[:, 0], 1.0, None, ALU.add).then_inc(dve_own, 1)
                        own.up()
                    if u < DOWN0 and step in (1, 3):
                        part = eg[:, 0, step // 2 * (COLS // 2):(step // 2 + 1) * (COLS // 2)]
                        dve.wait_ge(dve_own, own.now())
                        nc.vector.reciprocal(part, part).then_inc(dve_own, 1)
                        own.up()
                    if u < DOWN0 and step == 5:
                        dve.wait_ge(dve_own, own.now())
                        nc.vector.tensor_tensor(silu1, acc[:, 0, 0], eg[:, 0], ALU.mult).then_inc(free[0], 1)
                    if u < DOWN0 and u % (2 * UP_UNITS) == 2 * UP_UNITS - 1:
                        half = u // (2 * UP_UNITS)
                        dve.wait_ge(used, lin(M0 + u + 1, PASS_UNITS, i))
                        dve.wait_ge(free[0], lin(ffn_uses[1] + half + 1, 4, i))
                        dve.wait_ge(slot_ready, i + 1)
                        nc.vector.scalar_tensor_tensor(out=hid1, in0=acc[:, 0, 1], scalar=slot_gate, in1=silu1,
                                                       op0=ALU.mult, op1=ALU.mult).then_inc(free[1], 1)
                    if u in turn_at:
                        dve.wait_ge(hT_hi, lin(GROUPS[0] + turn_at[u] + 1, HALVES, i))
                        at = slice(turn_at[u] * GC, turn_at[u] * GC + GC)
                        nc.vector.tensor_tensor(hT_l[:, at].rearrange("p c n -> p (c n)"), X[:, 0],
                                                hT_h[:, at].rearrange("p c n -> p (c n)").bitcast(F32),
                                                ALU.subtract).then_inc(hT_ready, 1)
                    if u == DOWN0:
                        make_pick()
                    if u in down_end:
                        c = down_end[u]
                        dve.wait_ge(y_hi_ready, lin(c + 1, NCOL, i))
                        nc.vector.tensor_tensor(y_l[:, c % 2], acc[:, 0, c % 2], y_h[:, c % 2].bitcast(F32),
                                                ALU.subtract).then_inc(free[c % 2], 1)
                    if u in pick_at:
                        picked_low(4 + pick_at[u], 4, i)
                    if u in put_at:
                        c = put_at[u]
                        dve.wait_ge(y_ps, lin(c + 1, NCOL, i))
                        hc = h[:, :, c * COLS:(c + 1) * COLS]
                        nc.vector.tensor_tensor(hc, hc, acc[:, 1], ALU.add).then_inc(y_added, 1)
                own.leave(passes)
            dve.wait_ge(ss_ready, 5)
            refine(rr, ss, xx, tt, 1.0 / D, ss_ready, 5)
            dve.wait_ge(fin_in, 16)
            for b in range(BLOCKS):
                nc.vector.scalar_tensor_tensor(out=h[:, b, :], in0=h[:, b, :], scalar=rr[:, b:b + 1], in1=scr[:, 0:D],
                                               op0=ALU.mult, op1=ALU.mult).then_inc(r_ready, 1)

        @block.tensor
        def _(pe):
            def products(lhs_hi, lhs_lo, k0, s, first, last, u, per=0, i=None):
                slot = u % SPLIT_SLOTS
                low_ready(pe, u, per, i)
                for c in range(UNIT_CHUNKS):
                    for b in range(BLOCKS):
                        hi = lhs_hi[:, k0 + c, b * P:(b + 1) * P]
                        lo = lhs_lo[:, k0 + c, b * P:(b + 1) * P]
                        dst = acc[:, s, b]
                        nc.tensor.matmul(dst, hi, w_hi[:, slot, c], start=first and c == 0, stop=False)
                        nc.tensor.matmul(dst, hi, w_lo[:, slot, c], start=False, stop=False)
                        ins = nc.tensor.matmul(dst, lo, w_hi[:, slot, c], start=False,
                                               stop=last and c == UNIT_CHUNKS - 1)
                return ins

            def turn_input(n, quarter):
                pe.wait_ge(xn_ready, 4 * n + quarter + 1)
                if quarter >= 2:
                    pe.wait_ge(a_ready, CH * n + 4 * (quarter - 1))
                for k in range(4):
                    for b in range(BLOCKS):
                        bank = 2 * (quarter % 2) + k // 2
                        at = (k % 2) * 256 + b * P
                        ins = nc.tensor.transpose(X[:, bank, at:at + P], xn[:, quarter % 2, b, k * P:(k + 1) * P], ident[:])
                ins.then_inc(xnT_ps, 1)

            def thin_products(n, dst, chunks):
                for k in chunks:
                    for w, a in ((thin_hi, a_hi), (thin_lo, a_hi), (thin_hi, a_lo)):
                        ins = nc.tensor.matmul(dst, w[:, n, k], a[:, k], start=k == 0 and w is thin_hi and a is a_hi,
                                               stop=k == CH - 1 and a is a_lo)
                return ins

            pe.wait_ge(consts, N_CONSTS)
            pe.wait_ge(small_in, 16 * N_SMALL)
            nc.tensor.transpose(X[:, 3, 0:NROWS], rows[0:NROWS, :], ident[0:NROWS, 0:NROWS]).then_inc(gain_ps, 1)

            for layer in range(DEPTH):
                L = layer
                U0 = layer_start[layer]
                turn_input(2 * L, 0)
                if layer == 0:
                    pe.wait_ge(gain_ready, 1)
                turn_input(2 * L, 1)
                for u in range(ATT_UNITS):
                    if u < PROJ_UNITS:
                        j, ju = u // JOB_UNITS, u % JOB_UNITS
                        s, use = j % 2, att_uses[layer] + j // 2
                        if ju == 0 and use > 0:
                            pe.wait_ge(free[s], use)
                        if j == 0:
                            if ju in (2, 4):
                                turn_input(2 * L, ju // 2 + 1)
                            pe.wait_ge(a_ready, CH * 2 * L + UNIT_CHUNKS * (ju + 1))
                        first, last, lhs, k0 = ju == 0, ju == JOB_UNITS - 1, (a_hi, a_lo), UNIT_CHUNKS * ju
                    else:
                        c, ju = out_units[u - PROJ_UNITS]
                        s, use = c % 2, att_uses[layer] + NJ // 2 + c // 2
                        if ju == 0:
                            pe.wait_ge(free[s], use)
                        if c == 0:
                            pe.wait_ge(oT_ready, 8 * L + ju + 1)
                        first, last, lhs, k0 = ju == 0, ju == JOB_UNITS - 1, (o_hi, o_lo), UNIT_CHUNKS * ju
                    ins = products(*lhs, k0, s, first, last, U0 + u)
                    ins.then_inc(used, 1)
                    if JOB_UNITS <= u < F_AT:
                        if u == JOB_UNITS:
                            pe.wait_ge(thin_ready, 1)
                        k = UNIT_CHUNKS * (u - JOB_UNITS)
                        ins = thin_products(L, X[0:HEADS, 0, 0:BLOCKS * P], range(k, k + UNIT_CHUNKS))
                        if u == F_AT - 1:
                            ins.then_inc(f_ps, 1)
                    if u == F_AT + 4:
                        pe.wait_ge(f_log, L + 1)
                        for b in range(BLOCKS):
                            ins = nc.tensor.transpose(X[:, 1, b * HEADS:(b + 1) * HEADS], fc[:, b * P:(b + 1) * P],
                                                      ident[0:HEADS, 0:HEADS])
                        ins.then_inc(c_ps, 1)
                    for name, q, p in steps.get(u, ()):
                        nq, np_ = 4 * L + q, 8 * L + 2 * q + p
                        fx = q >= 2
                        if name == "qk":
                            if fx:
                                pe.wait_ge(q_done, 4 * L + 2 * (q - 2) + 2)
                                pe.wait_ge(k_done, 4 * L + 2 * (q - 2) + 2)
                            else:
                                jq = 3 * q
                                pe.wait_ge(free[jq % 2], att_uses[layer] + jq // 2 + 1)
                                pe.wait_ge(free[(jq + 1) % 2], att_uses[layer] + (jq + 1) // 2 + 1)
                            if q == 0:
                                pe.wait_ge(c_ready, L + 1)
                            else:
                                pe.wait_ge(oT_ready, np_)
                            for n, v in enumerate((q_nat, k_nat)):
                                for hd in range(QUAD):
                                    for b in range(BLOCKS):
                                        at = (hd % 2) * 256 + b * P
                                        ins = nc.tensor.transpose(X[:, 2 * n + hd // 2, at:at + P],
                                                                  v[:, b, hd * P:(hd + 1) * P], ident[:])
                            ins.then_inc(qkT_ps, 1)
                        elif name == "scores":
                            pe.wait_ge(qT_ready, nq + 1)
                            pe.wait_ge(kT_ready, nq + 1)
                            if p:
                                pe.wait_ge(oT_ready, np_)
                            if fx:
                                pe.wait_ge(c_ready, L + 1)
                            for a in range(2):
                                hd = 2 * p + a
                                qh, kh = qT[:, hd], kT[:, hd]
                                if fx:
                                    hot = onehot[:, 4 * (q - 2) + hd, :]
                                    nc.tensor.matmul(X[:, a, 0:P], qh[:, 0:P], kh[:, 0:P], start=True, stop=False)
                                    nc.tensor.matmul(X[:, a, 0:P], hot, ncT[:, 0:P], start=False, stop=True)
                                    nc.tensor.matmul(X[:, a, P:PW], qh[:, P:2 * P], kh, start=True, stop=False)
                                    ins = nc.tensor.matmul(X[:, a, P:PW], hot, ncT[:], start=False, stop=True)
                                else:
                                    nc.tensor.matmul(X[:, a, 0:2 * P], kh[:, 0:P], qh, start=True, stop=True)
                                    ins = nc.tensor.matmul(X[:, a, 2 * P:PW], kh[:, P:2 * P], qh[:, P:2 * P],
                                                           start=True, stop=True)
                            ins.then_inc(z_ps, 1)
                        elif name == "second" and not fx:
                            pe.wait_ge(sp_ready, 4 * L + 2 * q + p + 1)
                            for a in range(2):
                                nc.tensor.matmul(X[:, 2 + a, 0:PW], tri_ge[:], sp[:, a], start=True, stop=False)
                                ins = nc.tensor.matmul(X[:, 2 + a, P:2 * P], ones[:], sp[:, a, 2 * P:PW],
                                                       start=False, stop=True)
                            ins.then_inc(rev_ps, 1)
                        elif name == "second":
                            pe.wait_ge(p_ready, 4 * L + 2 * (q - 2) + p + 1)
                            for a in range(2):
                                for n in range(3):
                                    ins = nc.tensor.transpose(X[:, 2 + a, n * P:(n + 1) * P],
                                                              sp[:, a, n * P:(n + 1) * P], ident[:])
                            ins.then_inc(pT_ps, 1)
                        elif name == "values":
                            pe.wait_ge(w_ready, np_ + 1)
                            jv = max(j for j in range(NJ) if jobs[j][0] == q and jobs[j][1] == "v")
                            pe.wait_ge(free[jv % 2], att_uses[layer] + jv // 2 + 1)
                            for a in range(2):
                                v = v_nat[:, :, (2 * p + a) * P:(2 * p + a + 1) * P]
                                lo, hi_ = a * P, (2 + a) * P
                                nc.tensor.matmul(X[:, 0, lo:lo + P], wT[:, a, 0:P], v[:, 0], start=True, stop=True)
                                nc.tensor.matmul(X[:, 0, hi_:hi_ + P], wT[:, a, P:2 * P], v[:, 0], start=True, stop=False)
                                ins = nc.tensor.matmul(X[:, 0, hi_:hi_ + P], wT[:, a, 2 * P:PW], v[:, 1], start=False,
                                                       stop=True)
                            ins.then_inc(o_ps, 1)
                        elif name == "turn":
                            pe.wait_ge(o_normed, np_ + 1)
                            for n in range(4):
                                ins = nc.tensor.transpose(X[:, 1, n * P:(n + 1) * P], ob[:, n], ident[:])
                            ins.then_inc(oT_ps, 1)

                F0, G0, A0, NG = ffn_start[layer], groups_before[layer], ffn_uses[layer], GROUPS[layer]
                turn_input(2 * L + 1, 0)
                turn_input(2 * L + 1, 1)
                if L == 1:
                    break

                def input_job(s, use, u0, uses_per=0, per=0, i=None, after=None, fresh=None):
                    pe.wait_ge(free[s], lin(use, uses_per, i))
                    for u in range(JOB_UNITS):
                        if fresh is not None:
                            if u in (2, 4):
                                turn_input(fresh, u // 2 + 1)
                            pe.wait_ge(a_ready, CH * fresh + UNIT_CHUNKS * (u + 1))
                        ins = products(a_hi, a_lo, UNIT_CHUNKS * u, s, u == 0, u == JOB_UNITS - 1, u0 + u, per, i)
                        ins.then_inc(used, 1)
                        if after is not None:
                            after(u)

                def turn_hidden(n, per=0, i=None):
                    pe.wait_ge(free[1], lin(A0 + 3 * n + 1, 3 * per, i))
                    if i is None or per:
                        pe.wait_ge(hT_ready, lin(G0 + n, per, i)) if G0 + n > 0 else None
                    for c in range(GC):
                        for b in range(BLOCKS):
                            at = (c % 2) * 256 + b * P
                            ins = nc.tensor.transpose(X[:, c // 2, at:at + P], hid[:, b, c * P:(c + 1) * P], ident[:])
                    ins.then_inc(hT_ps, 1)

                def down_jobs(n, gate_between, u0, per=0, i=None):
                    pe.wait_ge(hT_ready, lin(G0 + n + 1, per, i))
                    for c in range(NCOL):
                        s = 1 - c % 2
                        use = A0 + 3 * n + c // 2 + 1 + (1 if s == 0 and gate_between else 0)
                        pe.wait_ge(free[s], lin(use, 3 * per, i))
                        for u in range(DOWN_UNITS):
                            ins = products(o_hi, o_lo, UNIT_CHUNKS * u, s, u == 0, u == DOWN_UNITS - 1,
                                           u0 + DOWN_UNITS * c + u, GROUP_UNITS * per, i)
                            ins.then_inc(used, 1)

                input_job(0, A0, F0, fresh=2 * L + 1)
                F1 = F0 + UP_UNITS
                with pe.Fori(0, NG - 1) as i:
                    input_job(1, A0, F1, 3, GROUP_UNITS, i)

                    def then(u):
                        if u == TURN_AT - UP_UNITS:
                            turn_hidden(0, 1, i)
                    input_job(0, A0 + 1, F1 + UP_UNITS, 3, GROUP_UNITS, i, after=then)
                    down_jobs(0, True, F1 + 2 * UP_UNITS, 1, i)
                F2 = F1 + GROUP_UNITS * (NG - 1)
                input_job(1, A0 + 3 * (NG - 1), F2)
                turn_hidden(NG - 1)
                down_jobs(NG - 1, False, F2 + UP_UNITS)

            logits = acc[0:EXPERTS, 0, 0, 0:BLOCKS * P]
            for quarter in range(4):
                if quarter < 2:
                    turn_input(3, quarter + 2)
                pe.wait_ge(a_ready, CH * 3 + 4 * (quarter + 1))
                ins = thin_products(2, logits, range(4 * quarter, 4 * quarter + 4))
            ins.then_inc(rt_ps, 1)
            pe.wait_ge(rt_copied, 1)
            for b in range(BLOCKS):
                ins = nc.tensor.transpose(acc[:, 0, 1, b * EXPERTS:(b + 1) * EXPERTS], rt_logits[:, b * P:(b + 1) * P],
                                          ident[0:EXPERTS, 0:EXPERTS])
            ins.then_inc(rtT_ps, 1)
            pe.wait_ge(chosen, 1)
            nc.tensor.matmul(X[:, 0, 0:EXPERTS], tri_le[:], both_e[:, 0], start=True, stop=True)
            nc.tensor.matmul(X[:, 0, EXPERTS:2 * EXPERTS], ones[:], both_e[:, 0], start=True, stop=False)
            nc.tensor.matmul(X[:, 0, EXPERTS:2 * EXPERTS], tri_le[:], both_e[:, 1], start=False, stop=True)
            nc.tensor.matmul(X[:, 0, 2 * EXPERTS:3 * EXPERTS], ones[:], both_e[:, 0], start=True, stop=False)
            nc.tensor.matmul(X[:, 0, 2 * EXPERTS:3 * EXPERTS], ones[:], both_e[:, 1], start=False, stop=True)\
              .then_inc(ranks_ps, 1)

            def pick_quarter(n, per=0, i=None):
                pe.wait_ge(pick_ready, lin(n // 4 + 1, per // 4, i))
                if n >= 2:
                    pe.wait_ge(picked_hi, lin(n - 1, per, i))
                    pe.wait_ge(picked_lo, lin(n - 1, per, i))
                for part, src in enumerate((n_hi, n_lo)):
                    for c in range(4):
                        k = n % 4 * 4 + c
                        for b in range(BLOCKS):
                            ins = nc.tensor.matmul(X[:, 2 - 2 * (n % 2) + part, c * P:(c + 1) * P],
                                                   src[:, b, k * P:(k + 1) * P], pick[:, b],
                                                   start=b == 0, stop=b == BLOCKS - 1)
                ins.then_inc(picked_ps, 1)

            def pass_products(lhs_hi, lhs_lo, k0, s, first, last, u, i):
                slot = u % SPLIT_SLOTS
                low_ready(pe, M0 + u, PASS_UNITS, i)
                for c in range(UNIT_CHUNKS):
                    hi, lo, dst = lhs_hi[:, k0 + c], lhs_lo[:, k0 + c], acc[:, 0, s]
                    nc.tensor.matmul(dst, hi, w_hi[:, slot, c], start=first and c == 0, stop=False)
                    nc.tensor.matmul(dst, hi, w_lo[:, slot, c], start=False, stop=False)
                    ins = nc.tensor.matmul(dst, lo, w_hi[:, slot, c], start=False, stop=last and c == UNIT_CHUNKS - 1)
                ins.then_inc(used, 1)

            pe.wait_ge(n_lo_ready, 4)
            for n in range(4):
                pick_quarter(n)
            pe.wait_ge(table_ready, 1)
            passes = pe.value_load(table[0:1, TABLE:TABLE + 1], min_val=EXPERTS, max_val=MAX_PASSES)
            with pe.Fori(0, passes) as i:
                for u in range(PASS_UNITS):
                    if u < DOWN0:
                        job, ju = u // UP_UNITS, u % UP_UNITS
                        s = job % 2
                        if ju == 0:
                            pe.wait_ge(free[s], lin(ffn_uses[1] + job // 2, 4, i))
                        if job == 0 and ju % 2 == 0:
                            pe.wait_ge(picked_hi, lin(ju // 2 + 1, 4, i))
                            pe.wait_ge(picked_lo, lin(ju // 2 + 1, 4, i))
                        pass_products(x_hi, x_lo, UNIT_CHUNKS * ju, s, ju == 0, ju == UP_UNITS - 1, u, i)
                    else:
                        c, k = down_units[u - DOWN0]
                        s = c % 2
                        if k == 0:
                            pe.wait_ge(free[s], lin(ffn_uses[1] + 2 + c // 2, 4, i))
                        if c == 0:
                            pe.wait_ge(hT_ready, lin(GROUPS[0] + k // DOWN_UNITS + 1, HALVES, i))
                        pass_products(hT_h, hT_l, UNIT_CHUNKS * k, s, k == 0, k == HALVES * DOWN_UNITS - 1, u, i)
                    if u == 3:
                        pe.wait_ge(picked_lo, lin(4, 4, i))
                        for b in range(BLOCKS):
                            nc.tensor.matmul(X[:, 1, b * P:(b + 1) * P], pick[:, b], ident_r[:], start=True, stop=True)
                        for b in range(BLOCKS):
                            ins = nc.tensor.matmul(X[:, 1, BLOCKS * P:BLOCKS * P + 1], pick_g[:, b], ones[:, 0:1],
                                                   start=b == 0, stop=b == BLOCKS - 1)
                        ins.then_inc(put_ps, 1)
                    if u in turn_at:
                        pe.wait_ge(free[1], lin(ffn_uses[1] + turn_at[u] + 1, 4, i))
                        pe.wait_ge(picked_hi, lin(4, 4, i))
                        for c in range(GC):
                            ins = nc.tensor.transpose(X[:, 0, c * P:(c + 1) * P], hid1[:, c * P:(c + 1) * P], ident[:])
                        ins.then_inc(hT_ps, 1)
                    if u in pick_at:
                        pe.wait_ge(slot_ready, i + 1)
                        pe.wait_ge(hT_ready, lin(GROUPS[0] + HALVES, HALVES, i))
                        pick_quarter(4 + pick_at[u], 4, i)
                    if u in put_at:
                        c = put_at[u]
                        pe.wait_ge(free[c % 2], lin(ffn_uses[1] + 3 + c // 2, 4, i))
                        if c:
                            pe.wait_ge(y_added, lin(c, NCOL, i))
                        for b in range(BLOCKS):
                            nc.tensor.matmul(acc[:, 1, b], put[:, b * P:(b + 1) * P], y_h[:, c % 2], start=True, stop=False)
                            ins = nc.tensor.matmul(acc[:, 1, b], put[:, b * P:(b + 1) * P], y_l[:, c % 2], start=False,
                                                   stop=True)
                        ins.then_inc(y_ps, 1)


_INS = ["x", "attn_norm", "w_in", "b_forget", "fox_q_norm", "fox_k_norm", "sb_out_norm", "fox_out_norm", "w_out",
        "ffn_norm", "dense_w_gate", "dense_w_up", "dense_w_down", "router_w", "moe_w_gate", "moe_w_up",
        "moe_w_down", "final_norm"]


def kernel(**inputs):
    import numpy as _np
    import concourse.bacc as _bacc
    from concourse import mybir as _mybir
    from concourse.bass_utils import run_bass_kernel_spmd as _run

    nc = _bacc.Bacc("TRN2", target_bir_lowering=False, num_devices=1)
    arrays, args = {}, []
    for name in _INS:
        a = _np.ascontiguousarray(inputs[name])
        arrays[f"in_{name}"] = a
        args.append(nc.dram_tensor(f"in_{name}", a.shape, _mybir.dt.from_np(a.dtype), kind="ExternalInput").ap())
    shape = arrays["in_x"].shape
    args.append(nc.dram_tensor("out_0", shape, _mybir.dt.float32, kind="ExternalOutput").ap())
    trunk(nc, *args)
    r = _run(nc, [arrays], core_ids=[0])
    return r.results[0]["out_0"]
```

```python
from contextlib import ExitStack

import concourse.bass as bass
from concourse import mybir

F32 = mybir.dt.float32
F32R = mybir.dt.float32r
U32 = mybir.dt.uint32
ALU = mybir.AluOpType
ACT = mybir.ActivationFunctionType
AX = mybir.AxisListType

P = 128
COLS = 512
BLOCKS = 2
UNIT_CHUNKS = 2
TILE_UNITS = 2
RAW_SLOTS = 4
SPLIT_SLOTS = 4
POOL_UNIT = 3
LEAD = 3
QUAD = 4
QUAD_PAIRS = 2
NEG = -1e30
EPS = 1e-6


class Own:

    def __init__(self):
        self.n, self.i, self.per = 0, None, 0

    def up(self):
        self.n += 1
        return self.n if self.i is None else self.i * self.per + self.n

    def now(self):
        return self.n if self.i is None else self.i * self.per + self.n

    def enter(self, i, per):
        self.i, self.per, self.start = i, per, self.n

    def leave(self, trips):
        assert self.n - self.start == self.per, (self.n, self.start, self.per)
        self.n, self.i = self.start + self.per * trips, None


def lin(const, per=0, i=None):
    return const if i is None else i * per + const


def trunk(nc, x, attn_norm, w_in, b_forget, fox_q_norm, fox_k_norm, sb_out_norm, fox_out_norm, w_out,
          ffn_norm, dense_w_gate, dense_w_up, dense_w_down, router_w, moe_w_gate, moe_w_up, moe_w_down,
          final_norm, out):
    D = x.shape[2]
    DEPTH = w_in.shape[0]
    CH = D // P
    HEADS = sb_out_norm.shape[1] // P
    W = sb_out_norm.shape[1]
    EXPERTS = router_w.shape[2]
    F_EXP = moe_w_gate.shape[3]
    SCALE = float(P) ** -0.5
    assert x.shape[1] == BLOCKS * P and DEPTH == 2 and CH == 16 and HEADS == 8 and EXPERTS == 8
    NCOL = D // COLS
    GC = COLS // P

    JOB_UNITS = CH // UNIT_CHUNKS
    jobs = []
    for quad in range(4):
        base = (quad % 2) * COLS + (0 if quad < 2 else 3 * W)
        for n, what in enumerate("qkv" if quad < 2 else "qkvg"):
            jobs.append((quad, what, base + n * W))
    NJ = len(jobs)
    PROJ_UNITS = NJ * JOB_UNITS
    out_units = [(c, u) for c in range(NCOL) for u in range(JOB_UNITS - 2)]
    out_units += [(c, u) for c in range(NCOL) for u in (JOB_UNITS - 2, JOB_UNITS - 1)]
    OUT_FIRST, OUT_LAST = (0, JOB_UNITS - 2), (JOB_UNITS - 3, JOB_UNITS - 1)
    ATT_UNITS = PROJ_UNITS + len(out_units)
    F_AT = 2 * JOB_UNITS
    quad_start = [(1 + max(j for j in range(NJ) if jobs[j][0] == q)) * JOB_UNITS for q in range(4)]
    PAIR_STEPS = {"scores": (2, 11), "second": (5, 14), "values": (6, 17), "turn": (9, 20)}
    steps = {}
    for q in range(4):
        steps.setdefault(quad_start[q], []).append(("qk", q, 0))
        for p in range(QUAD_PAIRS):
            for name, at in PAIR_STEPS.items():
                steps.setdefault(quad_start[q] + at[p], []).append((name, q, p))

    GROUPS = [dense_w_gate.shape[2] // COLS, EXPERTS * F_EXP // COLS]
    UP_UNITS, DOWN_UNITS = JOB_UNITS, GC // UNIT_CHUNKS
    GROUP_UNITS = 2 * UP_UNITS + NCOL * DOWN_UNITS
    TURN_AT = UP_UNITS + 1
    ffn_start = [ATT_UNITS, 2 * ATT_UNITS + GROUPS[0] * GROUP_UNITS]
    layer_start = [0, ATT_UNITS + GROUPS[0] * GROUP_UNITS]
    HALVES = F_EXP // COLS
    M0 = ffn_start[1]
    DOWN0 = 2 * HALVES * UP_UNITS
    down_units = [(c, k) for cs in ((0, 1),) for k0 in (0, 2) for c in cs for k in (k0, k0 + 1)]
    down_units += [(c, k) for c in range(2, NCOL) for k in range(HALVES * DOWN_UNITS)]
    PASS_UNITS = DOWN0 + len(down_units)
    PASS_TILES = PASS_UNITS // TILE_UNITS
    down_end = {DOWN0 + n: c for n, (c, k) in enumerate(down_units) if k == HALVES * DOWN_UNITS - 1}
    put_at = {u + 2 if c < NCOL - 1 else u: c for u, c in down_end.items()}
    pick_at = {DOWN0 + 3: 0, DOWN0 + 6: 1, DOWN0 + 9: 2, PASS_UNITS - 1: 3}
    turn_at = {2 * UP_UNITS + 1: 0, DOWN0 + 1: 1}
    MAX_PASSES = EXPERTS + (2 * BLOCKS * P - EXPERTS) // P
    TABLE = 16
    OWN_DVE_PASS = 9
    assert MAX_PASSES < TABLE and M0 % 8 == 0 and PASS_UNITS % 8 == 0
    groups_before = [0, GROUPS[0]]
    ATT_USES = (NJ + 2 * NCOL) // 2
    att_uses = [0, ATT_USES + 3 * GROUPS[0]]
    ffn_uses = [u + ATT_USES for u in att_uses]
    TURN_AT_END = {-6: 0, -4: 1, -2: 2}
    SPLIT_AT_END = {-5: 0, -3: 1, -1: 2}
    SQUARE_AT_END = {-4: 0, -2: 1}
    SILU_STEPS = 2 + BLOCKS
    OWN_DVE_GROUP = SILU_STEPS
    silu_at = {2 * UP_UNITS - 1: 0, 2 * UP_UNITS: 1, 2 * UP_UNITS + 2: 2, 2 * UP_UNITS + 4: 3}
    gexp = [0, 2 + GROUPS[0]]

    with ExitStack() as ctx:
        def sb(name, shape, dt=F32):
            return ctx.enter_context(nc.sbuf_tensor(name, shape, dt))

        def sem(name):
            return ctx.enter_context(nc.semaphore(name))

        raw = sb("raw", [P, RAW_SLOTS, TILE_UNITS, UNIT_CHUNKS, COLS])
        w_hi = sb("w_hi", [P, SPLIT_SLOTS, UNIT_CHUNKS, COLS], F32R)
        w_lo = sb("w_lo", [P, SPLIT_SLOTS, UNIT_CHUNKS, COLS], F32R)
        h = sb("h", [P, BLOCKS, D])
        a_hi = sb("a_hi", [P, CH, BLOCKS * P], F32R)
        a_lo = sb("a_lo", [P, CH, BLOCKS * P], F32R)
        o_hi = sb("o_hi", [P, CH, BLOCKS * P], F32R)
        o_lo = sb("o_lo", [P, CH, BLOCKS * P], F32R)
        scr = sb("scr", [P, 4 * COLS])
        PW = 3 * P
        zs = scr[:, 0:2 * PW].rearrange("p (a n) -> p a n", a=2)
        t1 = scr[:, 2 * PW:4 * PW].rearrange("p (a n) -> p a n", a=2)
        sp = sb("sp", [P, 2, PW])
        wT = sb("wT", [P, 2, PW])
        nat = sb("nat", [P, 4, BLOCKS, COLS])
        q_nat, k_nat, v_nat, g_nat = (nat[:, n] for n in range(4))
        silu, hid = nat[:, 1], nat[:, 2]
        silu1, hid1 = nat[:, 2, 0], nat[:, 3, 0]
        eg = sb("eg", [P, BLOCKS, COLS])
        qT = sb("qT", [P, QUAD, BLOCKS * P])
        kT = sb("kT", [P, QUAD, BLOCKS * P])
        ob = sb("ob", [P, 4, P])
        ident = sb("ident", [P, P])
        ones = sb("ones", [P, P])
        tri_ge = sb("tri_ge", [P, P])
        tri_le = sb("tri_le", [P, P])
        sb_off = sb("sb_off", [P, PW])
        fx_neg = sb("fx_neg", [P, PW])
        onehot = sb("onehot", [HEADS, HEADS, P])
        thin_hi = sb("thin_hi", [P, 3, CH, HEADS], F32R)
        thin_lo = sb("thin_lo", [P, 3, CH, HEADS], F32R)
        thin = eg[:, 0, 0:3 * P].rearrange("p (t c n) -> p t c n", t=3, c=CH)
        rows = eg[:, 1, 0:P]
        NG_ATT, NG_FFN, NG_HEAD, NG_QK = 0, 2 * CH, 4 * CH, 4 * CH + 4 * HEADS
        NROWS = NG_QK + 4
        gain = sb("gain", [P, P])
        gq = sb("gq", [P, 2])
        bf = sb("bf", [HEADS, DEPTH])
        epsc = sb("epsc", [P, 1])
        sm = sb("sm", [P, 192])
        ss, rr, xx, tt = (sm[:, 2 * n:2 * n + 2] for n in range(4))
        hss, hr, hx, ht = (sm[:, 8 + 8 * n:16 + 8 * n] for n in range(4))
        sums = sm[:, 56:56 + BLOCKS * NCOL].rearrange("p (b c) -> p b c", b=BLOCKS)
        rr8 = sm[:, 64:64 + BLOCKS * HEADS].rearrange("p (b n) -> p b n", b=BLOCKS)
        nrr = sm[:, 184:184 + BLOCKS]
        kss, kr = (sm[:, 40 + 8 * n:48 + 8 * n] for n in range(2))
        fz, fl, fm, fc = (eg[0:HEADS, n // 2, n % 2 * BLOCKS * P:(n % 2 + 1) * BLOCKS * P] for n in range(4))
        rt_logits = eg[0:EXPERTS, 0, 0:BLOCKS * P]
        cum = sm[:, 104:120].rearrange("p (b n) -> p b n", b=2)
        nm = sm[:, 120:124]
        lsum = sm[:, 124:128]
        rl = sm[:, 128:132]
        lg, gts, eq = (sm[:, 136 + 16 * n:152 + 16 * n].rearrange("p (b n) -> p b n", b=2) for n in range(3))
        top, gt1 = (sb(f"top{n}", [P, 2, 8]) for n in range(2))
        topi = sb("topi", [P, 2, 8], U32)
        topf = sb("topf", [P, 2, 8])
        count = sp[:].rearrange("p a n -> p (a n)")[:, 0:P]
        pick_a = wT[:].rearrange("p a n -> p (a n)")[:, 0:2 * P].rearrange("p (b n) -> p b n", b=2)
        pick_b = wT[:].rearrange("p a n -> p (a n)")[:, 2 * P:4 * P].rearrange("p (b n) -> p b n", b=2)
        pick_g = wT[:].rearrange("p a n -> p (a n)")[:, 4 * P:6 * P].rearrange("p (b n) -> p b n", b=2)
        pick = sb("pick", [P, BLOCKS, P], F32R)
        put = sb("put", [P, BLOCKS * P], F32R)
        ident_r = sb("ident_r", [P, P], F32R)
        rt = sb("rt", [P, 96])
        first, second, both_e, where = (rt[:, 16 * n:16 * n + 16].rearrange("p (b e) -> p b e", b=2) for n in range(4))
        n_pass, last_pass, off_e = (rt[:, 64 + 8 * n:72 + 8 * n] for n in range(3))
        pos = rt[:, 88:92]
        slot_gate = rt[:, 92:93]
        hits = ob[:].rearrange("p a n -> p (a n)")[:, 0:TABLE * EXPERTS].rearrange("p (t e) -> p t e", t=TABLE)
        table_f = sb("table_f", [P, TABLE])
        table = sb("table", [P, TABLE + 1], mybir.dt.int32)
        flat = lambda t: t[:].rearrange("p c n -> p (c n)")
        n_hi, n_lo = (flat(t).rearrange("p (b n) -> p b n", b=BLOCKS) for t in (o_hi, o_lo))
        x_hi, x_lo = (flat(t)[:, 0:D].rearrange("p (c n) -> p c n", c=CH) for t in (a_hi, a_lo))
        hT_h, hT_l = (flat(t)[:, D:D + F_EXP].rearrange("p (c n) -> p c n", n=P) for t in (a_hi, a_lo))
        y_h, y_l = (flat(t)[:, D + F_EXP:D + F_EXP + 2 * COLS].rearrange("p (s n) -> p s n", s=2)
                    for t in (a_hi, a_lo))
        gain_row = nat[:, 0:2].rearrange("p a b n -> p (a b n)")
        ncT = sb("ncT", [HEADS, BLOCKS * P])
        acc = ctx.enter_context(nc.psum_tensor("acc", [P, 2, BLOCKS, COLS], F32))
        X = ctx.enter_context(nc.psum_tensor("X", [P, 4, COLS], F32))

        loaded = [sem(f"loaded{s}") for s in range(RAW_SLOTS)]
        hi_ready = sem("hi_ready")
        lo_ready = sem("lo_ready")
        pool_ready = sem("pool_ready")
        used = sem("used")
        free = [sem(f"free{s}") for s in range(2)]
        x_in = [sem(f"x_in{b}") for b in range(BLOCKS)]
        small_in = sem("small_in")
        fin_in = sem("fin_in")
        stored = sem("stored")
        consts = sem("consts")
        gain_ps = sem("gain_ps")
        gain_ready = sem("gain_ready")
        thin_in = sem("thin_in")
        thin_h = sem("thin_h")
        thin_ready = sem("thin_ready")
        sq_cols = sem("sq_cols")
        ss_sum = sem("ss_sum")
        ss_ready = sem("ss_ready")
        r_ready = sem("r_ready")
        rr_ready = sem("rr_ready")
        xnT_ps = sem("xnT_ps")
        a_hi_ready = sem("a_hi_ready")
        a_ready = sem("a_ready")
        f_ps = sem("f_ps")
        f_x = sem("f_x")
        f_ln = sem("f_ln")
        f_log = sem("f_log")
        c_ps = sem("c_ps")
        c_ready = sem("c_ready")
        g_exp = sem("g_exp")
        sq_sum = sem("sq_sum")
        sq_r = sem("sq_r")
        q_done = sem("q_done")
        k_done = sem("k_done")
        qkT_ps = sem("qkT_ps")
        qT_ready = sem("qT_ready")
        kT_ready = sem("kT_ready")
        z_ps = sem("z_ps")
        z_scaled = sem("z_scaled")
        z_ln = sem("z_ln")
        sp_ready = sem("sp_ready")
        rev_ps = sem("rev_ps")
        arg_ready = sem("arg_ready")
        m_ready = sem("m_ready")
        p_ready = sem("p_ready")
        pT_ps = sem("pT_ps")
        w_ready = sem("w_ready")
        o_ps = sem("o_ps")
        o_sum = sem("o_sum")
        o_r = sem("o_r")
        o_normed = sem("o_normed")
        oT_ps = sem("oT_ps")
        oT_hi = sem("oT_hi")
        oT_ready = sem("oT_ready")
        rt_ps = sem("rt_ps")
        rt_copied = sem("rt_copied")
        rtT_ps = sem("rtT_ps")
        rt_max = sem("rt_max")
        rt_exp = sem("rt_exp")
        chosen = sem("chosen")
        ranks_ps = sem("ranks_ps")
        table_ready = sem("table_ready")
        row_in = sem("row_in")
        n_ready = sem("n_ready")
        n_hi_ready = sem("n_hi_ready")
        n_lo_ready = sem("n_lo_ready")
        pick_ready = sem("pick_ready")
        gates_ready = sem("gates_ready")
        picked_ps = sem("picked_ps")
        picked_hi = sem("picked_hi")
        picked_lo = sem("picked_lo")
        put_ps = sem("put_ps")
        put_ready = sem("put_ready")
        slot_ready = sem("slot_ready")
        y_hi_ready = sem("y_hi_ready")
        y_ps = sem("y_ps")
        y_added = sem("y_added")
        hT_ps = sem("hT_ps")
        hT_hi = sem("hT_hi")
        hT_ready = sem("hT_ready")
        act_own = sem("act_own")
        dve_own = sem("dve_own")
        pool_own = sem("pool_own")

        def pools(u):
            return u % 2 == 1 if u >= M0 else u % 4 == POOL_UNIT

        def low_ready(eng, u, per=0, i=None):
            if u >= M0:
                if pools(u):
                    eng.wait_ge(pool_ready, lin(M0 // 4 + (u - M0) // 2 + 1, per // 2, i))
                else:
                    eng.wait_ge(lo_ready, lin(3 * M0 // 4 + (u - M0) // 2 + 1, per // 2, i))
            elif pools(u):
                eng.wait_ge(pool_ready, lin(u // 4 + 1, per // 4, i))
            else:
                eng.wait_ge(lo_ready, lin(3 * (u // 4) + u % 4 + 1, 3 * per // 4, i))

        def head_gain(layer, head):
            return NG_HEAD + (head // HEADS * DEPTH + layer) * HEADS + head % HEADS

        def h_ready(eng, n, c):
            if n == 0:
                for b in range(BLOCKS):
                    eng.wait_ge(x_in[b], 16)
            elif n == 2:
                eng.wait_ge(free[1 - c % 2], att_uses[1] - 1 + c // 2)
            else:
                eng.wait_ge(free[c % 2], ffn_uses[n // 2] - 1 + c // 2)

        block = ctx.enter_context(nc.Block())
        N_SMALL = 4 + 2 + DEPTH

        @block.sync
        def _(sp_):
            def load(tile, src, per=0, i=None):
                slot = tile % RAW_SLOTS
                if i is not None or tile >= RAW_SLOTS:
                    u = TILE_UNITS * (tile - RAW_SLOTS) + TILE_UNITS - 1
                    low_ready(sp_, u, TILE_UNITS * per, i)
                sp_.dma_start(raw[:, slot].rearrange("p u c n -> p (u c) n"),
                              src.rearrange("(c p) n -> p c n", p=P)).then_inc(loaded[slot], 16)

            def load_wide(tile, w, col, per=0, i=None):
                for t in range(CH // GC):
                    load(tile + t, w[t * COLS:(t + 1) * COLS, col], per, i)

            for b in range(BLOCKS):
                sp_.dma_start(h[:, b, :], x[0, b * P:(b + 1) * P, :]).then_inc(x_in[b], 16)
            for layer in range(DEPTH):
                tile = layer_start[layer] // TILE_UNITS
                for j, (_, _, col) in enumerate(jobs):
                    if layer == 0 and j == 0:
                        load(0, w_in[0, 0:COLS, col:col + COLS])
                        sp_.wait_ge(small_in, 16 * N_SMALL)
                        for t in range(1, CH // GC):
                            load(t, w_in[0, t * COLS:(t + 1) * COLS, col:col + COLS])
                        continue
                    load_wide(tile + j * CH // GC, w_in[layer], slice(col, col + COLS))
                for n, (c, u) in enumerate(out_units):
                    if n % TILE_UNITS == 0:
                        r = u * UNIT_CHUNKS * P
                        load(tile + (PROJ_UNITS + n) // TILE_UNITS,
                             w_out[layer, r:r + COLS, c * COLS:(c + 1) * COLS])
                tile = ffn_start[layer] // TILE_UNITS
                per_group = GROUP_UNITS // TILE_UNITS
                if layer == 0:
                    wg, wu, wd = dense_w_gate[0], dense_w_up[0], dense_w_down[0]
                    load_wide(tile, wg, slice(0, COLS))
                    tile += CH // GC
                    with sp_.Fori(0, GROUPS[0] - 1) as i:
                        load_wide(tile, wu, bass.ts(i, COLS), per_group, i)
                        load_wide(tile + CH // GC, wg, bass.ds(i * COLS + COLS, COLS), per_group, i)
                        for c in range(NCOL):
                            load(tile + 2 * CH // GC + c, wd[bass.ts(i, COLS), c * COLS:(c + 1) * COLS],
                                 per_group, i)
                    tile += per_group * (GROUPS[0] - 1)
                    last = GROUPS[0] - 1
                    load_wide(tile, wu, slice(last * COLS, (last + 1) * COLS))
                    for c in range(NCOL):
                        load(tile + CH // GC + c, wd[last * COLS:(last + 1) * COLS, c * COLS:(c + 1) * COLS])
                else:
                    wg, wu, wd = moe_w_gate[0], moe_w_up[0], moe_w_down[0]
                    sp_.wait_ge(qkT_ps, 4 * DEPTH)
                    sp_.dma_start(gain_row, ffn_norm[1:2, :].broadcast_to([P, D])).then_inc(row_in, 16)
                    load_wide(tile, wg[0], slice(0, COLS))
                    tile += CH // GC
                    sp_.wait_ge(table_ready, 1)
                    passes = sp_.value_load(table[0:1, TABLE:TABLE + 1], min_val=EXPERTS, max_val=MAX_PASSES)
                    with sp_.Fori(0, passes) as i:
                        e = sp_.value_load(table[0:1, bass.ds(i, 1)], min_val=0, max_val=EXPERTS - 1)
                        t = tile
                        for half in range(HALVES):
                            col = slice(half * COLS, (half + 1) * COLS)
                            if half:
                                load_wide(t, wg[e], col, PASS_TILES, i)
                                t += CH // GC
                            load_wide(t, wu[e], col, PASS_TILES, i)
                            t += CH // GC
                        for n, (c, k) in enumerate(down_units):
                            if n % TILE_UNITS == 0:
                                r = k * UNIT_CHUNKS * P
                                load(t, wd[e][r:r + COLS, c * COLS:(c + 1) * COLS], PASS_TILES, i)
                                t += 1
                        e = sp_.value_load(table[0:1, bass.ds(i + 1, 1)], min_val=0, max_val=EXPERTS - 1)
                        load_wide(t, wg[e], slice(0, COLS), PASS_TILES, i)
                    for slot in range(RAW_SLOTS):
                        sp_.wait_ge(loaded[slot], passes * (16 * PASS_TILES // RAW_SLOTS) + 16 * (tile // RAW_SLOTS))
            sp_.wait_ge(xnT_ps, 4 * 4)
            sp_.dma_start(scr[:, 0:D], final_norm.rearrange("(a n) -> a n", a=1).broadcast_to([P, D]))\
               .then_inc(fin_in, 16)
            for b in range(BLOCKS):
                for n, half in enumerate((slice(0, D // 2), slice(D // 2, D))):
                    sp_.wait_ge(r_ready, 1 + 2 * b + n)
                    sp_.dma_start(out[0, b * P:(b + 1) * P, half], h[:, b, half]).then_inc(stored, 16)
            sp_.wait_ge(stored, 16 * 2 * BLOCKS)

        @block.gpsimd
        def _(pool):
            pool.memset(onehot[:], 0.0).then_inc(pool_own, 1)
            pool.memset(ident[:], 0.0).then_inc(pool_own, 1)
            pool.memset(ones[:], 1.0).then_inc(pool_own, 1)
            pool.memset(sb_off[:], 0.0).then_inc(pool_own, 1)
            pool.memset(fx_neg[:], 0.0).then_inc(pool_own, 1)
            pool.memset(epsc[:], EPS).then_inc(pool_own, 1)
            pool.wait_ge(pool_own, 6)
            pool.affine_select(out=ident[:], in_=ident[:], compare_op=ALU.not_equal, fill=1.0, base=0,
                               pattern=[[-1, P]], channel_multiplier=1).then_inc(consts, 1)
            pool.affine_select(out=tri_ge[:], in_=ones[:], compare_op=ALU.is_ge, fill=0.0, base=0,
                               pattern=[[-1, P]], channel_multiplier=1).then_inc(consts, 1)
            pool.affine_select(out=tri_le[:], in_=ones[:], compare_op=ALU.is_ge, fill=0.0, base=0,
                               pattern=[[1, P]], channel_multiplier=-1).then_inc(consts, 1)
            for at in (0, 2 * P):
                pool.affine_select(out=sb_off[:, at:at + P], in_=sb_off[:, at:at + P], compare_op=ALU.is_gt,
                                   fill=-1.0, base=0, pattern=[[1, P]], channel_multiplier=-1).then_inc(consts, 1)
                pool.affine_select(out=fx_neg[:, at:at + P], in_=fx_neg[:, at:at + P], compare_op=ALU.is_ge,
                                   fill=NEG, base=0, pattern=[[-1, P]], channel_multiplier=1).then_inc(consts, 1)
            pool.affine_select(out=onehot[:], in_=onehot[:], compare_op=ALU.not_equal, fill=1.0, base=0,
                               pattern=[[-1, HEADS], [0, P]], channel_multiplier=1).then_inc(consts, 1)

            def low_parts(u, per, i):
                pool.wait_ge(hi_ready, lin(u + 1, per, i))
                low_ready(pool, u - 1, per, i)
                nc.gpsimd.tensor_tensor(w_lo[:, u % SPLIT_SLOTS],
                                        raw[:, (u // TILE_UNITS) % RAW_SLOTS, u % TILE_UNITS],
                                        w_hi[:, u % SPLIT_SLOTS].bitcast(F32), ALU.subtract).then_inc(pool_ready, 1)

            with pool.Fori(0, M0 // 8) as i:
                low_parts(POOL_UNIT, 8, i)
                low_parts(4 + POOL_UNIT, 8, i)
            low_parts(M0 + 1, 0, None)
            pool.wait_ge(w_ready, 8 * DEPTH)
            nc.gpsimd.iota(count, pattern=[[1, P]], base=0, channel_multiplier=0,
                           allow_small_or_imprecise_dtypes=True).then_inc(pool_own, 1)
            for q in range(4):
                pool.wait_ge(n_hi_ready, q + 1)
                nc.gpsimd.tensor_tensor(n_lo[:, :, q * COLS:(q + 1) * COLS], nat[:, 2 + q % 2],
                                        n_hi[:, :, q * COLS:(q + 1) * COLS].bitcast(F32), ALU.subtract)\
                  .then_inc(n_lo_ready, 1)
            pool.wait_ge(table_ready, 1)
            passes = pool.value_load(table[0:1, TABLE:TABLE + 1], min_val=EXPERTS, max_val=MAX_PASSES)
            with pool.Fori(0, passes * (PASS_UNITS // 8)) as i:
                for n in range(3, 11, 2):
                    low_parts(M0 + n, 8, i)
        N_CONSTS = 8

        @block.scalar
        def _(act):
            own = Own()

            def split_hi(u, per=0, i=None):
                slot = u % SPLIT_SLOTS
                tile = u // TILE_UNITS
                if u % TILE_UNITS == 0:
                    act.wait_ge(loaded[tile % RAW_SLOTS],
                                lin(16 * (tile // RAW_SLOTS + 1), 16 * per // (TILE_UNITS * RAW_SLOTS), i))
                if i is not None or u >= SPLIT_SLOTS:
                    act.wait_ge(used, lin(u - SPLIT_SLOTS + 1, per, i))
                nc.scalar.activation(w_hi[:, slot], raw[:, tile % RAW_SLOTS, u % TILE_UNITS], ACT.Copy)\
                  .then_inc(hi_ready, 1)

            def rsqrt_guess(y, s, n, scale, signal):
                nc.scalar.activation(y, s, ACT.Ln, bias=epsc[:, 0:1], scale=scale).then_inc(act_own, 1)
                act.wait_ge(act_own, own.up())
                nc.scalar.activation(y, y, ACT.Exp, scale=-0.5).then_inc(signal, 1)

            def by_token(dst, src, func, scale, signal):
                for b in range(BLOCKS):
                    ins = nc.scalar.activation(dst[:, b], src[:, b], func, scale=scale[:, b:b + 1])
                ins.then_inc(signal, 1)

            def at_end(n, u):
                if u in SPLIT_AT_END:
                    input_hi(n, SPLIT_AT_END[u])
                if u in SQUARE_AT_END:
                    square_cols(n, SQUARE_AT_END[u])

            def at_start(n, u):
                if u == 0 and n:
                    square_cols(n, 2)
                    square_cols(n, 3)
                if u == 1:
                    input_hi(n, 3)
                if u == 2 and n:
                    norm_guess(n)

            squared = [0]

            def square_cols(n, c):
                h_ready(act, n, c)
                if squared[0]:
                    act.wait_ge(sq_cols, squared[0])
                squared[0] += 1
                for b in range(BLOCKS):
                    ins = nc.scalar.activation(eg[:, b], h[:, b, c * COLS:(c + 1) * COLS], ACT.Square,
                                               accum_out=sums[:, b, c:c + 1])
                ins.then_inc(sq_cols, 1)

            def norm_guess(n):
                act.wait_ge(ss_sum, n)
                rsqrt_guess(rr, ss, 2, 1.0 / D, ss_ready)

            def input_hi(n, quarter):
                act.wait_ge(xnT_ps, 4 * n + quarter + 1)
                for k in range(4 * quarter, 4 * quarter + 4):
                    g = (NG_ATT if n % 2 == 0 else NG_FFN) + (n // 2) * CH + k
                    bank = 2 * (quarter % 2) + (k % 4) // 2
                    nc.scalar.activation(a_hi[:, k, :], X[:, bank, (k % 2) * 256:(k % 2) * 256 + 256], ACT.Copy,
                                         scale=gain[:, g:g + 1]).then_inc(a_hi_ready, 1)

            nc.scalar.preload_act_table_set("natural_log_exp_and_others")
            for src, at, n in ((attn_norm, NG_ATT, CH), (ffn_norm, NG_FFN, CH), (sb_out_norm, NG_HEAD, HEADS),
                               (fox_out_norm, NG_HEAD + DEPTH * HEADS, HEADS)):
                act.dma_start(rows[at:at + DEPTH * n, :], src.rearrange("l (c p) -> (l c) p", p=P)).then_inc(small_in, 16)
            act.dma_start(rows[NG_QK:NG_QK + 2, :], fox_q_norm[:, :]).then_inc(small_in, 16)
            act.dma_start(rows[NG_QK + 2:NG_QK + 4, :], fox_k_norm[:, :]).then_inc(small_in, 16)
            for l in range(DEPTH):
                act.dma_start(bf[:, l:l + 1], b_forget[l].rearrange("(n o) -> n o", o=1)).then_inc(small_in, 16)
            act.wait_ge(consts, 1)

            for layer in range(DEPTH):
                L = layer
                U0 = layer_start[layer]
                if layer == 0:
                    act.wait_ge(gain_ready, 1)
                    for u in range(LEAD):
                        split_hi(u)
                        input_hi(0, u)
                    for l in range(DEPTH):
                        act.dma_start(thin[:, l], w_in[l].rearrange("(c p) n -> p c n", p=P)[:, :, 3 * W + 4 * W:])\
                           .then_inc(thin_in, 16)
                    act.dma_start(thin[:, 2], router_w[0].rearrange("(c p) n -> p c n", p=P)).then_inc(thin_in, 16)
                    for b in range(BLOCKS):
                        nc.scalar.activation(scr[:, 0:D], h[:, b, :], ACT.Square, accum_out=ss[:, b:b + 1])\
                          .then_inc(act_own, 1)
                        act.wait_ge(act_own, own.up())
                    rsqrt_guess(rr, ss, 2, 1.0 / D, ss_ready)
                for u in range(ATT_UNITS):
                    split_hi(U0 + u + LEAD)
                    at_start(2 * L, u)
                    at_end(2 * L + 1, u - ATT_UNITS)
                    j, last = u // JOB_UNITS, u % JOB_UNITS == JOB_UNITS - 1
                    if layer == 0 and u == JOB_UNITS - 3:
                        act.wait_ge(thin_in, 16 * (DEPTH + 1))
                        nc.scalar.activation(thin_hi[:], thin, ACT.Copy).then_inc(thin_h, 1)
                    if u == F_AT + 1:
                        act.wait_ge(f_x, L + 1)
                        nc.scalar.activation(fl, fz, ACT.Abs).then_inc(act_own, 1)
                        act.wait_ge(act_own, own.up())
                        nc.scalar.activation(fl, fl, ACT.Exp, scale=-1.0).then_inc(act_own, 1)
                        act.wait_ge(act_own, own.up())
                        nc.scalar.activation(fl, fl, ACT.Ln, bias=1.0).then_inc(f_ln, 1)
                    if j < NJ and last:
                        quad, what, _ = jobs[j]
                        pair = acc[:, j % 2]
                        use = att_uses[layer] + j // 2 + 1
                        if what == "q":
                            act.wait_ge(used, U0 + u + 1)
                            act.wait_ge(rr_ready, 2 * L + 1)
                            if quad == 3:
                                act.wait_ge(free[(j - 1) % 2], att_uses[layer] + (j - 1) // 2 + 1)
                            by_token(q_nat, pair, ACT.Copy, rr, free[j % 2] if quad < 2 else q_done)
                        if quad >= 2 and what in "qk":
                            act.wait_ge(used, U0 + u + 1)
                            if what == "k":
                                act.wait_ge(k_done, 4 * L + (quad - 2) * 2 + 1)
                            by_token(eg, pair, ACT.Square, rr, free[j % 2])
                        if what == "v":
                            act.wait_ge(used, U0 + u + 1)
                            by_token(v_nat, pair, ACT.Copy, rr, free[j % 2])
                        if what == "g":
                            act.wait_ge(used, U0 + u + 1)
                            by_token(eg, pair, ACT.Exp, nrr, g_exp)
                    if 0 < j <= NJ and u % JOB_UNITS == 0 and jobs[j - 1][0] >= 2 and jobs[j - 1][1] in "qk":
                        n = 4 * L + (jobs[j - 1][0] - 2) * 2 + "qk".index(jobs[j - 1][1])
                        act.wait_ge(sq_sum, n + 1)
                        rsqrt_guess(kr, kss, 8, 1.0 / P, sq_r)
                    for name, q, p in steps.get(u, ()):
                        nq, np_ = 4 * L + q, 8 * L + 2 * q + p
                        fx = q >= 2
                        if name == "qk":
                            act.wait_ge(qkT_ps, nq + 1)
                            nc.scalar.activation(qT[:], X[:, 0:2].rearrange("p a (h n) -> p (a h) n", h=2), ACT.Copy,
                                                 scale=gq[:, L:L + 1] if fx else 1.0).then_inc(qT_ready, 1)
                        elif name == "scores" and not fx:
                            zp = X[:, 0:2, 0:PW]
                            act.wait_ge(z_ps, np_ + 1)
                            nc.scalar.activation(zs, zp, ACT.Copy, scale=SCALE).then_inc(z_scaled, 1)
                            nc.scalar.activation(t1, zp, ACT.Abs, scale=SCALE).then_inc(act_own, 1)
                            act.wait_ge(act_own, own.up())
                            nc.scalar.activation(t1, t1, ACT.Exp, scale=-1.0).then_inc(act_own, 1)
                            act.wait_ge(act_own, own.up())
                            nc.scalar.activation(t1, t1, ACT.Ln, bias=1.0).then_inc(z_ln, 1)
                        elif name == "scores":
                            act.wait_ge(m_ready, 4 * L + 2 * (q - 2) + p + 1)
                            for a in range(2):
                                for s, e, n in ((0, P, 0), (P, PW, 1)):
                                    ins = nc.scalar.activation(sp[:, a, s:e], zs[:, a, s:e], ACT.Exp,
                                                               bias=nm[:, 2 * a + n:2 * a + n + 1],
                                                               accum_out=lsum[:, 2 * n + a:2 * n + a + 1])
                            ins.then_inc(p_ready, 1)
                        elif name == "second" and not fx:
                            act.wait_ge(arg_ready, 4 * L + 2 * q + p + 1)
                            nc.scalar.activation(wT[:], zs, ACT.Exp).then_inc(w_ready, 1)
                        elif name == "second":
                            act.wait_ge(pT_ps, 4 * L + 2 * (q - 2) + p + 1)
                            nc.scalar.activation(wT[:], X[:, 2:4, 0:PW], ACT.Copy).then_inc(w_ready, 1)
                        elif name == "values":
                            act.wait_ge(o_sum, np_ + 1)
                            rsqrt_guess(hr[:, 0:4], hss[:, 0:4], 4, 1.0 / P, o_r)
                        elif name == "turn":
                            act.wait_ge(oT_ps, np_ + 1)
                            for a in range(2):
                                hd = 4 * q + 2 * p + a
                                g = head_gain(L, hd)
                                nc.scalar.activation(
                                    o_hi[:, hd, :].rearrange("p (b n) -> p b n", b=2),
                                    X[:, 1].rearrange("p (b a n) -> p a b n", b=2, a=2)[:, a], ACT.Copy,
                                    scale=gain[:, g:g + 1]).then_inc(oT_hi, 1)
                if L == 1:
                    break

                F0, G0, A0, NG = ffn_start[layer], groups_before[layer], ffn_uses[layer], GROUPS[layer]

                def gate_exp(end, i=None):
                    if i is not None:
                        act.wait_ge(free[1], lin(A0 + 1, 3, i))
                    act.wait_ge(used, lin(end, GROUP_UNITS, i))
                    by_token(eg, acc[:, 0], ACT.Exp, nrr, g_exp)
                    by_token(silu, acc[:, 0], ACT.Copy, rr, free[0])

                def hidden_hi(n, per=0, i=None):
                    act.wait_ge(hT_ps, lin(G0 + n + 1, per, i))
                    nc.scalar.activation(o_hi[:, 0:GC].rearrange("p c n -> p (c n)"),
                                         X[:, 0:2].rearrange("p a n -> p (a n)"), ACT.Copy).then_inc(hT_hi, 1)

                for u in range(UP_UNITS):
                    split_hi(F0 + u + LEAD)
                    at_start(2 * L + 1, u)
                act.wait_ge(rr_ready, 2 * L + 2)
                gate_exp(F0 + UP_UNITS)
                F1 = F0 + UP_UNITS
                with act.Fori(0, NG - 1) as i:
                    for u in range(GROUP_UNITS):
                        split_hi(F1 + u + LEAD, GROUP_UNITS, i)
                        if u == TURN_AT:
                            hidden_hi(0, 1, i)
                        if u == 2 * UP_UNITS - 1:
                            gate_exp(F1 + u + 1, i)
                F2 = F1 + GROUP_UNITS * (NG - 1)
                for u in range(GROUP_UNITS - UP_UNITS):
                    split_hi(F2 + u + LEAD)
                    if u == UP_UNITS - 1:
                        hidden_hi(NG - 1)
                    at_end(2, u - (GROUP_UNITS - UP_UNITS))
            nc.scalar.activation(ident_r[:], ident[:], ACT.Copy).then_inc(act_own, 1)
            own.up()
            at_start(3, 0)
            norm_guess(3)
            input_hi(3, 3)
            for q in range(4):
                act.wait_ge(n_ready, q + 1)
                nc.scalar.activation(n_hi[:, :, q * COLS:(q + 1) * COLS], nat[:, 2 + q % 2], ACT.Copy)\
                  .then_inc(n_hi_ready, 1)
            act.wait_ge(rt_max, 1)
            nc.scalar.activation(eq, lg, ACT.Exp).then_inc(rt_exp, 1)

            def picked_high(n, per=0, i=None):
                act.wait_ge(picked_ps, lin(n + 1, per, i))
                nc.scalar.activation(x_hi[:, n % 4 * 4:n % 4 * 4 + 4].rearrange("p c n -> p (c n)"),
                                     X[:, 2 - 2 * (n % 2)], ACT.Copy).then_inc(picked_hi, 1)

            for n in range(4):
                picked_high(n)
            act.wait_ge(table_ready, 1)
            passes = act.value_load(table[0:1, TABLE:TABLE + 1], min_val=EXPERTS, max_val=MAX_PASSES)
            with act.Fori(0, passes) as i:
                for u in range(PASS_UNITS):
                    split_hi(M0 + u + LEAD, PASS_UNITS, i)
                    if u == 3:
                        act.wait_ge(put_ps, i + 1)
                        nc.scalar.activation(put[:], X[:, 1, 0:BLOCKS * P], ACT.Copy).then_inc(put_ready, 1)
                    if u < DOWN0 and u % (2 * UP_UNITS) == UP_UNITS - 1:
                        act.wait_ge(used, lin(M0 + u + 1, PASS_UNITS, i))
                        nc.scalar.activation(eg[:, 0], acc[:, 0, 0], ACT.Exp, scale=-1.0).then_inc(g_exp, 1)
                    if u in turn_at:
                        act.wait_ge(hT_ps, lin(GROUPS[0] + turn_at[u] + 1, HALVES, i))
                        nc.scalar.activation(hT_h[:, turn_at[u] * GC:turn_at[u] * GC + GC].rearrange("p c n -> p (c n)"),
                                             X[:, 0], ACT.Copy).then_inc(hT_hi, 1)
                    if u in down_end:
                        c = down_end[u]
                        act.wait_ge(used, lin(M0 + u + 1, PASS_UNITS, i))
                        if c >= 2:
                            act.wait_ge(y_ps, lin(c - 1, NCOL, i))
                        nc.scalar.activation(y_h[:, c % 2], acc[:, 0, c % 2], ACT.Copy).then_inc(y_hi_ready, 1)
                    if u in pick_at:
                        picked_high(4 + pick_at[u], 4, i)
            act.wait_ge(free[1], passes * 4 + ffn_uses[1])
            for b in range(BLOCKS):
                nc.scalar.activation(nat[:, 2 * b:2 * b + 2].rearrange("p a b n -> p (a b n)")[:, 0:D - COLS],
                                     h[:, b, 0:D - COLS], ACT.Square, accum_out=sums[:, b, 0:1])
            act.wait_ge(y_added, passes * NCOL)
            for b in range(BLOCKS):
                ins = nc.scalar.activation(eg[:, b], h[:, b, D - COLS:D], ACT.Square, accum_out=sums[:, b, 1:2])
            ins.then_inc(sq_cols, 1)
            norm_guess(4)

        @block.vector
        def _(dve):
            own = Own()

            def split_lo(u, per=0, i=None):
                if pools(u):
                    return
                slot = u % SPLIT_SLOTS
                dve.wait_ge(hi_ready, lin(u + 1, per, i))
                nc.vector.tensor_tensor(w_lo[:, slot], raw[:, (u // TILE_UNITS) % RAW_SLOTS, u % TILE_UNITS],
                                        w_hi[:, slot].bitcast(F32), ALU.subtract).then_inc(lo_ready, 1)

            def refine(y, s, x_, t_, scale, guessed, value):
                nc.vector.tensor_scalar(x_, s, scale, EPS, ALU.mult, ALU.add).then_inc(dve_own, 1)
                own.up()
                dve.wait_ge(guessed, value)
                nc.vector.tensor_tensor(t_, y, y, ALU.mult).then_inc(dve_own, 1)
                dve.wait_ge(dve_own, own.up())
                nc.vector.tensor_tensor(t_, t_, x_, ALU.mult).then_inc(dve_own, 1)
                dve.wait_ge(dve_own, own.up())
                nc.vector.tensor_scalar(t_, t_, -0.5, 1.5, ALU.mult, ALU.add).then_inc(dve_own, 1)
                dve.wait_ge(dve_own, own.up())
                nc.vector.tensor_tensor(y, y, t_, ALU.mult).then_inc(dve_own, 1)
                dve.wait_ge(dve_own, own.up())

            def input_lo(n, quarter):
                for k in range(4 * quarter, 4 * quarter + 4):
                    g = (NG_ATT if n % 2 == 0 else NG_FFN) + (n // 2) * CH + k
                    bank = 2 * (quarter % 2) + (k % 4) // 2
                    dve.wait_ge(a_hi_ready, CH * n + k // 2 * 2 + 2)
                    nc.vector.scalar_tensor_tensor(
                        out=a_lo[:, k, :], in0=X[:, bank, (k % 2) * 256:(k % 2) * 256 + 256],
                        scalar=gain[:, g:g + 1], in1=a_hi[:, k, :].bitcast(F32), op0=ALU.mult,
                        op1=ALU.subtract).then_inc(a_ready, 1)

            def at_end(n, u):
                if u in SPLIT_AT_END:
                    input_lo(n, SPLIT_AT_END[u])

            def one_over_rms(n):
                if n:
                    dve.wait_ge(sq_cols, NCOL * n if n < 4 else NCOL * 3 + 1)
                    nc.vector.reduce_sum(ss, sums if n < 4 else sums[:, :, 0:2], AX.X).then_inc(ss_sum, 1)
                    dve.wait_ge(ss_sum, n)
                else:
                    dve.wait_ge(ss_ready, 1)
                refine(rr, ss, xx, tt, 1.0 / D, ss_ready, n + 1)
                for b in range(BLOCKS):
                    nc.vector.tensor_scalar(rr8[:, b], ones[:, 0:HEADS], rr[:, b:b + 1], None, ALU.mult)
                nc.vector.tensor_scalar(nrr, rr, -1.0, None, ALU.mult).then_inc(rr_ready, 1)

            def at_start(n, u):
                if u == 1:
                    input_lo(n, 3)
                if u == 2:
                    one_over_rms(n)

            def wide(ap, n):
                return ap.rearrange("p (n o) -> p n o", o=1).broadcast_to([P, n, P])

            def add_to_h(c, s, end):
                dve.wait_ge(used, end)
                nc.vector.tensor_tensor(h[:, :, c * COLS:(c + 1) * COLS], h[:, :, c * COLS:(c + 1) * COLS],
                                        acc[:, s], ALU.add).then_inc(free[s], 1)


            for layer in range(DEPTH):
                L = layer
                U0 = layer_start[layer]
                if L == 0:
                    dve.wait_ge(consts, N_CONSTS)
                    dve.wait_ge(gain_ps, 1)
                    nc.vector.tensor_copy(gain[:, 0:NROWS], X[:, 3, 0:NROWS]).then_inc(gain_ready, 1)
                    dve.wait_ge(gain_ready, 1)
                    nc.vector.tensor_scalar(gq[:], gain[:, NG_QK:NG_QK + 2], SCALE, None, ALU.mult)
                    for u in range(LEAD):
                        split_lo(u)
                        input_lo(0, u)
                for u in range(ATT_UNITS):
                    split_lo(U0 + u + LEAD)
                    at_start(2 * L, u)
                    at_end(2 * L + 1, u - ATT_UNITS)
                    j, last = u // JOB_UNITS, u % JOB_UNITS == JOB_UNITS - 1
                    if layer == 0 and u == JOB_UNITS - 2:
                        dve.wait_ge(thin_h, 1)
                        nc.vector.tensor_tensor(thin_lo[:], thin, thin_hi[:].bitcast(F32), ALU.subtract)\
                          .then_inc(thin_ready, 1)
                    if u == F_AT:
                        dve.wait_ge(small_in, 16 * N_SMALL)
                        dve.wait_ge(f_ps, L + 1)
                        nc.vector.tensor_copy(fc, X[0:HEADS, 1, 0:BLOCKS * P]).then_inc(dve_own, 1)
                        dve.wait_ge(dve_own, own.up())
                        nc.vector.tensor_tensor(fl, X[0:HEADS, 0, 0:BLOCKS * P], fc, ALU.mult).then_inc(dve_own, 1)
                        dve.wait_ge(dve_own, own.up())
                        nc.vector.tensor_scalar(fz, fl, bf[:, L:L + 1], None, ALU.add)
                        nc.vector.tensor_scalar(fm, fl, bf[:, L:L + 1], 0.0, ALU.add, ALU.min).then_inc(f_x, 1)
                    if u == F_AT + 2:
                        dve.wait_ge(f_ln, L + 1)
                        nc.vector.tensor_tensor_scan(fc, fm, fl, 0.0, ALU.add, ALU.subtract).then_inc(f_log, 1)
                        dve.wait_ge(f_log, L + 1)
                        nc.vector.tensor_scalar(ncT[:], fc, -1.0, None, ALU.mult)
                    if u == F_AT + 5:
                        dve.wait_ge(c_ps, L + 1)
                        nc.vector.tensor_copy(cum, X[:, 1, 0:2 * HEADS].rearrange("p (b n) -> p b n", b=2))\
                          .then_inc(c_ready, 1)
                    if j < NJ and last:
                        quad, what, _ = jobs[j]
                        pair = acc[:, j % 2]
                        use = att_uses[layer] + j // 2 + 1
                        if what == "k":
                            dve.wait_ge(used, U0 + u + 1)
                            for b in range(BLOCKS):
                                ins = nc.vector.tensor_scalar(k_nat[:, b], pair[:, b], rr[:, b:b + 1], None, ALU.mult)
                            ins.then_inc(free[j % 2] if quad < 2 else k_done, 1)
                        if quad >= 2 and what in "qk":
                            dve.wait_ge(free[j % 2], use)
                            nc.vector.reduce_sum(kss, eg[:].rearrange("p b (h n) -> p (b h) n", n=P), AX.X)\
                              .then_inc(sq_sum, 1)
                        if what == "g":
                            dve.wait_ge(g_exp, gexp[L] + quad - 1)
                            nc.vector.tensor_scalar(g_nat, eg[:], 1.0, None, ALU.add).then_inc(free[j % 2], 1)
                    if 0 < j <= NJ and 0 <= u % JOB_UNITS - 2 < BLOCKS and jobs[j - 1][1] == "g":
                        dve.wait_ge(free[(j - 1) % 2], att_uses[layer] + (j - 1) // 2 + 1)
                        gb = g_nat[:, u % JOB_UNITS - 2]
                        nc.vector.reciprocal(gb, gb).then_inc(dve_own, 1)
                        own.up()
                    if 0 < j <= NJ and u % JOB_UNITS == 0 and jobs[j - 1][0] >= 2 and jobs[j - 1][1] in "qk":
                        what = jobs[j - 1][1]
                        n = 4 * L + (jobs[j - 1][0] - 2) * 2 + "qk".index(what)
                        dve.wait_ge(sq_sum, n + 1)
                        refine(kr, kss, hx, ht, 1.0 / P, sq_r, n + 1)
                        v = (q_nat if what == "q" else k_nat).rearrange("p b (h n) -> p (b h) n", n=P)
                        nc.vector.tensor_tensor(v, v, wide(kr, 8), ALU.mult).then_inc(q_done if what == "q" else k_done, 1)
                    for name, q, p in steps.get(u, ()):
                        nq, np_ = 4 * L + q, 8 * L + 2 * q + p
                        fx = q >= 2
                        if name == "qk":
                            kp = X[:, 2:4].rearrange("p a n -> p (a n)")
                            kv = kT[:].rearrange("p h n -> p (h n)")
                            dve.wait_ge(qkT_ps, nq + 1)
                            if fx:
                                nc.vector.tensor_scalar(kv, kp, gain[:, NG_QK + 2 + L:NG_QK + 3 + L], None, ALU.mult)\
                                  .then_inc(kT_ready, 1)
                            else:
                                nc.vector.tensor_copy(kv, kp).then_inc(kT_ready, 1)
                        elif name == "scores" and not fx:
                            dve.wait_ge(z_scaled, 4 * L + 2 * q + p + 1)
                            dve.wait_ge(z_ln, 4 * L + 2 * q + p + 1)
                            nc.vector.scalar_tensor_tensor(out=sp[:], in0=zs, scalar=0.0, in1=t1, op0=ALU.max,
                                                           op1=ALU.add).then_inc(dve_own, 1)
                            dve.wait_ge(dve_own, own.up())
                            for a in range(2):
                                ins = nc.vector.scalar_tensor_tensor(out=sp[:, a], in0=sb_off[:], scalar=1.0,
                                                                     in1=sp[:, a], op0=ALU.add, op1=ALU.mult)
                            ins.then_inc(sp_ready, 1)
                            for a in range(2):
                                ins = nc.vector.scalar_tensor_tensor(out=zs[:, a], in0=sb_off[:], scalar=-NEG,
                                                                     in1=zs[:, a], op0=ALU.mult, op1=ALU.add)
                            ins.then_inc(dve_own, 1)
                            own.up()
                        elif name == "scores":
                            dve.wait_ge(z_ps, np_ + 1)
                            for a in range(2):
                                hd = 4 * (q - 2) + 2 * p + a
                                for s, e, n in ((0, P, 0), (P, PW, 1)):
                                    ins = nc.vector.scalar_tensor_tensor(
                                        out=zs[:, a, s:e], in0=X[:, a, s:e], scalar=cum[:, n, hd:hd + 1],
                                        in1=fx_neg[:, s:e], op0=ALU.add, op1=ALU.add)
                            ins.then_inc(dve_own, 1)
                            dve.wait_ge(dve_own, own.up())
                            for a in range(2):
                                for s, e, n in ((0, P, 0), (P, PW, 1)):
                                    ins = nc.vector.tensor_reduce(nm[:, 2 * a + n:2 * a + n + 1], zs[:, a, s:e],
                                                                  AX.X, ALU.max, negate=True)
                            ins.then_inc(m_ready, 1)
                        elif name == "second" and not fx:
                            dve.wait_ge(rev_ps, 4 * L + 2 * q + p + 1)
                            dve.wait_ge(dve_own, own.n)
                            nc.vector.tensor_tensor(zs, zs, X[:, 2:4, 0:PW], ALU.subtract).then_inc(arg_ready, 1)
                        elif name == "values":
                            po = X[:, 0].rearrange("p (g n) -> p g n", n=P)
                            dve.wait_ge(o_ps, np_ + 1)
                            if fx:
                                dve.wait_ge(p_ready, 4 * L + 2 * (q - 2) + p + 1)
                                nc.vector.reciprocal(rl, lsum).then_inc(dve_own, 1)
                                dve.wait_ge(dve_own, own.up())
                                nc.vector.tensor_tensor(ob[:], po, wide(rl, 4), ALU.mult).then_inc(dve_own, 1)
                            else:
                                nc.vector.tensor_copy(ob[:], po).then_inc(dve_own, 1)
                            dve.wait_ge(dve_own, own.up())
                            sq = scr[:, 2 * PW:2 * PW + 4 * P].rearrange("p (g n) -> p g n", n=P)
                            nc.vector.tensor_tensor(sq, ob[:], ob[:], ALU.mult).then_inc(dve_own, 1)
                            dve.wait_ge(dve_own, own.up())
                            nc.vector.reduce_sum(hss[:, 0:4], sq, AX.X).then_inc(o_sum, 1)
                            dve.wait_ge(o_sum, np_ + 1)
                            refine(hr[:, 0:4], hss[:, 0:4], hx[:, 0:4], ht[:, 0:4], 1.0 / P, o_r, np_ + 1)
                            if fx:
                                nc.vector.tensor_tensor(ob[:], ob[:], wide(hr[:, 0:4], 4), ALU.mult).then_inc(dve_own, 1)
                                dve.wait_ge(dve_own, own.up())
                                gg = g_nat[:, :, 2 * p * P:(2 * p + 2) * P]
                                o2 = ob[:].rearrange("p (b a) n -> p b (a n)", b=2)
                                nc.vector.tensor_tensor(o2, o2, gg, ALU.mult).then_inc(o_normed, 1)
                            else:
                                nc.vector.tensor_tensor(ob[:], ob[:], wide(hr[:, 0:4], 4), ALU.mult).then_inc(o_normed, 1)
                        elif name == "turn":
                            for a in range(2):
                                hd = 4 * q + 2 * p + a
                                g = head_gain(L, hd)
                                dve.wait_ge(oT_hi, 2 * np_ + 2)
                                ins = nc.vector.scalar_tensor_tensor(
                                    out=o_lo[:, hd, :].rearrange("p (b n) -> p b n", b=2),
                                    in0=X[:, 1].rearrange("p (b a n) -> p a b n", b=2, a=2)[:, a],
                                    scalar=gain[:, g:g + 1],
                                    in1=o_hi[:, hd, :].rearrange("p (b n) -> p b n", b=2).bitcast(F32),
                                    op0=ALU.mult, op1=ALU.subtract)
                            ins.then_inc(oT_ready, 1)
                    if u >= PROJ_UNITS and out_units[u - PROJ_UNITS][1] in OUT_LAST:
                        c = out_units[u - PROJ_UNITS][0]
                        add_to_h(c, c % 2, U0 + u + 1)
                if L == 1:
                    break

                F0, G0, A0, NG = ffn_start[layer], groups_before[layer], ffn_uses[layer], GROUPS[layer]
                F1 = F0 + UP_UNITS

                def gate_silu(step, n, per=0, i=None):
                    if step == 0:
                        dve.wait_ge(g_exp, lin(gexp[L] + 2 + n + 1, per, i))
                        nc.vector.tensor_scalar(eg[:], eg[:], 1.0, None, ALU.add).then_inc(dve_own, 1)
                    elif step <= BLOCKS:
                        dve.wait_ge(dve_own, own.now())
                        nc.vector.reciprocal(eg[:, step - 1], eg[:, step - 1]).then_inc(dve_own, 1)
                    else:
                        dve.wait_ge(free[0], lin(A0 + max(3 * n - 1, 1), 3 * per, i))
                        dve.wait_ge(dve_own, own.now())
                        nc.vector.tensor_tensor(silu, silu, eg[:], ALU.mult).then_inc(dve_own, 1)
                    own.up()

                def hidden(n, per=0, i=None):
                    dve.wait_ge(used, lin(F1 + GROUP_UNITS * n + UP_UNITS, GROUP_UNITS * per, i))
                    dve.wait_ge(dve_own, own.now())
                    for b in range(BLOCKS):
                        ins = nc.vector.scalar_tensor_tensor(out=hid[:, b], in0=acc[:, 1, b], scalar=rr[:, b:b + 1],
                                                             in1=silu[:, b], op0=ALU.mult, op1=ALU.mult)
                    ins.then_inc(free[1], 1)

                def hidden_lo(n, per=0, i=None):
                    dve.wait_ge(hT_hi, lin(G0 + n + 1, per, i))
                    nc.vector.tensor_tensor(o_lo[:, 0:GC].rearrange("p c n -> p (c n)"),
                                            X[:, 0:2].rearrange("p a n -> p (a n)"),
                                            o_hi[:, 0:GC].rearrange("p c n -> p (c n)").bitcast(F32),
                                            ALU.subtract).then_inc(hT_ready, 1)

                for u in range(UP_UNITS):
                    split_lo(F0 + u + LEAD)
                    at_start(2 * L + 1, u)
                for step in range(SILU_STEPS):
                    gate_silu(step, 0)
                with dve.Fori(0, NG - 1) as i:
                    own.enter(i, OWN_DVE_GROUP)
                    for u in range(GROUP_UNITS):
                        split_lo(F1 + u + LEAD, GROUP_UNITS, i)
                        if u == UP_UNITS - 1:
                            hidden(0, 1, i)
                        if u == TURN_AT:
                            hidden_lo(0, 1, i)
                        if u in silu_at:
                            gate_silu(silu_at[u], 1, 1, i)
                        if u >= 2 * UP_UNITS and u % DOWN_UNITS == DOWN_UNITS - 1:
                            c = (u - 2 * UP_UNITS) // DOWN_UNITS
                            add_to_h(c, 1 - c % 2, lin(F1 + u + 1, GROUP_UNITS, i))
                    own.leave(NG - 1)
                F2 = F1 + GROUP_UNITS * (NG - 1)
                for u in range(GROUP_UNITS - UP_UNITS):
                    split_lo(F2 + u + LEAD)
                    at_end(2, u - (GROUP_UNITS - UP_UNITS))
                    if u == UP_UNITS - 1:
                        hidden(NG - 1)
                        hidden_lo(NG - 1)
                    if u >= UP_UNITS and u % DOWN_UNITS == DOWN_UNITS - 1:
                        c = (u - UP_UNITS) // DOWN_UNITS
                        add_to_h(c, 1 - c % 2, F2 + u + 1)
            one_over_rms(3)

            def by_tokens(q):
                if q >= 2:
                    dve.wait_ge(n_lo_ready, q - 1)
                for b in range(BLOCKS):
                    ins = nc.vector.scalar_tensor_tensor(out=nat[:, 2 + q % 2, b],
                                                         in0=h[:, b, q * COLS:(q + 1) * COLS], scalar=rr[:, b:b + 1],
                                                         in1=gain_row[:, q * COLS:(q + 1) * COLS], op0=ALU.mult,
                                                         op1=ALU.mult)
                ins.then_inc(n_ready, 1)

            dve.wait_ge(row_in, 16)
            by_tokens(0)
            input_lo(3, 3)
            by_tokens(1)
            dve.wait_ge(rt_ps, 1)
            nc.vector.tensor_copy(rt_logits, acc[0:EXPERTS, 0, 0, 0:BLOCKS * P]).then_inc(rt_copied, 1)
            by_tokens(2)
            dve.wait_ge(rtT_ps, 1)
            for b in range(BLOCKS):
                ins = nc.vector.tensor_scalar(gts[:, b], acc[:, 0, 1, b * EXPERTS:(b + 1) * EXPERTS], rr[:, b:b + 1],
                                              None, ALU.mult)
            ins.then_inc(dve_own, 1)
            dve.wait_ge(dve_own, own.up())
            for b in range(BLOCKS):
                nc.vector.max(top[:, b], gts[:, b]).then_inc(dve_own, 1)
                own.up()
            dve.wait_ge(dve_own, own.n)
            for b in range(BLOCKS):
                nc.vector.max_index(topi[:, b], top[:, b], gts[:, b])
                ins = nc.vector.tensor_scalar(lg[:, b], top[:, b], top[:, b, 0:1], None, ALU.subtract)
            ins.then_inc(rt_max, 1)
            dve.wait_ge(rt_max, 1)
            nc.vector.tensor_copy(topf[:], topi[:]).then_inc(dve_own, 1)
            dve.wait_ge(dve_own, own.up())
            dve.wait_ge(pool_own, 7)
            for b in range(BLOCKS):
                nc.vector.tensor_scalar(first[:, b], count[:, 0:8], topf[:, b, 0:1], None, ALU.is_equal)
                ins = nc.vector.tensor_scalar(second[:, b], count[:, 0:8], topf[:, b, 1:2], None, ALU.is_equal)
            ins.then_inc(dve_own, 1)
            dve.wait_ge(dve_own, own.up())
            nc.vector.tensor_tensor(both_e, first, second, ALU.add).then_inc(chosen, 1)
            by_tokens(3)
            dve.wait_ge(rt_exp, 1)
            nc.vector.tensor_tensor(gt1[:, :, 0:1], eq[:, :, 0:1], eq[:, :, 1:2], ALU.add).then_inc(dve_own, 1)
            dve.wait_ge(dve_own, own.up())
            nc.vector.reciprocal(gt1[:, :, 1:2], gt1[:, :, 0:1]).then_inc(dve_own, 1)
            dve.wait_ge(dve_own, own.up())
            for b in range(BLOCKS):
                ins = nc.vector.tensor_scalar(gt1[:, b, 2:4], eq[:, b, 0:2], gt1[:, b, 1:2], None, ALU.mult)
            ins.then_inc(dve_own, 1)
            own.up()
            dve.wait_ge(ranks_ps, 1)
            nc.vector.memset(off_e, 0.0)
            nc.vector.tensor_scalar(n_pass, X[:, 0, 2 * EXPERTS:3 * EXPERTS], float(P), 1.0, ALU.is_gt, ALU.add)\
              .then_inc(dve_own, 1)
            dve.wait_ge(dve_own, own.up())
            nc.vector.tensor_tensor_scan(last_pass, n_pass, off_e, 0.0, ALU.add, ALU.add).then_inc(dve_own, 1)
            dve.wait_ge(dve_own, own.up())
            nc.vector.tensor_tensor(off_e, last_pass, n_pass, ALU.subtract).then_inc(dve_own, 1)
            dve.wait_ge(dve_own, own.up())
            nc.vector.tensor_scalar(off_e, off_e, float(P), -1.0, ALU.mult, ALU.add).then_inc(dve_own, 1)
            dve.wait_ge(dve_own, own.up())
            for b in range(BLOCKS):
                ins = nc.vector.tensor_tensor(where[:, b], X[:, 0, b * EXPERTS:(b + 1) * EXPERTS], off_e, ALU.add)
            ins.then_inc(dve_own, 1)
            dve.wait_ge(dve_own, own.up())
            nc.vector.tensor_tensor(first, first, where, ALU.mult)
            nc.vector.tensor_tensor(second, second, where, ALU.mult).then_inc(dve_own, 1)
            dve.wait_ge(dve_own, own.up())
            nc.vector.reduce_sum(pos[:, 0:2], first, AX.X)
            nc.vector.reduce_sum(pos[:, 2:4], second, AX.X).then_inc(dve_own, 1)
            own.up()
            def make_pick():
                for b in range(BLOCKS):
                    ins = nc.vector.tensor_scalar(pick_a[:, b], count, pos[:, b:b + 1], None, ALU.is_equal)
                ins.then_inc(dve_own, 1)
                dve.wait_ge(dve_own, own.up())
                for b in range(BLOCKS):
                    ins = nc.vector.scalar_tensor_tensor(out=pick[:, b], in0=count, scalar=pos[:, 2 + b:3 + b],
                                                         in1=pick_a[:, b], op0=ALU.is_equal, op1=ALU.add)
                ins.then_inc(pick_ready, 1)
                for b in range(BLOCKS):
                    nc.vector.tensor_scalar(pick_b[:, b], count, pos[:, b:b + 1], gt1[:, b, 2:3], ALU.is_equal,
                                            ALU.mult)
                    ins = nc.vector.tensor_scalar(pick_g[:, b], count, pos[:, 2 + b:3 + b], gt1[:, b, 3:4],
                                                  ALU.is_equal, ALU.mult)
                ins.then_inc(dve_own, 1)
                dve.wait_ge(dve_own, own.up())
                nc.vector.tensor_scalar(pos, pos, -float(P), None, ALU.add).then_inc(dve_own, 1)
                dve.wait_ge(dve_own, own.up())
                nc.vector.tensor_tensor(pick_g, pick_g, pick_b, ALU.add).then_inc(gates_ready, 1)

            def picked_low(n, per=0, i=None):
                dve.wait_ge(picked_ps, lin(n + 1, per, i))
                nc.vector.tensor_copy(x_lo[:, n % 4 * 4:n % 4 * 4 + 4].rearrange("p c n -> p (c n)"),
                                      X[:, 3 - 2 * (n % 2)]).then_inc(picked_lo, 1)

            dve.wait_ge(dve_own, own.n)
            make_pick()
            nc.vector.tensor_tensor(hits, last_pass.rearrange("p (o e) -> p o e", o=1).broadcast_to([P, TABLE, EXPERTS]),
                                    count[:, 0:TABLE].rearrange("p (t o) -> p t o", o=1)
                                    .broadcast_to([P, TABLE, EXPERTS]), ALU.is_le).then_inc(dve_own, 1)
            dve.wait_ge(dve_own, own.up())
            nc.vector.reduce_sum(table_f[:], hits, AX.X).then_inc(dve_own, 1)
            dve.wait_ge(dve_own, own.up())
            nc.vector.tensor_scalar(table[:, 0:TABLE], table_f[:], float(EXPERTS - 1), None, ALU.min)
            nc.vector.tensor_copy(table[:, TABLE:TABLE + 1], last_pass[:, EXPERTS - 1:EXPERTS]).then_inc(table_ready, 1)
            for n in range(4):
                picked_low(n)
            dve.wait_ge(table_ready, 1)
            passes = dve.value_load(table[0:1, TABLE:TABLE + 1], min_val=EXPERTS, max_val=MAX_PASSES)
            with dve.Fori(0, passes) as i:
                own.enter(i, OWN_DVE_PASS)
                for u in range(PASS_UNITS):
                    split_lo(M0 + u + LEAD, PASS_UNITS, i)
                    if u == 3:
                        dve.wait_ge(put_ready, i + 1)
                        nc.vector.tensor_copy(slot_gate, X[:, 1, BLOCKS * P:BLOCKS * P + 1]).then_inc(slot_ready, 1)
                    half, step = u // (2 * UP_UNITS), u % (2 * UP_UNITS) - (UP_UNITS - 1)
                    if u < DOWN0 and step == 0:
                        dve.wait_ge(g_exp, lin(gexp[1] + 2 + half + 1, HALVES, i))
                        nc.vector.tensor_scalar(eg[:, 0], eg[:, 0], 1.0, None, ALU.add).then_inc(dve_own, 1)
                        own.up()
                    if u < DOWN0 and step in (1, 3):
                        part = eg[:, 0, step // 2 * (COLS // 2):(step // 2 + 1) * (COLS // 2)]
                        dve.wait_ge(dve_own, own.now())
                        nc.vector.reciprocal(part, part).then_inc(dve_own, 1)
                        own.up()
                    if u < DOWN0 and step == 5:
                        dve.wait_ge(dve_own, own.now())
                        nc.vector.tensor_tensor(silu1, acc[:, 0, 0], eg[:, 0], ALU.mult).then_inc(free[0], 1)
                    if u < DOWN0 and u % (2 * UP_UNITS) == 2 * UP_UNITS - 1:
                        half = u // (2 * UP_UNITS)
                        dve.wait_ge(used, lin(M0 + u + 1, PASS_UNITS, i))
                        dve.wait_ge(free[0], lin(ffn_uses[1] + half + 1, 4, i))
                        dve.wait_ge(slot_ready, i + 1)
                        nc.vector.scalar_tensor_tensor(out=hid1, in0=acc[:, 0, 1], scalar=slot_gate, in1=silu1,
                                                       op0=ALU.mult, op1=ALU.mult).then_inc(free[1], 1)
                    if u in turn_at:
                        dve.wait_ge(hT_hi, lin(GROUPS[0] + turn_at[u] + 1, HALVES, i))
                        at = slice(turn_at[u] * GC, turn_at[u] * GC + GC)
                        nc.vector.tensor_tensor(hT_l[:, at].rearrange("p c n -> p (c n)"), X[:, 0],
                                                hT_h[:, at].rearrange("p c n -> p (c n)").bitcast(F32),
                                                ALU.subtract).then_inc(hT_ready, 1)
                    if u == 2 * UP_UNITS + 4:
                        make_pick()
                    if u in down_end:
                        c = down_end[u]
                        dve.wait_ge(y_hi_ready, lin(c + 1, NCOL, i))
                        nc.vector.tensor_tensor(y_l[:, c % 2], acc[:, 0, c % 2], y_h[:, c % 2].bitcast(F32),
                                                ALU.subtract).then_inc(free[c % 2], 1)
                    if u in pick_at:
                        picked_low(4 + pick_at[u], 4, i)
                    if u in put_at:
                        c = put_at[u]
                        dve.wait_ge(y_ps, lin(c + 1, NCOL, i))
                        hc = h[:, :, c * COLS:(c + 1) * COLS]
                        nc.vector.tensor_tensor(hc, hc, acc[:, 1], ALU.add).then_inc(y_added, 1)
                own.leave(passes)
            one_over_rms(4)
            dve.wait_ge(fin_in, 16)
            for b in range(BLOCKS):
                for half in (slice(0, D // 2), slice(D // 2, D)):
                    nc.vector.scalar_tensor_tensor(out=h[:, b, half], in0=h[:, b, half], scalar=rr[:, b:b + 1],
                                                   in1=scr[:, half], op0=ALU.mult, op1=ALU.mult).then_inc(r_ready, 1)

        @block.tensor
        def _(pe):
            def products(lhs_hi, lhs_lo, k0, s, first, last, u, per=0, i=None):
                slot = u % SPLIT_SLOTS
                low_ready(pe, u, per, i)
                for c in range(UNIT_CHUNKS):
                    for b in range(BLOCKS):
                        hi = lhs_hi[:, k0 + c, b * P:(b + 1) * P]
                        lo = lhs_lo[:, k0 + c, b * P:(b + 1) * P]
                        dst = acc[:, s, b]
                        nc.tensor.matmul(dst, hi, w_hi[:, slot, c], start=first and c == 0, stop=False)
                        nc.tensor.matmul(dst, hi, w_lo[:, slot, c], start=False, stop=False)
                        ins = nc.tensor.matmul(dst, lo, w_hi[:, slot, c], start=False,
                                               stop=last and c == UNIT_CHUNKS - 1)
                return ins

            def turn_input(n, quarter):
                h_ready(pe, n, quarter)
                if quarter >= 2:
                    pe.wait_ge(a_ready, CH * n + 4 * (quarter - 1))
                for k in range(4):
                    for b in range(BLOCKS):
                        bank = 2 * (quarter % 2) + k // 2
                        at = (k % 2) * 256 + b * P
                        col = (4 * quarter + k) * P
                        ins = nc.tensor.transpose(X[:, bank, at:at + P], h[:, b, col:col + P], ident[:])
                ins.then_inc(xnT_ps, 1)

            def at_end(n, u):
                if u in TURN_AT_END:
                    turn_input(n, TURN_AT_END[u])

            def thin_products(n, dst, chunks):
                for k in chunks:
                    for w, a in ((thin_hi, a_hi), (thin_lo, a_hi), (thin_hi, a_lo)):
                        ins = nc.tensor.matmul(dst, w[:, n, k], a[:, k], start=k == 0 and w is thin_hi and a is a_hi,
                                               stop=k == CH - 1 and a is a_lo)
                return ins

            pe.wait_ge(consts, N_CONSTS)
            turn_input(0, 0)
            pe.wait_ge(small_in, 16 * N_SMALL)
            nc.tensor.transpose(X[:, 3, 0:NROWS], rows[0:NROWS, :], ident[0:NROWS, 0:NROWS]).then_inc(gain_ps, 1)
            pe.wait_ge(gain_ready, 1)
            turn_input(0, 1)
            turn_input(0, 2)

            for layer in range(DEPTH):
                L = layer
                U0 = layer_start[layer]
                for u in range(ATT_UNITS):
                    if u < PROJ_UNITS:
                        j, ju = u // JOB_UNITS, u % JOB_UNITS
                        s, use = j % 2, att_uses[layer] + j // 2
                        if ju == 0 and use > 0:
                            pe.wait_ge(free[s], use)
                        if j == 0:
                            if ju == 1:
                                turn_input(2 * L, 3)
                            pe.wait_ge(a_ready, CH * 2 * L + UNIT_CHUNKS * (ju + 1))
                        first, last, lhs, k0 = ju == 0, ju == JOB_UNITS - 1, (a_hi, a_lo), UNIT_CHUNKS * ju
                    else:
                        c, ju = out_units[u - PROJ_UNITS]
                        s, use = c % 2, att_uses[layer] + NJ // 2 + c // 2 + NCOL // 2 * (ju >= OUT_FIRST[1])
                        if ju in OUT_FIRST:
                            pe.wait_ge(free[s], use)
                        if c == 0:
                            pe.wait_ge(oT_ready, 8 * L + ju + 1)
                        first, last, lhs, k0 = ju in OUT_FIRST, ju in OUT_LAST, (o_hi, o_lo), UNIT_CHUNKS * ju
                    ins = products(*lhs, k0, s, first, last, U0 + u)
                    ins.then_inc(used, 1)
                    at_end(2 * L + 1, u - ATT_UNITS)
                    if JOB_UNITS <= u < F_AT:
                        if u == JOB_UNITS:
                            pe.wait_ge(thin_ready, 1)
                        k = UNIT_CHUNKS * (u - JOB_UNITS)
                        ins = thin_products(L, X[0:HEADS, 0, 0:BLOCKS * P], range(k, k + UNIT_CHUNKS))
                        if u == F_AT - 1:
                            pe.wait_ge(rr_ready, 2 * L + 1)
                            for b in range(BLOCKS):
                                ins = nc.tensor.matmul(X[0:HEADS, 1, b * P:(b + 1) * P], rr8[:, b], ident[:], start=True,
                                                       stop=True)
                            ins.then_inc(f_ps, 1)
                    if u == F_AT + 4:
                        pe.wait_ge(f_log, L + 1)
                        for b in range(BLOCKS):
                            ins = nc.tensor.transpose(X[:, 1, b * HEADS:(b + 1) * HEADS], fc[:, b * P:(b + 1) * P],
                                                      ident[0:HEADS, 0:HEADS])
                        ins.then_inc(c_ps, 1)
                    for name, q, p in steps.get(u, ()):
                        nq, np_ = 4 * L + q, 8 * L + 2 * q + p
                        fx = q >= 2
                        if name == "qk":
                            if fx:
                                pe.wait_ge(q_done, 4 * L + 2 * (q - 2) + 2)
                                pe.wait_ge(k_done, 4 * L + 2 * (q - 2) + 2)
                            else:
                                jq = 3 * q
                                pe.wait_ge(free[jq % 2], att_uses[layer] + jq // 2 + 1)
                                pe.wait_ge(free[(jq + 1) % 2], att_uses[layer] + (jq + 1) // 2 + 1)
                            if q == 0:
                                pe.wait_ge(c_ready, L + 1)
                            else:
                                pe.wait_ge(oT_ready, np_)
                            for n, v in enumerate((q_nat, k_nat)):
                                for hd in range(QUAD):
                                    for b in range(BLOCKS):
                                        at = (hd % 2) * 256 + b * P
                                        ins = nc.tensor.transpose(X[:, 2 * n + hd // 2, at:at + P],
                                                                  v[:, b, hd * P:(hd + 1) * P], ident[:])
                            ins.then_inc(qkT_ps, 1)
                        elif name == "scores":
                            pe.wait_ge(qT_ready, nq + 1)
                            pe.wait_ge(kT_ready, nq + 1)
                            if p:
                                pe.wait_ge(oT_ready, np_)
                            if fx:
                                pe.wait_ge(c_ready, L + 1)
                            for a in range(2):
                                hd = 2 * p + a
                                qh, kh = qT[:, hd], kT[:, hd]
                                if fx:
                                    hot = onehot[:, 4 * (q - 2) + hd, :]
                                    nc.tensor.matmul(X[:, a, 0:P], qh[:, 0:P], kh[:, 0:P], start=True, stop=False)
                                    nc.tensor.matmul(X[:, a, 0:P], hot, ncT[:, 0:P], start=False, stop=True)
                                    nc.tensor.matmul(X[:, a, P:PW], qh[:, P:2 * P], kh, start=True, stop=False)
                                    ins = nc.tensor.matmul(X[:, a, P:PW], hot, ncT[:], start=False, stop=True)
                                else:
                                    nc.tensor.matmul(X[:, a, 0:2 * P], kh[:, 0:P], qh, start=True, stop=True)
                                    ins = nc.tensor.matmul(X[:, a, 2 * P:PW], kh[:, P:2 * P], qh[:, P:2 * P],
                                                           start=True, stop=True)
                            ins.then_inc(z_ps, 1)
                        elif name == "second" and not fx:
                            pe.wait_ge(sp_ready, 4 * L + 2 * q + p + 1)
                            for a in range(2):
                                nc.tensor.matmul(X[:, 2 + a, 0:PW], tri_ge[:], sp[:, a], start=True, stop=False)
                                ins = nc.tensor.matmul(X[:, 2 + a, P:2 * P], ones[:], sp[:, a, 2 * P:PW],
                                                       start=False, stop=True)
                            ins.then_inc(rev_ps, 1)
                        elif name == "second":
                            pe.wait_ge(p_ready, 4 * L + 2 * (q - 2) + p + 1)
                            for a in range(2):
                                for n in range(3):
                                    ins = nc.tensor.transpose(X[:, 2 + a, n * P:(n + 1) * P],
                                                              sp[:, a, n * P:(n + 1) * P], ident[:])
                            ins.then_inc(pT_ps, 1)
                        elif name == "values":
                            pe.wait_ge(w_ready, np_ + 1)
                            jv = max(j for j in range(NJ) if jobs[j][0] == q and jobs[j][1] == "v")
                            pe.wait_ge(free[jv % 2], att_uses[layer] + jv // 2 + 1)
                            for a in range(2):
                                v = v_nat[:, :, (2 * p + a) * P:(2 * p + a + 1) * P]
                                lo, hi_ = a * P, (2 + a) * P
                                nc.tensor.matmul(X[:, 0, lo:lo + P], wT[:, a, 0:P], v[:, 0], start=True, stop=True)
                                nc.tensor.matmul(X[:, 0, hi_:hi_ + P], wT[:, a, P:2 * P], v[:, 0], start=True, stop=False)
                                ins = nc.tensor.matmul(X[:, 0, hi_:hi_ + P], wT[:, a, 2 * P:PW], v[:, 1], start=False,
                                                       stop=True)
                            ins.then_inc(o_ps, 1)
                        elif name == "turn":
                            pe.wait_ge(o_normed, np_ + 1)
                            for n in range(4):
                                ins = nc.tensor.transpose(X[:, 1, n * P:(n + 1) * P], ob[:, n], ident[:])
                            ins.then_inc(oT_ps, 1)

                F0, G0, A0, NG = ffn_start[layer], groups_before[layer], ffn_uses[layer], GROUPS[layer]
                if L == 1:
                    break

                def input_job(s, use, u0, uses_per=0, per=0, i=None, after=None, fresh=None):
                    pe.wait_ge(free[s], lin(use, uses_per, i))
                    for u in range(JOB_UNITS):
                        if fresh is not None:
                            if u == 1:
                                turn_input(fresh, 3)
                            pe.wait_ge(a_ready, CH * fresh + UNIT_CHUNKS * (u + 1))
                        ins = products(a_hi, a_lo, UNIT_CHUNKS * u, s, u == 0, u == JOB_UNITS - 1, u0 + u, per, i)
                        ins.then_inc(used, 1)
                        if after is not None:
                            after(u)

                def turn_hidden(n, per=0, i=None):
                    pe.wait_ge(free[1], lin(A0 + 3 * n + 1, 3 * per, i))
                    if i is None or per:
                        pe.wait_ge(hT_ready, lin(G0 + n, per, i)) if G0 + n > 0 else None
                    for c in range(GC):
                        for b in range(BLOCKS):
                            at = (c % 2) * 256 + b * P
                            ins = nc.tensor.transpose(X[:, c // 2, at:at + P], hid[:, b, c * P:(c + 1) * P], ident[:])
                    ins.then_inc(hT_ps, 1)

                def down_jobs(n, gate_between, u0, per=0, i=None, fresh=None):
                    pe.wait_ge(hT_ready, lin(G0 + n + 1, per, i))
                    for c in range(NCOL):
                        s = 1 - c % 2
                        use = A0 + 3 * n + c // 2 + 1 + (1 if s == 0 and gate_between else 0)
                        pe.wait_ge(free[s], lin(use, 3 * per, i))
                        for u in range(DOWN_UNITS):
                            ins = products(o_hi, o_lo, UNIT_CHUNKS * u, s, u == 0, u == DOWN_UNITS - 1,
                                           u0 + DOWN_UNITS * c + u, GROUP_UNITS * per, i)
                            ins.then_inc(used, 1)
                            if fresh is not None:
                                at_end(fresh, DOWN_UNITS * (c - NCOL) + u)

                input_job(0, A0, F0, fresh=2 * L + 1)
                F1 = F0 + UP_UNITS
                with pe.Fori(0, NG - 1) as i:
                    input_job(1, A0, F1, 3, GROUP_UNITS, i)

                    def then(u):
                        if u == TURN_AT - UP_UNITS:
                            turn_hidden(0, 1, i)
                    input_job(0, A0 + 1, F1 + UP_UNITS, 3, GROUP_UNITS, i, after=then)
                    down_jobs(0, True, F1 + 2 * UP_UNITS, 1, i)
                F2 = F1 + GROUP_UNITS * (NG - 1)
                input_job(1, A0 + 3 * (NG - 1), F2)
                turn_hidden(NG - 1)
                down_jobs(NG - 1, False, F2 + UP_UNITS, fresh=2 * L + 2)

            logits = acc[0:EXPERTS, 0, 0, 0:BLOCKS * P]
            pe.wait_ge(free[0], ffn_uses[1])
            for quarter in range(4):
                if quarter == 3:
                    turn_input(3, 3)
                pe.wait_ge(a_ready, CH * 3 + 4 * (quarter + 1))
                ins = thin_products(2, logits, range(4 * quarter, 4 * quarter + 4))
            ins.then_inc(rt_ps, 1)
            pe.wait_ge(rt_copied, 1)
            for b in range(BLOCKS):
                ins = nc.tensor.transpose(acc[:, 0, 1, b * EXPERTS:(b + 1) * EXPERTS], rt_logits[:, b * P:(b + 1) * P],
                                          ident[0:EXPERTS, 0:EXPERTS])
            ins.then_inc(rtT_ps, 1)
            pe.wait_ge(chosen, 1)
            nc.tensor.matmul(X[:, 0, 0:EXPERTS], tri_le[:], both_e[:, 0], start=True, stop=True)
            nc.tensor.matmul(X[:, 0, EXPERTS:2 * EXPERTS], ones[:], both_e[:, 0], start=True, stop=False)
            nc.tensor.matmul(X[:, 0, EXPERTS:2 * EXPERTS], tri_le[:], both_e[:, 1], start=False, stop=True)
            nc.tensor.matmul(X[:, 0, 2 * EXPERTS:3 * EXPERTS], ones[:], both_e[:, 0], start=True, stop=False)
            nc.tensor.matmul(X[:, 0, 2 * EXPERTS:3 * EXPERTS], ones[:], both_e[:, 1], start=False, stop=True)\
              .then_inc(ranks_ps, 1)

            def pick_quarter(n, per=0, i=None):
                pe.wait_ge(pick_ready, lin(n // 4 + 1, per // 4, i))
                if n >= 2:
                    pe.wait_ge(picked_hi, lin(n - 1, per, i))
                    pe.wait_ge(picked_lo, lin(n - 1, per, i))
                for part, src in enumerate((n_hi, n_lo)):
                    for c in range(4):
                        k = n % 4 * 4 + c
                        for b in range(BLOCKS):
                            ins = nc.tensor.matmul(X[:, 2 - 2 * (n % 2) + part, c * P:(c + 1) * P],
                                                   src[:, b, k * P:(k + 1) * P], pick[:, b],
                                                   start=b == 0, stop=b == BLOCKS - 1)
                ins.then_inc(picked_ps, 1)

            def pass_products(lhs_hi, lhs_lo, k0, s, first, last, u, i):
                slot = u % SPLIT_SLOTS
                low_ready(pe, M0 + u, PASS_UNITS, i)
                for c in range(UNIT_CHUNKS):
                    hi, lo, dst = lhs_hi[:, k0 + c], lhs_lo[:, k0 + c], acc[:, 0, s]
                    nc.tensor.matmul(dst, hi, w_hi[:, slot, c], start=first and c == 0, stop=False)
                    nc.tensor.matmul(dst, hi, w_lo[:, slot, c], start=False, stop=False)
                    ins = nc.tensor.matmul(dst, lo, w_hi[:, slot, c], start=False, stop=last and c == UNIT_CHUNKS - 1)
                ins.then_inc(used, 1)

            for n in range(4):
                pe.wait_ge(n_lo_ready, n + 1)
                pick_quarter(n)
            pe.wait_ge(table_ready, 1)
            passes = pe.value_load(table[0:1, TABLE:TABLE + 1], min_val=EXPERTS, max_val=MAX_PASSES)
            with pe.Fori(0, passes) as i:
                for u in range(PASS_UNITS):
                    if u < DOWN0:
                        job, ju = u // UP_UNITS, u % UP_UNITS
                        s = job % 2
                        if ju == 0:
                            pe.wait_ge(free[s], lin(ffn_uses[1] + job // 2, 4, i))
                        if job == 0 and ju % 2 == 0:
                            pe.wait_ge(picked_hi, lin(ju // 2 + 1, 4, i))
                            pe.wait_ge(picked_lo, lin(ju // 2 + 1, 4, i))
                        pass_products(x_hi, x_lo, UNIT_CHUNKS * ju, s, ju == 0, ju == UP_UNITS - 1, u, i)
                    else:
                        c, k = down_units[u - DOWN0]
                        s = c % 2
                        if k == 0:
                            pe.wait_ge(free[s], lin(ffn_uses[1] + 2 + c // 2, 4, i))
                        if c == 0:
                            pe.wait_ge(hT_ready, lin(GROUPS[0] + k // DOWN_UNITS + 1, HALVES, i))
                        pass_products(hT_h, hT_l, UNIT_CHUNKS * k, s, k == 0, k == HALVES * DOWN_UNITS - 1, u, i)
                    if u == 3:
                        pe.wait_ge(picked_lo, lin(4, 4, i))
                        pe.wait_ge(gates_ready, i + 1)
                        for b in range(BLOCKS):
                            nc.tensor.matmul(X[:, 1, b * P:(b + 1) * P], pick[:, b], ident_r[:], start=True, stop=True)
                        for b in range(BLOCKS):
                            ins = nc.tensor.matmul(X[:, 1, BLOCKS * P:BLOCKS * P + 1], pick_g[:, b], ones[:, 0:1],
                                                   start=b == 0, stop=b == BLOCKS - 1)
                        ins.then_inc(put_ps, 1)
                    if u in turn_at:
                        pe.wait_ge(free[1], lin(ffn_uses[1] + turn_at[u] + 1, 4, i))
                        pe.wait_ge(picked_hi, lin(4, 4, i))
                        for c in range(GC):
                            ins = nc.tensor.transpose(X[:, 0, c * P:(c + 1) * P], hid1[:, c * P:(c + 1) * P], ident[:])
                        ins.then_inc(hT_ps, 1)
                    if u in pick_at:
                        pe.wait_ge(slot_ready, i + 1)
                        pe.wait_ge(hT_ready, lin(GROUPS[0] + HALVES, HALVES, i))
                        pick_quarter(4 + pick_at[u], 4, i)
                    if u in put_at:
                        c = put_at[u]
                        pe.wait_ge(free[c % 2], lin(ffn_uses[1] + 3 + c // 2, 4, i))
                        if c:
                            pe.wait_ge(y_added, lin(c, NCOL, i))
                        for b in range(BLOCKS):
                            nc.tensor.matmul(acc[:, 1, b], put[:, b * P:(b + 1) * P], y_h[:, c % 2], start=True, stop=False)
                            ins = nc.tensor.matmul(acc[:, 1, b], put[:, b * P:(b + 1) * P], y_l[:, c % 2], start=False,
                                                   stop=True)
                        ins.then_inc(y_ps, 1)


_INS = ["x", "attn_norm", "w_in", "b_forget", "fox_q_norm", "fox_k_norm", "sb_out_norm", "fox_out_norm", "w_out",
        "ffn_norm", "dense_w_gate", "dense_w_up", "dense_w_down", "router_w", "moe_w_gate", "moe_w_up",
        "moe_w_down", "final_norm"]


def kernel(**inputs):
    import numpy as _np
    import concourse.bacc as _bacc
    from concourse import mybir as _mybir
    from concourse.bass_utils import run_bass_kernel_spmd as _run

    nc = _bacc.Bacc("TRN2", target_bir_lowering=False, num_devices=1)
    arrays, args = {}, []
    for name in _INS:
        a = _np.ascontiguousarray(inputs[name])
        arrays[f"in_{name}"] = a
        args.append(nc.dram_tensor(f"in_{name}", a.shape, _mybir.dt.from_np(a.dtype), kind="ExternalInput").ap())
    shape = arrays["in_x"].shape
    args.append(nc.dram_tensor("out_0", shape, _mybir.dt.float32, kind="ExternalOutput").ap())
    trunk(nc, *args)
    r = _run(nc, [arrays], core_ids=[0])
    return r.results[0]["out_0"]
```
